# Optimizing a Trainium2 kernel written in Bass

```python
import math
import jax
import jax.numpy as jnp
from jax import lax
import numpy as np

D_MODEL = 1024
BATCH = 1
SEQ = 2048
DEPTH = 1

CTX_LEN = 256
GRID_W = 64
MIX_W = D_MODEL
HEAD_DIM = 64
ATT_W = MIX_W // 2
HYENA_W = MIX_W - ATT_W
N_HEADS = ATT_W // HEAD_DIM
N_KV_HEADS = 2
GQA_GROUP = N_HEADS // N_KV_HEADS
KV_W = N_KV_HEADS * HEAD_DIM
ATT_SCALE = HEAD_DIM ** -0.5
WINDOW = 128
Q_BLOCK = 128
NEG_INF = -1e30
ROPE_THETA = 10000.0
ROPE_PAIRS = HEAD_DIM // 4
HYENA_ORDER = 2
HYENA_PROJ_W = (HYENA_ORDER + 1) * HYENA_W
HYENA_BANDS = 16
HYENA_EMB = 2 * HYENA_BANDS + 1
HYENA_FILTER_HIDDEN = 64
SHORT_CONV = 3
DECAY_TARGET = 1e-2
FAST_DECAY_PCT = 0.3
SLOW_DECAY_PCT = 1.5
K_OFF = ATT_W
V_OFF = ATT_W + KV_W
HY_OFF = ATT_W + 2 * KV_W
PROJ_W = HY_OFF + HYENA_PROJ_W
N_GROUPS = 4
EXPERTS_PER_GROUP = 8
N_EXPERTS = N_GROUPS * EXPERTS_PER_GROUP
EXPERT_HIDDEN = D_MODEL // 2
TOP_K = 2
MOE_BLOCK = 128
EPS = 1e-6

kernel_name = 'hymba_swa_hyena_hmoe_dit_block'

def rms_norm(x, w):
    xf = x.astype(jnp.float32)
    y = xf * lax.rsqrt(jnp.mean(xf * xf, axis=-1, keepdims=True) + EPS)
    return y.astype(x.dtype) * w

def modulate(h, shift, scale):
    return h * (1.0 + scale) + shift

def split_heads(t, n_heads):
    return t.reshape(t.shape[:-1] + (n_heads, HEAD_DIM))

def rotate_pairs(x, ang):
    m = x.shape[-1] // 2
    cos = jnp.cos(ang).astype(x.dtype)
    sin = jnp.sin(ang).astype(x.dtype)
    x1, x2 = x[..., :m], x[..., m:]
    return jnp.concatenate([x1 * cos - x2 * sin, x2 * cos + x1 * sin], axis=-1)

def rope_2d(x, ang_r, ang_c):
    half = HEAD_DIM // 2
    return jnp.concatenate([rotate_pairs(x[..., :half], ang_r), rotate_pairs(x[..., half:], ang_c)], axis=-1)

def short_conv(u, w, b):
    seq_len = u.shape[1]
    half = SHORT_CONV // 2
    up = jnp.pad(u, ((0, 0), (half, half), (0, 0)))
    out = b
    for j in range(SHORT_CONV):
        out = out + up[:, j:j + seq_len] * w[j]
    return out

def implicit_filter_spectrum(seq_len, w1, b1, w2, b2, w3, sin_freq):
    pos = jnp.arange(seq_len, dtype=jnp.float32)
    t = pos / seq_len
    bands = jnp.linspace(1e-4, HYENA_BANDS - 1, HYENA_BANDS, dtype=jnp.float32)
    ang = (2.0 * math.pi / seq_len) * pos[:, None] * bands[None, :]
    feat = jnp.concatenate([t[:, None], jnp.cos(ang), -jnp.sin(ang)], axis=-1).astype(w1.dtype)
    h = jnp.sin(sin_freq[0] * (feat @ w1 + b1))
    h = jnp.sin(sin_freq[1] * (h @ w2 + b2))
    h = (h @ w3).astype(jnp.float32).reshape(seq_len, HYENA_ORDER, 2, HYENA_W)
    max_decay = math.log(DECAY_TARGET) / FAST_DECAY_PCT
    min_decay = math.log(DECAY_TARGET) / SLOW_DECAY_PCT
    deltas = jnp.abs(jnp.linspace(min_decay, max_decay, HYENA_W, dtype=jnp.float32))
    h = h * jnp.exp(-t[:, None] * deltas[None, :])[:, None, None, :]
    fwd, bwd = h[:, :, 0], h[:, :, 1]
    kern = jnp.concatenate([fwd, jnp.zeros((1, HYENA_ORDER, HYENA_W), jnp.float32), bwd[1:][::-1]], axis=0)
    return jnp.fft.rfft(kern, axis=0)

def hyena_mixer(u, conv_w, conv_b, w1, b1, w2, b2, w3, sin_freq, skip):
    seq_len = u.shape[1]
    parts = jnp.split(short_conv(u, conv_w, conv_b), HYENA_ORDER + 1, axis=-1)
    spec = implicit_filter_spectrum(seq_len, w1, b1, w2, b2, w3, sin_freq)
    z = parts[0].astype(jnp.float32)
    for o in range(HYENA_ORDER):
        zf = jnp.fft.rfft(z, n=2 * seq_len, axis=1)
        conv = jnp.fft.irfft(zf * spec[None, :, o], n=2 * seq_len, axis=1)[:, :seq_len]
        z = parts[o + 1].astype(jnp.float32) * (conv + skip[o].astype(jnp.float32) * z)
    return z.astype(u.dtype)

def windowed_attention(q, k, v, kc, vc, sink):
    bsz, seq_len = q.shape[:2]
    n_blocks = seq_len // Q_BLOCK
    band = Q_BLOCK + 2 * WINDOW
    pad = ((0, 0), (WINDOW, WINDOW), (0, 0), (0, 0))
    k_pad = jnp.pad(k, pad)
    v_pad = jnp.pad(v, pad)
    qg = q.reshape(bsz, seq_len, N_KV_HEADS, GQA_GROUP, HEAD_DIM)
    n_ctx = kc.shape[1]
    s_sink = jnp.broadcast_to(sink.reshape(N_KV_HEADS, GQA_GROUP, 1, 1).astype(jnp.float32),
                              (bsz, N_KV_HEADS, GQA_GROUP, Q_BLOCK, 1))

    def block(i):
        q0 = i * Q_BLOCK
        qb = lax.dynamic_slice_in_dim(qg, q0, Q_BLOCK, axis=1)
        kb = lax.dynamic_slice_in_dim(k_pad, q0, band, axis=1)
        vb = lax.dynamic_slice_in_dim(v_pad, q0, band, axis=1)
        q_pos = q0 + jnp.arange(Q_BLOCK)
        k_pos = q0 - WINDOW + jnp.arange(band)
        valid = ((jnp.abs(k_pos[None, :] - q_pos[:, None]) <= WINDOW)
                 & (k_pos[None, :] >= 0) & (k_pos[None, :] < seq_len))
        s_band = jnp.einsum('bqkgd,bskd->bkgqs', qb, kb).astype(jnp.float32) * ATT_SCALE
        s_band = jnp.where(valid, s_band, NEG_INF)
        s_ctx = jnp.einsum('bqkgd,bckd->bkgqc', qb, kc).astype(jnp.float32) * ATT_SCALE
        p = jax.nn.softmax(jnp.concatenate([s_sink, s_ctx, s_band], axis=-1), axis=-1).astype(v.dtype)
        o = (jnp.einsum('bkgqc,bckd->bqkgd', p[..., 1:1 + n_ctx], vc)
             + jnp.einsum('bkgqs,bskd->bqkgd', p[..., 1 + n_ctx:], vb))
        return o.reshape(bsz, Q_BLOCK, ATT_W)

    out = lax.map(block, jnp.arange(n_blocks))
    return out.transpose(1, 0, 2, 3).reshape(bsz, seq_len, ATT_W)

def context_attention(qc, kc, vc, sink):
    bsz, n_ctx = qc.shape[:2]
    qg = qc.reshape(bsz, n_ctx, N_KV_HEADS, GQA_GROUP, HEAD_DIM)
    s = jnp.einsum('bqkgd,bckd->bkgqc', qg, kc).astype(jnp.float32) * ATT_SCALE
    s_sink = jnp.broadcast_to(sink.reshape(N_KV_HEADS, GQA_GROUP, 1, 1).astype(jnp.float32),
                              (bsz, N_KV_HEADS, GQA_GROUP, n_ctx, 1))
    p = jax.nn.softmax(jnp.concatenate([s_sink, s], axis=-1), axis=-1).astype(vc.dtype)
    o = jnp.einsum('bkgqc,bckd->bqkgd', p[..., 1:], vc)
    return o.reshape(bsz, n_ctx, ATT_W)

def hierarchical_moe(h, router_g_w, router_g_b, router_e_w, router_e_b, exp_w1, exp_w3, exp_w2):
    bsz, seq_len, d = h.shape
    n_tok = bsz * seq_len
    xt = h.reshape(n_tok, d)
    g_prob = jax.nn.softmax((xt @ router_g_w + router_g_b).astype(jnp.float32), axis=-1)
    g_val, g_idx = lax.top_k(g_prob, 1)
    e_logits = (xt @ router_e_w + router_e_b).astype(jnp.float32).reshape(n_tok, N_GROUPS, EXPERTS_PER_GROUP)
    e_logits = jnp.take_along_axis(e_logits, g_idx[:, :, None], axis=1)[:, 0]
    e_val, e_idx = lax.top_k(jax.nn.softmax(e_logits, axis=-1), TOP_K)
    gate = g_val * e_val / jnp.sum(e_val, axis=-1, keepdims=True)
    expert = g_idx * EXPERTS_PER_GROUP + e_idx
    n_assign = n_tok * TOP_K
    e_flat = expert.reshape(n_assign)
    order = jnp.argsort(e_flat)
    e_sorted = e_flat[order]
    tok_sorted = order // TOP_K
    gate_sorted = gate.reshape(n_assign)[order]
    counts = jnp.bincount(e_flat, length=N_EXPERTS)
    starts = jnp.cumsum(counts) - counts
    padded = (counts + MOE_BLOCK - 1) // MOE_BLOCK * MOE_BLOCK
    padded_end = jnp.cumsum(padded)
    padded_start = padded_end - padded
    dest = padded_start[e_sorted] + jnp.arange(n_assign) - starts[e_sorted]
    n_blocks = -(-n_assign // MOE_BLOCK) + N_EXPERTS
    buf = jnp.zeros((n_blocks * MOE_BLOCK, d), h.dtype).at[dest].set(xt[tok_sorted])
    block_expert = jnp.minimum(
        jnp.searchsorted(padded_end, jnp.arange(n_blocks) * MOE_BLOCK, side='right'), N_EXPERTS - 1)

    def expert_block(args):
        xb, e = args
        return (jax.nn.silu(xb @ exp_w1[e]) * (xb @ exp_w3[e])) @ exp_w2[e]

    y_buf = lax.map(expert_block, (buf.reshape(n_blocks, MOE_BLOCK, d), block_expert))
    y = y_buf.reshape(n_blocks * MOE_BLOCK, d)[dest] * gate_sorted[:, None].astype(h.dtype)
    out = jnp.zeros((n_tok, d), h.dtype).at[tok_sorted].add(y)
    return out.reshape(bsz, seq_len, d)

def trunk_layer(x, xc, mod_lat, mod_ctx, ang_r, ang_c, norm1_w, w_in, q_norm_w, k_norm_w, attn_sink,
                hy_conv_w, hy_conv_b, hy_w1, hy_b1, hy_w2, hy_b2, hy_w3, hy_sin_freq, hy_skip,
                group_norm_w, w_out, norm2_w, router_g_w, router_g_b, router_e_w, router_e_b,
                exp_w1, exp_w3, exp_w2, update_ctx):
    sh1, sc1, g1, sh2, sc2, g2 = jnp.split(mod_lat[:, None, :], 6, axis=-1)
    csh1, csc1, cg1, csh2, csc2, cg2 = jnp.split(mod_ctx, 6, axis=-1)
    h = modulate(rms_norm(x, norm1_w), sh1, sc1)
    hc = modulate(rms_norm(xc, norm1_w), csh1, csc1)
    proj = h @ w_in
    if update_ctx:
        proj_c = hc @ w_in
        kv_c = proj_c[..., K_OFF:HY_OFF]
    else:
        kv_c = hc @ w_in[:, K_OFF:HY_OFF]
    kc = rms_norm(split_heads(kv_c[..., :KV_W], N_KV_HEADS), k_norm_w)
    vc = split_heads(kv_c[..., KV_W:], N_KV_HEADS)
    q = rope_2d(rms_norm(split_heads(proj[..., :K_OFF], N_HEADS), q_norm_w), ang_r, ang_c)
    k = rope_2d(rms_norm(split_heads(proj[..., K_OFF:V_OFF], N_KV_HEADS), k_norm_w), ang_r, ang_c)
    v = split_heads(proj[..., V_OFF:HY_OFF], N_KV_HEADS)
    att = windowed_attention(q, k, v, kc, vc, attn_sink)
    hy = hyena_mixer(proj[..., HY_OFF:], hy_conv_w, hy_conv_b, hy_w1, hy_b1, hy_w2, hy_b2, hy_w3,
                     hy_sin_freq, hy_skip)
    mix = jnp.concatenate([rms_norm(att, group_norm_w[:ATT_W]), rms_norm(hy, group_norm_w[ATT_W:])],
                          axis=-1) @ w_out
    x = x + g1 * mix
    x = x + g2 * hierarchical_moe(modulate(rms_norm(x, norm2_w), sh2, sc2), router_g_w, router_g_b,
                                  router_e_w, router_e_b, exp_w1, exp_w3, exp_w2)
    if update_ctx:
        qc = rms_norm(split_heads(proj_c[..., :K_OFF], N_HEADS), q_norm_w)
        att_c = context_attention(qc, kc, vc, attn_sink)
        hy_c = hyena_mixer(proj_c[..., HY_OFF:], hy_conv_w, hy_conv_b, hy_w1, hy_b1, hy_w2, hy_b2, hy_w3,
                           hy_sin_freq, hy_skip)
        mix_c = jnp.concatenate([rms_norm(att_c, group_norm_w[:ATT_W]), rms_norm(hy_c, group_norm_w[ATT_W:])],
                                axis=-1) @ w_out
        xc = xc + cg1 * mix_c
        xc = xc + cg2 * hierarchical_moe(modulate(rms_norm(xc, norm2_w), csh2, csc2), router_g_w, router_g_b,
                                         router_e_w, router_e_b, exp_w1, exp_w3, exp_w2)
    return x, xc

def setup_inputs(seed: int = 0) -> dict:
    key = jax.random.key(seed)
    ks = jax.random.split(key, 30)

    def nrm(k, shape, scale):
        return jax.random.normal(k, shape, jnp.float32) * scale

    hy_out = HYENA_ORDER * 2 * HYENA_W
    return {
        'x': nrm(ks[0], (BATCH, SEQ, D_MODEL), 1.0),
        'c': nrm(ks[1], (BATCH, D_MODEL), 1.0),
        'ctx': nrm(ks[2], (BATCH, CTX_LEN, D_MODEL), 1.0),
        'c_ctx': nrm(ks[3], (D_MODEL,), 1.0),
        'ada_w': nrm(ks[4], (DEPTH, D_MODEL, 6 * D_MODEL), 0.5 * D_MODEL ** -0.5),
        'ada_b': nrm(ks[5], (DEPTH, 6 * D_MODEL), 0.02),
        'norm1_w': 1.0 + nrm(ks[6], (DEPTH, D_MODEL), 0.05),
        'w_in': nrm(ks[7], (DEPTH, D_MODEL, PROJ_W), D_MODEL ** -0.5),
        'q_norm_w': 1.0 + nrm(ks[8], (DEPTH, HEAD_DIM), 0.05),
        'k_norm_w': 1.0 + nrm(ks[9], (DEPTH, HEAD_DIM), 0.05),
        'attn_sink': nrm(ks[10], (DEPTH, N_HEADS), 0.5),
        'hy_conv_w': nrm(ks[11], (DEPTH, SHORT_CONV, HYENA_PROJ_W), SHORT_CONV ** -0.5),
        'hy_conv_b': nrm(ks[12], (DEPTH, HYENA_PROJ_W), 0.02),
        'hy_w1': nrm(ks[13], (DEPTH, HYENA_EMB, HYENA_FILTER_HIDDEN), HYENA_EMB ** -0.5),
        'hy_b1': nrm(ks[14], (DEPTH, HYENA_FILTER_HIDDEN), 0.1),
        'hy_w2': nrm(ks[15], (DEPTH, HYENA_FILTER_HIDDEN, HYENA_FILTER_HIDDEN), HYENA_FILTER_HIDDEN ** -0.5),
        'hy_b2': nrm(ks[16], (DEPTH, HYENA_FILTER_HIDDEN), 0.1),
        'hy_w3': nrm(ks[17], (DEPTH, HYENA_FILTER_HIDDEN, hy_out), 0.05 * HYENA_FILTER_HIDDEN ** -0.5),
        'hy_sin_freq': 1.0 + nrm(ks[18], (DEPTH, 2, HYENA_FILTER_HIDDEN), 0.05),
        'hy_skip': nrm(ks[19], (DEPTH, HYENA_ORDER, HYENA_W), 1.0),
        'group_norm_w': 1.0 + nrm(ks[20], (DEPTH, MIX_W), 0.05),
        'w_out': nrm(ks[21], (DEPTH, MIX_W, D_MODEL), MIX_W ** -0.5),
        'norm2_w': 1.0 + nrm(ks[22], (DEPTH, D_MODEL), 0.05),
        'router_g_w': nrm(ks[23], (DEPTH, D_MODEL, N_GROUPS), D_MODEL ** -0.5),
        'router_g_b': nrm(ks[24], (DEPTH, N_GROUPS), 0.01),
        'router_e_w': nrm(ks[25], (DEPTH, D_MODEL, N_EXPERTS), D_MODEL ** -0.5),
        'router_e_b': nrm(ks[26], (DEPTH, N_EXPERTS), 0.01),
        'exp_w1': nrm(ks[27], (DEPTH, N_EXPERTS, D_MODEL, EXPERT_HIDDEN), D_MODEL ** -0.5),
        'exp_w3': nrm(ks[28], (DEPTH, N_EXPERTS, D_MODEL, EXPERT_HIDDEN), D_MODEL ** -0.5),
        'exp_w2': nrm(ks[29], (DEPTH, N_EXPERTS, EXPERT_HIDDEN, D_MODEL), EXPERT_HIDDEN ** -0.5),
    }

def reference(x, c, ctx, c_ctx, ada_w, ada_b, norm1_w, w_in, q_norm_w, k_norm_w, attn_sink,
              hy_conv_w, hy_conv_b, hy_w1, hy_b1, hy_w2, hy_b2, hy_w3, hy_sin_freq, hy_skip,
              group_norm_w, w_out, norm2_w, router_g_w, router_g_b, router_e_w, router_e_b,
              exp_w1, exp_w3, exp_w2):
    seq_len = x.shape[1]
    n_rows = seq_len // GRID_W
    rows = jnp.repeat(jnp.arange(n_rows, dtype=jnp.float32), GRID_W)
    cols = jnp.tile(jnp.arange(GRID_W, dtype=jnp.float32), n_rows)
    inv_freq = ROPE_THETA ** (-jnp.arange(ROPE_PAIRS, dtype=jnp.float32) / ROPE_PAIRS)
    ang_r = (rows[:, None] * inv_freq[None, :])[:, None, :]
    ang_c = (cols[:, None] * inv_freq[None, :])[:, None, :]
    xc = ctx
    for layer in range(DEPTH):
        mod_lat = jax.nn.silu(c) @ ada_w[layer] + ada_b[layer]
        mod_ctx = jax.nn.silu(c_ctx) @ ada_w[layer] + ada_b[layer]
        x, xc = trunk_layer(x, xc, mod_lat, mod_ctx, ang_r, ang_c, norm1_w[layer], w_in[layer],
                            q_norm_w[layer], k_norm_w[layer], attn_sink[layer], hy_conv_w[layer],
                            hy_conv_b[layer], hy_w1[layer], hy_b1[layer], hy_w2[layer], hy_b2[layer],
                            hy_w3[layer], hy_sin_freq[layer], hy_skip[layer], group_norm_w[layer],
                            w_out[layer], norm2_w[layer], router_g_w[layer], router_g_b[layer],
                            router_e_w[layer], router_e_b[layer], exp_w1[layer], exp_w3[layer],
                            exp_w2[layer], layer < DEPTH - 1)
    return x


_drawn_inputs = setup_inputs


def setup_inputs(seed=0):
    import zlib

    import numpy as np

    out = dict(_drawn_inputs(seed))
    spreads = {}
    factors = {'norm1_w': 2.768,
     'q_norm_w': 8.0,
     'k_norm_w': 8.0,
     'attn_sink': 8.0,
     'hy_conv_b': 2.744,
     'hy_sin_freq': 4.644,
     'group_norm_w': 3.216,
     'norm2_w': 2.724,
     'router_g_b': 8.0,
     'router_e_b': 8.0}
    for name, (base, spread) in spreads.items():
        noise = np.random.default_rng([zlib.crc32(name.encode()), seed]).standard_normal(out[name].shape)
        drawn = base * np.exp(spread * noise) if base else spread * noise
        out[name] = jnp.asarray(drawn.astype(out[name].dtype))
    for name, factor in factors.items():
        out[name] = (out[name] * factor).astype(out[name].dtype)
    return out
```

```python
from contextlib import ExitStack, contextmanager

import numpy as np

import concourse.bass as bass
from concourse import mybir

F32 = mybir.dt.float32
I32 = mybir.dt.int32
U32 = mybir.dt.uint32
ALU = mybir.AluOpType
ACT = mybir.ActivationFunctionType
AX = mybir.AxisListType

P = 128
D = 1024
T = 2048
C = 256
KT = D // P
NT = T // P
HD = 64
NH, NKV = 8, 2
AW = 512
HW = 512
Q = 16
NE = 32
NG, EPG = 4, 8
FH = 512
EPS = 1e-6
SCALE = HD ** -0.5
NEG = -1e30
LANE = 128
NL = HW // LANE
NOWHERE = 4095
CAP = T

C_ADAB, C_N1, C_N2, C_GN, C_CW, C_CB, C_QN, C_KN, C_B1, C_B2, C_SF = 0, 48, 56, 64, 72, 108, 120, 121, 122, 123, 124


def constants():
    k = {}
    p = np.arange(P)[:, None, None]
    q = np.arange(Q)[None, :, None]
    k2 = np.arange(P)[None, None, :]
    th = 2 * np.pi * (((16 * p + q) * k2) % 4096) / 4096
    fre, fim = np.cos(th), -np.sin(th)
    fim[:, :, 0] = np.where(np.arange(P) % 2, -1.0, 1.0)[:, None]
    k["dft_fwd"] = np.concatenate([fre, fim], axis=2).reshape(P, Q * 256)
    ire = 2 / 4096 * np.cos(th).transpose(2, 1, 0)
    iim = -2 / 4096 * np.sin(th).transpose(2, 1, 0)
    ire[0] = 1 / 4096
    iim[0] = np.where(np.arange(P) % 2, -1.0, 1.0)[None, :] / 4096
    k["dft_inv"] = np.stack([ire, iim], axis=2).reshape(P, Q * 256)
    w = np.exp(-2j * np.pi * np.outer(np.arange(16), np.arange(16)) / 16)
    x = np.zeros((4, 16, 2, 4, 16, 2))
    for s in range(4):
        x[s, :, 0, s, :, 0] = w.real
        x[s, :, 0, s, :, 1] = w.imag
        x[s, :, 1, s, :, 0] = -w.imag
        x[s, :, 1, s, :, 1] = w.real
    xs = x.copy()
    xs[0, :, :, 0] = 0
    qq = np.arange(16)
    xs[0, :, 0, 0, 0, 0] = 1
    xs[0, :, 0, 0, 0, 1] = (-1.0) ** qq
    for k1 in range(1, 8):
        xs[0, :, 0, 0, k1, 0] = w[:, k1].real
        xs[0, :, 0, 0, k1, 1] = w[:, k1].imag
    for k1 in range(8):
        v = np.exp(-2j * np.pi * qq * (k1 + 0.5) / 16)
        xs[0, :, 1, 0, 8 + k1, 0] = v.real
        xs[0, :, 1, 0, 8 + k1, 1] = v.imag

    def spectra(m, special):
        h1, h2 = m.copy(), m.copy()
        h1[..., 1] = m[..., 0]
        h2[..., 0] = m[..., 1]
        h2[..., 1] = -m[..., 1]
        if special:
            h1[:, :, :, 0, 0, 1] = m[:, :, :, 0, 0, 1]
            h2[:, :, :, 0, 0, :] = 0
        return h1, h2

    inv = np.zeros((4, 16, 2, 4, 16, 2))
    wi = np.conj(w).T
    for s in range(4):
        inv[s, :, 0, s, :, 0] = wi.real
        inv[s, :, 0, s, :, 1] = wi.imag
        inv[s, :, 1, s, :, 0] = -wi.imag
        inv[s, :, 1, s, :, 1] = wi.real
    invs = inv.copy()
    invs[0, :, :, 0] = 0
    invs[0, 0, 0, 0, :, 0] = 1
    invs[0, 0, 1, 0, :, 0] = (-1.0) ** qq
    for k1 in range(1, 8):
        invs[0, k1, 0, 0, :, 0] = 2 * wi[k1].real
        invs[0, k1, 1, 0, :, 0] = -2 * wi[k1].imag
    for k1 in range(8):
        v = np.exp(2j * np.pi * qq * (k1 + 0.5) / 16)
        invs[0, 8 + k1, 0, 0, :, 1] = 2 * v.real
        invs[0, 8 + k1, 1, 0, :, 1] = -2 * v.imag
    mats = []
    for m, n, special in ((x, inv, False), (xs, invs, True)):
        h1, h2 = spectra(m, special)
        mats += [m, h1, h2, n, n[:, :, ::-1]]
    k["dft_mid"] = np.stack([m.reshape(P, P) for m in mats], axis=1).reshape(P, 10 * P)
    tf = (16 * np.arange(P)[None, :] + np.arange(Q)[:, None]).reshape(-1)
    pos = np.concatenate([tf, T - tf]).astype(np.float64)
    bands = np.linspace(1e-4, 15, 16).astype(np.float32).astype(np.float64)
    ang = 2 * np.pi / T * pos[None, :] * bands[:, None]
    k["feat"] = np.concatenate([pos[None] / T, np.cos(ang), -np.sin(ang)], axis=0)
    k["tneg"] = -(np.stack([tf.reshape(Q, P).T, (T - tf).reshape(Q, P).T], axis=1) / T).reshape(P, 2 * Q)
    deltas = np.abs(np.linspace(np.log(1e-2) / 1.5, np.log(1e-2) / 0.3, HW))
    k["deltas"] = np.broadcast_to(deltas[None], (P, HW))
    tok = np.arange(T)
    inv_freq = 10000.0 ** (-np.arange(16) / 16)
    a = np.concatenate([np.outer(inv_freq, tok // 64), np.outer(inv_freq, tok // 64),
                        np.outer(inv_freq, tok % 64), np.outer(inv_freq, tok % 64)])
    sign = np.where(np.arange(64) % 32 < 16, -1.0, 1.0)[:, None]
    k["rope_cos"] = np.concatenate([np.cos(a)] * 2)
    k["rope_sin"] = np.concatenate([np.sin(a) * sign] * 2)
    c = np.arange(P)
    k["head_ones"] = (c[:, None] // 64 == c[None, :] // 64) * 1.0
    k["pair_swap"] = (c[:, None] == (c[None, :] ^ 16)) * 1.0
    k["ident"] = np.eye(P)
    k["upper"] = (c[:, None] < c[None, :]) * 1.0
    qi, kj = np.arange(P)[:, None], np.arange(3 * P)[None, :] - P
    band = np.where(np.abs(kj - qi) <= P, 0.0, NEG)
    k["mask"] = np.concatenate([np.zeros((P, C)), band], axis=1)
    kb = np.zeros((1, NKV, C + T + 2 * P))
    kb[:, :, C:C + P] = NEG
    kb[:, :, C + P + T:] = NEG
    k["key_bias"] = kb.reshape(1, -1)
    k["rank8"] = np.broadcast_to(8.0 - np.arange(8)[None], (P, 8))
    k["slot0"] = np.broadcast_to(float(CAP) * np.arange(NE)[None], (P, NE))
    out = {n: np.ascontiguousarray(v, dtype=np.float32) for n, v in k.items()}
    out["token"] = (np.arange(P)[:, None] + P * np.arange(NT)[None]).astype(np.int32)
    return out


class Env:

    def __init__(self, nc, stack, inputs, debug=False):
        self.nc, self.stack, self.i, self.debug = nc, stack, inputs, debug
        self.sems = {}

    def sem(self, name):
        assert name not in self.sems
        self.sems[name] = self.nc.alloc_semaphore(name=name)
        return self.sems[name]

    def stage(self):
        @contextmanager
        def scope():
            with ExitStack() as st:
                yield st
            self.nc.clear_and_free_semaphores(list(self.sems.values()))
            self.nc.all_engine_barrier()
            self.sems = {}
        return scope()

    def sb(self, stack, name, shape, dt=F32):
        return stack.enter_context(self.nc.sbuf_tensor("sb_" + name, shape, dt))

    def ps(self, stack, name, shape, dt=F32):
        return stack.enter_context(self.nc.psum_tensor("ps_" + name, shape, dt))

    def dram(self, name, shape, dt=F32):
        kw = {"kind": "ExternalOutput"} if self.debug else {}
        return self.nc.dram_tensor("scr_" + name, shape, dt, **kw).ap()


class Chain:

    def __init__(self, eng, sem):
        self.eng, self.sem, self.n = eng, sem, 0

    def __call__(self, ins):
        ins.then_inc(self.sem, 1)
        self.n += 1
        return self.n

    def wait(self, n=None):
        self.eng.wait_ge(self.sem, self.n if n is None else n)


def stage1(e, g):
    nc = e.nc
    steps = [(o, q) for o in range(2) for q in range(Q)]
    TWO_PI_HI = float(np.float32(6.28125))
    TWO_PI_LO = float(np.float32(2 * np.pi - 6.28125))
    ROUND = 12582912.0
    with e.stage() as st:
        rows = e.sb(st, "rows", [P, P])
        crow = e.sb(st, "crow", [16, P])
        sil = e.sb(st, "sil", [P, 2, KT])
        csb = e.sb(st, "csb", [P, 16])
        ada = e.sb(st, "ada", [P, 2, 3 * D])
        feat = e.sb(st, "feat", [33, 2 * T])
        w1 = e.sb(st, "fw1", [33, 64])
        w2 = e.sb(st, "fw2", [64, 64])
        w3 = e.sb(st, "fw3", [64, 4 * HW])
        hid = e.sb(st, "hid", [64, 2, 2 * T])
        ang = e.sb(st, "ang", [64, 3, 512])
        fwd = e.sb(st, "fwd1", [P, Q, 2, P])
        dl = e.sb(st, "dl", [P, HW])
        tneg = e.sb(st, "tneg", [P, 2, Q])
        dec = e.sb(st, "dec", [P, 2, Q, HW])
        fb = e.sb(st, "fb", [P, 2, HW])
        eo = e.sb(st, "eo", [P, 2, 2, HW])
        out = e.sb(st, "fout", [P, 4, HW])
        gr = e.sb(st, "gr", [16, P])
        gcol = e.sb(st, "gcol", [P, 16])
        gen = e.ps(st, "gen", [P, 4, 512])
        spec = e.ps(st, "spec", [P, 2, 512])
        modp = e.ps(st, "modp", [P, 512])
        misc = e.ps(st, "misc", [P, 512])

        ld_small = e.sem("s1_small_loaded")
        ld_feat = e.sem("s1_feat_loaded")
        ld_ada = [e.sem(f"s1_ada_loaded{i}") for i in range(2)]
        rows_zero = e.sem("s1_rows_zeroed")
        turned = e.sem("s1_params_turned")
        cols_ok = e.sem("s1_cols_copied")
        sil_ok = e.sem("s1_silu_done")
        mlp_mm = e.sem("s1_mlp_product")
        mlp_arg = e.sem("s1_mlp_argument")
        mlp_sin = e.sem("s1_mlp_sine")
        dec_ok = e.sem("s1_decay_done")
        gen_mm = e.sem("s1_filter_generated")
        eo_ok = e.sem("s1_sum_difference")
        spec_mm = e.sem("s1_spectrum_product")
        spec_cp = e.sem("s1_spectrum_copied")
        stored = [e.sem(f"s1_spectrum_stored{i}") for i in range(4)]
        ada_mm = e.sem("s1_ada_product")
        dve = e.sem("s1_dve")
        g_cols = e.sem("s1_gate_cols")
        g_turn = e.sem("s1_gate_turned")
        g_copy = e.sem("s1_gate_copied")
        g_out = e.sem("s1_gate_stored")
        i = e.i
        small = [
            (rows[C_ADAB:C_ADAB + 48, :], i["ada_b"].rearrange("a (r p) -> (a r) p", p=P)),
            (rows[C_N1:C_N1 + 8, :], i["norm1_w"].rearrange("a (r p) -> (a r) p", p=P)),
            (rows[C_N2:C_N2 + 8, :], i["norm2_w"].rearrange("a (r p) -> (a r) p", p=P)),
            (rows[C_GN:C_GN + 8, :], i["group_norm_w"].rearrange("a (r p) -> (a r) p", p=P)),
            (rows[C_CW:C_CW + 36, :], i["hy_conv_w"].rearrange("a j (r p) -> (a j r) p", p=P)),
            (rows[C_CB:C_CB + 12, :], i["hy_conv_b"].rearrange("a (r p) -> (a r) p", p=P)),
            (rows[C_QN:C_QN + 1, 0:HD], i["q_norm_w"]), (rows[C_QN:C_QN + 1, HD:], i["q_norm_w"]),
            (rows[C_KN:C_KN + 1, 0:HD], i["k_norm_w"]), (rows[C_KN:C_KN + 1, HD:], i["k_norm_w"]),
            (rows[C_B1:C_B1 + 1, 0:64], i["hy_b1"]), (rows[C_B2:C_B2 + 1, 0:64], i["hy_b2"]),
            (rows[C_SF:C_SF + 2, 0:64], i["hy_sin_freq"].rearrange("a b c -> (a b) c")),
            (crow[0:8, :], i["c"].rearrange("a (r p) -> (a r) p", p=P)),
            (crow[8:16, :], i["c_ctx"].rearrange("(r p) -> r p", p=P)),
            (g.ident[:, :], i["ident"]),
        ]
        early = [
            (w1[:, :], i["hy_w1"][0]), (w2[:, :], i["hy_w2"][0]), (feat[:, :], i["feat"]),
            (dl[:, :], i["deltas"]), (tneg[:, :, :], i["tneg"].rearrange("p (d q) -> p d q", d=2)),
            (w3[:, :], i["hy_w3"][0]), (fwd[:, :, :, :], i["dft_fwd"].rearrange("p (q r k) -> p q r k", q=Q, r=2)),
        ]
        block = st.enter_context(nc.Block())

        @block.sync
        def _(sp):
            sp.wait_ge(rows_zero, 1)
            for dst, src in small:
                sp.dma_start(dst, src).then_inc(ld_small, 16)
            for dst, src in early:
                sp.dma_start(dst, src).then_inc(ld_feat, 16)
            for u in range(2 * KT):
                k, half = u // 2, u % 2
                if u >= 2:
                    sp.wait_ge(ada_mm, u - 1)
                sp.dma_start(ada[:, half, :], i["ada_w"][0, k * P:(k + 1) * P, half * 3 * D:(half + 1) * 3 * D])\
                    .then_inc(ld_ada[half], 16)

        @block.tensor
        def _(pe):
            pe.wait_ge(ld_small, 16 * len(small))
            pe.transpose(misc[:, 0:P], rows[:, :], g.ident[:, :]).then_inc(turned, 1)
            pe.transpose(misc[:, P:P + 16], crow[:, :], g.ident[0:16, 0:16]).then_inc(turned, 1)
            pe.wait_ge(ld_feat, 16 * len(early))
            for layer in range(2):
                for n in range(8):
                    at = 8 * layer + n
                    if at >= 2:
                        pe.wait_ge(mlp_arg, at - 1)
                    if layer == 1:
                        pe.wait_ge(mlp_sin, n + 1)
                    w, x = (w1[:, :], feat[:, n * 512:(n + 1) * 512]) if layer == 0 else \
                        (w2[:, :], hid[:, 0, n * 512:(n + 1) * 512])
                    pe.matmul(gen[0:64, at % 2, :], w, x, start=True, stop=True).then_inc(mlp_mm, 1)
            pe.wait_ge(mlp_sin, 16)

            def spectra(n):
                q = steps[n][1]
                pe.wait_ge(eo_ok, n + 1)
                for par in range(2):
                    if n >= 1:
                        pe.wait_ge(spec_cp, 2 * n + par - 1)
                    m = fwd[:, q, :, par::2]
                    pe.matmul(spec[:, par, :], m, eo[:, n % 2, par, :], start=True, stop=True).then_inc(spec_mm, 1)

            for n, (o, q) in enumerate(steps):
                if n >= 2:
                    pe.wait_ge(eo_ok, n - 1)
                elif n == 0:
                    pe.wait_ge(mlp_arg, 16)
                for d in range(2):
                    pe.matmul(gen[:, 2 * (n % 2) + d, :], hid[:, 1, d * T + q * P:d * T + (q + 1) * P],
                              w3[:, (2 * o + d) * HW:(2 * o + d + 1) * HW], start=True, stop=True).then_inc(gen_mm, 1)
                if n >= 1:
                    spectra(n - 1)
                if n % 2 == 1:
                    k, half = n // 4, (n // 2) % 2
                    pe.wait_ge(sil_ok, 1)
                    pe.wait_ge(ld_ada[half], 16 * (k + 1))
                    for mh in range(24):
                        m = 24 * half + mh
                        mm = pe.matmul(modp[:, 2 * m:2 * m + 2], ada[:, half, mh * P:(mh + 1) * P], sil[:, :, k],
                                       start=(k == 0 and m == 0), stop=(k == KT - 1), skip_group_check=True)
                    mm.then_inc(ada_mm, 1)
            spectra(len(steps) - 1)
            pe.wait_ge(g_cols, 1)
            pe.transpose(misc[0:16, 256:256 + P], gcol[:, :], g.ident[:, :]).then_inc(g_turn, 1)

        @block.scalar
        def _(act):
            act.wait_ge(turned, 2)
            act.wait_ge(cols_ok, 2)
            act.activation(sil[:, :, :], csb[:, :].rearrange("p (a k) -> p a k", a=2), ACT.Silu).then_inc(sil_ok, 1)
            act.wait_ge(ld_feat, 16 * len(early))
            for d in range(2):
                for q in range(Q):
                    act.activation(dec[:, d, q, :], dl[:, :], ACT.Exp, scale=tneg[:, d, q:q + 1]).then_inc(dec_ok, 1)
            for n in range(16):
                act.wait_ge(mlp_arg, n + 1)
                act.activation(hid[:, n // 8, (n % 8) * 512:(n % 8 + 1) * 512], ang[:, n % 3, :], ACT.Sin)\
                    .then_inc(mlp_sin, 1)

            def store(n):
                o, q = steps[n // 2]
                act.wait_ge(spec_cp, n + 1)
                for ri in range(2):
                    dst = g.filt_dram[o, :, q, ri].rearrange("l (j two) c -> two j l c", two=2)[n % 2]
                    act.dma_start(dst, out[64 * ri:64 * ri + 64, n % 4, :].rearrange("p (l c) -> p l c", c=LANE))\
                       .then_inc(stored[n % 4], 16)

            for n in range(2 * len(steps)):
                act.wait_ge(spec_mm, n + 1)
                if n >= 4:
                    act.wait_ge(stored[n % 4], 32 * (n // 4))
                act.copy(out[:, n % 4, :], spec[:, n % 2, :]).then_inc(spec_cp, 1)
                if n >= 1:
                    store(n - 1)
            store(2 * len(steps) - 1)
            act.wait_ge(g_turn, 1)
            act.copy(gr[:, :], misc[0:16, 256:256 + P]).then_inc(g_copy, 1)
            act.wait_ge(g_copy, 1)
            act.dma_start(g.gate_dram.rearrange("(r p) -> r p", p=P), gr[:, :]).then_inc(g_out, 16)
            act.wait_ge(g_out, 16)
            for b in range(4):
                act.wait_ge(stored[b], 32 * (2 * len(steps) // 4))

        @block.vector
        def _(ve):
            ch = Chain(ve, dve)
            ve.memset(rows[:, :], 0.0).then_inc(rows_zero, 1)
            ve.wait_ge(turned, 2)
            ve.tensor_copy(g.cols[:, :], misc[:, 0:P]).then_inc(cols_ok, 1)
            ve.tensor_copy(csb[:, :], misc[:, P:P + 16]).then_inc(cols_ok, 1)
            ve.wait_ge(cols_ok, 2)
            tmp = fb
            for n in range(16):
                layer, r = n // 8, n % 3
                ve.wait_ge(mlp_mm, n + 1)
                if n >= 3:
                    ve.wait_ge(mlp_sin, n - 2)
                ch(ve.tensor_scalar(tmp[0:64, 0, :], gen[0:64, n % 2, :], g.cols[0:64, C_B1 + layer:C_B1 + layer + 1],
                                    g.cols[0:64, C_SF + layer:C_SF + layer + 1], ALU.add, ALU.mult))
                ch.wait()
                ch(ve.tensor_scalar(tmp[0:64, 1, :], tmp[0:64, 0, :], float(1 / (2 * np.pi)), ROUND, ALU.mult, ALU.add))
                ch.wait()
                ch(ve.tensor_scalar(tmp[0:64, 1, :], tmp[0:64, 1, :], ROUND, None, ALU.subtract))
                ch.wait()
                ch(ve.scalar_tensor_tensor(out=tmp[0:64, 0, :], in0=tmp[0:64, 1, :], scalar=-TWO_PI_HI,
                                           in1=tmp[0:64, 0, :], op0=ALU.mult, op1=ALU.add))
                ch.wait()
                ch(ve.scalar_tensor_tensor(out=ang[:, r, :], in0=tmp[0:64, 1, :], scalar=-TWO_PI_LO,
                                           in1=tmp[0:64, 0, :], op0=ALU.mult, op1=ALU.add))
                ch.wait()
                ve.tensor_scalar(ang[:, r, :], ang[:, r, :], 3.1415925, -3.1415925, ALU.min, ALU.max)\
                    .then_inc(mlp_arg, 1)
            ve.wait_ge(dec_ok, 2 * Q)
            ve.wait_ge(ld_small, 16 * len(small))
            ch(ve.memset(dec[0:1, 1, 0, :], 0.0))
            ch.wait()
            for n, (o, q) in enumerate(steps):
                ve.wait_ge(gen_mm, 2 * n + 2)
                if n >= 2:
                    ve.wait_ge(spec_mm, 2 * n - 2)
                for d in range(2):
                    ch(ve.tensor_tensor(fb[:, d, :], gen[:, 2 * (n % 2) + d, :], dec[:, d, q, :], ALU.mult))
                ch.wait()
                ch(ve.tensor_tensor(eo[:, n % 2, 0, :], fb[:, 0, :], fb[:, 1, :], ALU.add))
                ve.tensor_tensor(eo[:, n % 2, 1, :], fb[:, 0, :], fb[:, 1, :], ALU.subtract).then_inc(eo_ok, 1)
                ve.wait_ge(eo_ok, n + 1)
                ch.wait()
            ve.wait_ge(ada_mm, 2 * KT)
            mp = modp[:, 0:96].rearrange("p (m a) -> p m a", a=2)
            ab = g.cols[:, C_ADAB:C_ADAB + 48]
            ch(ve.tensor_tensor(g.mods[:, 0, :], mp[:, :, 0], ab, ALU.add))
            ch(ve.tensor_tensor(g.mods[:, 1, :], mp[:, :, 1], ab, ALU.add))
            ch.wait()
            for a in range(2):
                ch(ve.scalar_tensor_tensor(out=g.scale1[:, a, :], in0=g.mods[:, a, 8:16], scalar=1.0,
                                           in1=g.cols[:, C_N1:C_N1 + 8], op0=ALU.add, op1=ALU.mult))
            ch(ve.scalar_tensor_tensor(out=g.scale2[:, :], in0=g.mods[:, 0, 32:40], scalar=1.0,
                                       in1=g.cols[:, C_N2:C_N2 + 8], op0=ALU.add, op1=ALU.mult))
            ch(ve.tensor_copy(gcol[:, 0:8], g.mods[:, 0, 16:24]))
            ve.tensor_copy(gcol[:, 8:16], g.mods[:, 0, 40:48]).then_inc(g_cols, 1)
            ve.wait_ge(g_cols, 1)
            ch.wait()


def stage2(e, g):
    nc, i = e.nc, e.i
    with e.stage() as st:
        xr = e.sb(st, "xr", [P, 2, D])
        sq = e.sb(st, "sq", [P, D])
        ss = e.sb(st, "ss", [P, 2, 1])
        rs = e.sb(st, "rs", [P, 2, 1])
        xn = e.sb(st, "xn", [P, 2, D])
        tp = e.ps(st, "tp", [P, 2, KT, P])
        loaded = [e.sem(f"s2_rows_loaded{b}") for b in range(2)]
        summed = e.sem("s2_squares_summed")
        inv = e.sem("s2_variance_inverted")
        root = e.sem("s2_rstd")
        scaled = e.sem("s2_rows_scaled")
        turned = e.sem("s2_rows_turned")
        out_v = e.sem("s2_written_by_vector")
        out_a = e.sem("s2_written_by_scalar")
        dve = e.sem("s2_dve")
        NS = NT + 2
        block = st.enter_context(nc.Block())

        def tiles(eng, body):
            for n in range(2):
                body(n, n, n, g.hT, 0)
            with eng.Fori(1, NT // 2) as j:
                for b in range(2):
                    body(2 * j + b, 2 * j + b, b, g.hT, 0)
            for n in range(2):
                body(NT + n, n, n, g.hcT, 1)

        @block.sync
        def _(sp):
            def load(n, at, b, hT, s):
                if not (isinstance(n, int) and n < 2):
                    sp.wait_ge(scaled, n - 1)
                src = i["x"][0] if s == 0 else i["ctx"][0]
                sp.dma_start(xr[:, b, :], src[bass.ds(at * P, P), :]).then_inc(loaded[b], 16)
            tiles(sp, load)

        @block.scalar
        def _(act):
            def half(n, at, b, hT, s):
                act.wait_ge(turned, n + 1)
                for k in range(4, KT):
                    ins = act.activation(hT[:, k, bass.ds(at * P, P)], tp[:, b, k, :], ACT.Identity,
                                         bias=g.mods[:, s, k:k + 1], scale=g.scale1[:, s, k:k + 1])
                ins.then_inc(out_a, 1)

            def tile(n, at, b, hT, s):
                act.wait_ge(loaded[b], (n - b) * 8 + 16)
                if not (isinstance(n, int) and n == 0):
                    act.wait_ge(summed, n)
                if not (isinstance(n, int) and n < 2):
                    act.wait_ge(inv, n - 1)
                act.activation(sq[:, :], xr[:, b, :], ACT.Square, accum_out=ss[:, b, :]).then_inc(summed, 1)
                act.wait_ge(inv, n + 1)
                if not (isinstance(n, int) and n < 2):
                    act.wait_ge(scaled, n - 1)
                act.activation(rs[:, b, :], ss[:, b, :], ACT.Sqrt).then_inc(root, 1)
                half(n, at, b, hT, s)
            tiles(act, tile)

        @block.vector
        def _(ve):
            def tile(n, at, b, hT, s):
                ve.wait_ge(summed, n + 1)
                ve.tensor_scalar(ss[:, b, :], ss[:, b, :], 1.0 / D, EPS, ALU.mult, ALU.add).then_inc(dve, 1)
                ve.wait_ge(dve, n + 1)
                ve.reciprocal(ss[:, b, :], ss[:, b, :]).then_inc(inv, 1)
                ve.wait_ge(root, n + 1)
                if not (isinstance(n, int) and n < 2):
                    ve.wait_ge(turned, n - 1)
                ve.tensor_scalar(xn[:, b, :], xr[:, b, :], rs[:, b, :], None, ALU.mult).then_inc(scaled, 1)
                ve.wait_ge(turned, n + 1)
                for k in range(4):
                    ins = ve.tensor_scalar(hT[:, k, bass.ds(at * P, P)], tp[:, b, k, :], g.scale1[:, s, k:k + 1],
                                           g.mods[:, s, k:k + 1], ALU.mult, ALU.add)
                ins.then_inc(out_v, 1)
            tiles(ve, tile)
            ve.wait_ge(out_a, NS)

        @block.tensor
        def _(pe):
            def turn(n, at, b, hT, s):
                pe.wait_ge(scaled, n + 1)
                if not (isinstance(n, int) and n < 2):
                    pe.wait_ge(out_v, n - 1)
                    pe.wait_ge(out_a, n - 1)
                for k in range(KT):
                    ins = pe.transpose(tp[:, b, k, :], xn[:, b, k * P:(k + 1) * P], g.ident[:, :])
                ins.then_inc(turned, 1)
            tiles(pe, turn)
            pe.wait_ge(out_v, NS)
            pe.wait_ge(out_a, NS)


def stage3(e, g):
    nc, i = e.nc, e.i
    PW = 256
    order = [2, 0, 1] + list(range(3, 9))
    CH = T // 512
    qk = [("k", 4, n) for n in range(CH)] + [("kc", 4, 0)] + [("q", ct, n) for ct in range(4) for n in range(CH)]
    hy = [(ct, n) for ct in range(12) for n in range(CH)]
    with e.stage() as st:
        w = e.sb(st, "win", [P, 3, KT, PW])
        cos = e.sb(st, "cos", [P, T])
        sin = e.sb(st, "sin", [P, T])
        ones = e.sb(st, "head_ones", [P, P])
        swap = e.sb(st, "pair_swap", [P, P])
        qw = e.sb(st, "qw", [P, 2, 512])
        sq = e.sb(st, "qsq", [P, 2, 512])
        rs = e.sb(st, "qrs", [P, 2, 512])
        rot = e.sb(st, "rot", [P, 2, 512])
        u = e.sb(st, "hu", [P, 2, T + 2])
        y = e.sb(st, "hyv", [P, 2, T])
        z = [m[:, :].rearrange("p (q c) -> p q c", q=Q) for m in (cos, sin)]
        mp = e.ps(st, "proj", [P, 4, 512])
        ap = e.ps(st, "paux", [P, 4, 512])
        ld = e.sem("s3_tables_loaded")
        ldw = [e.sem(f"s3_weights_loaded{b}") for b in range(3)]
        wdone = e.sem("s3_piece_used")
        mm = e.sem("s3_qk_product")
        w_qw = e.sem("s3_weighted")
        aux = e.sem("s3_norm_and_swap_product")
        inv = e.sem("s3_norm_inverted")
        root = e.sem("s3_rstd")
        auxr = e.sem("s3_swap_read")
        rotd = e.sem("s3_rotated")
        st_q = [e.sem(f"s3_stored{b}") for b in range(2)]
        v_mm = e.sem("s3_value_product")
        v_cp = e.sem("s3_value_copied")
        h_mm = e.sem("s3_hyena_product")
        h_cp = e.sem("s3_hyena_copied")
        conv = e.sem("s3_convolved")
        h_tr = e.sem("s3_hyena_turned")
        z_cp = e.sem("s3_hyena_turned_copied")
        st_z = [e.sem(f"s3_hyena_stored{b}") for b in range(2)]
        dve = e.sem("s3_dve")
        zeroed = e.sem("s3_zeroed")
        NV = NT + 2
        kpos = {"k": lambda n: C + P + 512 * n, "kc": lambda n: 0}
        block = st.enter_context(nc.Block())

        @block.sync
        def _(sp):
            for n, pc in enumerate(order):
                if n >= 3:
                    sp.wait_ge(wdone, n - 2)
                src = i["w_in"][0, :, pc * PW:(pc + 1) * PW].rearrange("(k p) c -> p k c", p=P)
                sp.dma_start(w[:, n % 3, :, :], src).then_inc(ldw[n % 3], 16)
                if n == 0:
                    for dst, src in ((ones, "head_ones"), (swap, "pair_swap"), (cos, "rope_cos"), (sin, "rope_sin")):
                        sp.dma_start(dst[:, :], i[src]).then_inc(ld, 16)
                    sp.dma_start(g.kT[HD:HD + 1, :, :].rearrange("p a t -> p (a t)"), i["key_bias"]).then_inc(ld, 16)

        @block.tensor
        def _(pe):
            pe.wait_ge(ld, 16 * 5)

            def product(n, kind, ct, c):
                pc = order.index(ct // 2)
                pe.wait_ge(ldw[pc % 3], 16 * (pc // 3 + 1))
                if n >= 4:
                    pe.wait_ge(w_qw, n - 3)
                N = C if kind == "kc" else 512
                for k in range(KT):
                    rhs = g.hcT[:, k, :] if kind == "kc" else g.hT[:, k, c * 512:(c + 1) * 512]
                    ins = pe.matmul(mp[:, n % 4, 0:N], w[:, pc % 3, k, (ct % 2) * P:(ct % 2 + 1) * P], rhs,
                                    start=(k == 0), stop=(k == KT - 1))
                ins.then_inc(mm, 1)

            def norm(n, kind):
                N = C if kind == "kc" else 512
                pe.wait_ge(w_qw, n + 1)
                if n >= 2:
                    pe.wait_ge(auxr, n - 1)
                b = 2 * (n % 2)
                pe.matmul(ap[:, b, 0:N], ones[:, :], sq[:, n % 2, 0:N], start=True, stop=True)
                pe.matmul(ap[:, b + 1, 0:N], swap[:, :], qw[:, n % 2, 0:N], start=True, stop=True).then_inc(aux, 1)

            for n, (kind, ct, c) in enumerate(qk):
                product(n, kind, ct, c)
                if n >= 1:
                    norm(n - 1, qk[n - 1][0])
                if n == 4:
                    for t in range(NV):
                        if t >= 4:
                            pe.wait_ge(v_cp, t - 3)
                        else:
                            pe.wait_ge(w_qw, n + 1)
                        for k in range(KT):
                            x = g.hT[:, k, t * P:(t + 1) * P] if t < NT else g.hcT[:, k, (t - NT) * P:(t - NT + 1) * P]
                            ins = pe.matmul(mp[:, (t + 1) % 4, 0:P], x, w[:, 0, k, P:2 * P],
                                            start=(k == 0), stop=(k == KT - 1))
                        ins.then_inc(v_mm, 1)
                    pe.wait_ge(v_cp, NV)
                    pe.nop().then_inc(wdone, 1)
                if kind == "q" and ct % 2 == 1 and c == CH - 1:
                    pe.wait_ge(mm, n + 1)
                    pe.nop().then_inc(wdone, 1)
            norm(len(qk) - 1, "q")
            pe.wait_ge(w_qw, len(qk))
            pe.wait_ge(auxr, len(qk))

            def turn(ct):
                pe.wait_ge(conv, ct + 1)
                for b in range(4):
                    if ct >= 1:
                        pe.wait_ge(z_cp, 4 * ct + b - 3)
                    for a in range(4):
                        ins = pe.transpose(ap[:, b, a * P:(a + 1) * P], y[:, ct % 2, 4 * b + a::Q], g.ident[:, :])
                    ins.then_inc(h_tr, 1)

            for n, (ct, c) in enumerate(hy):
                pc = 3 + ct // 2
                pe.wait_ge(ldw[pc % 3], 16 * (pc // 3 + 1))
                if n >= 4:
                    pe.wait_ge(h_cp, n - 3)
                for k in range(KT):
                    ins = pe.matmul(mp[:, n % 4, :], w[:, pc % 3, k, (ct % 2) * P:(ct % 2 + 1) * P],
                                    g.hT[:, k, c * 512:(c + 1) * 512], start=(k == 0), stop=(k == KT - 1))
                ins.then_inc(h_mm, 1)
                if ct % 2 == 1 and c == CH - 1:
                    pe.wait_ge(h_mm, n + 1)
                    pe.nop().then_inc(wdone, 1)
                if ct >= 1 and c == 1:
                    turn(ct - 1)
            turn(11)

        @block.scalar
        def _(act):
            def weigh(n, kind, ct):
                N = C if kind == "kc" else 512
                col = C_QN if kind == "q" else C_KN
                act.wait_ge(mm, n + 1)
                if n >= 2:
                    act.wait_ge(aux, n - 1)
                    act.wait_ge(rotd, n - 1)
                act.activation(qw[:, n % 2, 0:N], mp[:, n % 4, 0:N], ACT.Identity, scale=g.cols[:, col:col + 1])
                act.activation(sq[:, n % 2, 0:N], mp[:, n % 4, 0:N], ACT.Square).then_inc(w_qw, 1)

            def rstd(n, kind):
                N = C if kind == "kc" else 512
                act.wait_ge(inv, n + 1)
                act.activation(rs[:, n % 2, 0:N], rs[:, n % 2, 0:N], ACT.Sqrt).then_inc(root, 1)

            for n, (kind, ct, c) in enumerate(qk):
                weigh(n, kind, ct)
                if n >= 1:
                    rstd(n - 1, qk[n - 1][0])
                if n == 4:
                    for t in range(NV):
                        act.wait_ge(v_mm, t + 1)
                        at = 3 + t if t < NT else t - NT
                        act.copy(g.v[:, at, :], mp[:, (t + 1) % 4, 0:P]).then_inc(v_cp, 1)
            rstd(len(qk) - 1, "q")
            act.wait_ge(zeroed, 5)
            act.wait_ge(rotd, len(qk))

            def turned(ct):
                for b in range(4):
                    act.wait_ge(h_tr, 4 * ct + b + 1)
                    if ct >= 2 and b == 0:
                        act.wait_ge(st_z[ct % 2], 16 * (ct // 2))
                    act.copy(z[ct % 2][:, 4 * b:4 * b + 4, :].rearrange("p q c -> p (q c)"), ap[:, b, :]).then_inc(z_cp, 1)
                act.wait_ge(z_cp, 4 * ct + 4)
                dst = g.hy_dram[ct // 4].rearrange("(p q) c -> p q c", q=Q)[:, :, (ct % 4) * P:(ct % 4 + 1) * P]
                act.dma_start(dst, z[ct % 2]).then_inc(st_z[ct % 2], 16)

            for n, (ct, c) in enumerate(hy):
                act.wait_ge(h_mm, n + 1)
                if ct >= 2 and c == 0:
                    act.wait_ge(conv, ct - 1)
                act.copy(u[:, ct % 2, 1 + c * 512:1 + (c + 1) * 512], mp[:, n % 4, :]).then_inc(h_cp, 1)
                if ct >= 1 and c == 2:
                    turned(ct - 1)
            turned(11)
            for b in range(2):
                act.wait_ge(st_z[b], 16 * 6)

        @block.vector
        def _(ve):
            ch = Chain(ve, dve)
            ve.memset(u[:, :, 0:1], 0.0).then_inc(zeroed, 1)
            ve.memset(u[:, :, T + 1:T + 2], 0.0).then_inc(zeroed, 1)
            ve.memset(g.v[:, 2:20:17, :], 0.0).then_inc(zeroed, 1)
            for n, (kind, ct, c) in enumerate(qk):
                N = C if kind == "kc" else 512
                b = n % 2
                ve.wait_ge(aux, n + 1)
                if n >= 2:
                    ve.wait_ge(st_q[b], 32 * (n // 2))
                ch(ve.tensor_scalar(rs[:, b, 0:N], ap[:, 2 * b, 0:N], 1.0 / HD, EPS, ALU.mult, ALU.add))
                ch.wait()
                ve.reciprocal(rs[:, b, 0:N], rs[:, b, 0:N]).then_inc(inv, 1)
                if kind == "kc":
                    ve.wait_ge(root, n + 1)
                    ve.tensor_tensor(rot[:, b, 0:N], qw[:, b, 0:N], rs[:, b, 0:N], ALU.mult).then_inc(rotd, 1)
                    ve.nop().then_inc(auxr, 1)
                    continue
                ch(ve.tensor_tensor(rot[:, b, :], ap[:, 2 * b + 1, :], sin[:, c * 512:(c + 1) * 512], ALU.mult))
                ch(ve.tensor_tensor(qw[:, b, :], qw[:, b, :], cos[:, c * 512:(c + 1) * 512], ALU.mult))
                ch.wait()
                ve.tensor_tensor(rot[:, b, :], rot[:, b, :], qw[:, b, :], ALU.add).then_inc(auxr, 1)
                ve.wait_ge(root, n + 1)
                ve.wait_ge(auxr, n + 1)
                ve.tensor_tensor(rot[:, b, :], rot[:, b, :], rs[:, b, :], ALU.mult).then_inc(rotd, 1)
            for ct in range(12):
                b = ct % 2
                ve.wait_ge(h_cp, 4 * ct + 4)
                if ct >= 2:
                    ve.wait_ge(h_tr, 4 * ct - 4)
                wc = [g.cols[:, C_CW + 12 * j + ct:C_CW + 12 * j + ct + 1] for j in range(3)]
                ch(ve.tensor_scalar(y[:, b, :], u[:, b, 1:T + 1], wc[1], g.cols[:, C_CB + ct:C_CB + ct + 1],
                                    ALU.mult, ALU.add))
                ch.wait()
                ch(ve.scalar_tensor_tensor(out=y[:, b, :], in0=u[:, b, 0:T], scalar=wc[0], in1=y[:, b, :],
                                           op0=ALU.mult, op1=ALU.add))
                ch.wait()
                ve.scalar_tensor_tensor(out=y[:, b, :], in0=u[:, b, 2:T + 2], scalar=wc[2], in1=y[:, b, :],
                                        op0=ALU.mult, op1=ALU.add).then_inc(conv, 1)

        @block.gpsimd
        def _(pool):
            pool.memset(g.kT[0:HD, :, C:C + P], 0.0).then_inc(zeroed, 1)
            pool.memset(g.kT[0:HD, :, C + P + T:], 0.0).then_inc(zeroed, 1)
            for n, (kind, ct, c) in enumerate(qk):
                N = C if kind == "kc" else 512
                pool.wait_ge(rotd, n + 1)
                for h in range(2):
                    src = rot[HD * h:HD * h + HD, n % 2, 0:N]
                    if kind == "q":
                        dst = g.q_dram[4 * c:4 * c + 4, :, 2 * ct + h, :].rearrange("b d t -> d b t")
                        src = src.rearrange("p (b t) -> p b t", t=P)
                    else:
                        dst = g.kT[0:HD, h, kpos[kind](c):kpos[kind](c) + N]
                    pool.dma_start(dst, src).then_inc(st_q[n % 2], 16)
            for b in range(2):
                pool.wait_ge(st_q[b], 32 * ((len(qk) - b + 1) // 2))
            pool.wait_ge(zeroed, 5)


def stage4(e, g):
    nc, i = e.nc, e.i
    LN = 2
    jobs = [(r, o, l) for r in range(NL // LN) for o in range(2) for l in range(LN)]
    NJ, NC = len(jobs), 8
    order = []
    for b in range(0, NJ, LN):
        order += [(s, b + l) for s in ("I", "II", "V") for l in range(LN)]
    uses, use_of = [], {}
    for s, j in order:
        for c in range({"I": 8, "II": NC, "V": 4}[s]):
            use_of[s, j, c] = len(uses)
            uses.append("v" if s == "V" else "a")
    nth = [sum(x == uses[n] for x in uses[:n + 1]) for n in range(len(uses))]
    with e.stage() as st:
        fwd = e.sb(st, "fwd4", [P, Q, 2, P])
        inv = e.sb(st, "inv4", [P, Q, 2, P])
        mid = e.sb(st, "mid4", [P, 10, P])
        skip = e.sb(st, "skip", [P, LN, LANE])
        zr = [e.sb(st, f"zr{l}", [P, Q, LANE]) for l in range(LN)]
        gt = [e.sb(st, f"gt{l}", [P, Q, LANE]) for l in range(LN)]
        sp_ = [e.sb(st, f"sp{l}", [P, Q, 2, LANE]) for l in range(LN)]
        yx = [e.sb(st, f"yx{l}", [P, 32, LANE]) for l in range(LN)]
        yh = [e.sb(st, f"yh{l}", [P, 32, LANE]) for l in range(LN)]
        ab = e.sb(st, "ab", [P, 2, 2, 512])
        prod = e.ps(st, "prod", [P, 2, 3, 512])
        ob = e.ps(st, "ob", [P, 2, 512])
        y_dram = e.dram("hy_y", [LN, Q, 2, P, LANE])
        v_dram = e.dram("hy_v", [LN, Q, 2, P, LANE])
        ld = e.sem("s4_tables_loaded")
        ld_z = [e.sem(f"s4_z_loaded{l}") for l in range(LN)]
        ld_g = [e.sem(f"s4_gate_loaded{l}") for l in range(LN)]
        ld_h = [e.sem(f"s4_filter_loaded{l}") for l in range(LN)]
        i_mm = e.sem("s4_I_product")
        i_cp = [e.sem(f"s4_I_copied{l}") for l in range(LN)]
        y_st = [e.sem(f"s4_Y_stored{l}") for l in range(LN)]
        y_ld = [e.sem(f"s4_Y_loaded{l}") for l in range(LN)]
        x_mm = e.sem("s4_spectra_product")
        x_cp = e.sem("s4_X_copied")
        ab_ok = e.sem("s4_spectra_multiplied")
        v_mm = e.sem("s4_II_inverse_product")
        v_cp = [e.sem(f"s4_II_inverse_copied{l}") for l in range(LN)]
        v_st = [e.sem(f"s4_V_stored{l}") for l in range(LN)]
        v_ld = [[e.sem(f"s4_V_loaded{l}_{c}") for c in range(4)] for l in range(LN)]
        o_mm = e.sem("s4_conv_product")
        o_rd = e.sem("s4_conv_read")
        z_ok = [e.sem(f"s4_z_ready{l}") for l in range(LN)]
        z_st = [e.sem(f"s4_z_stored{l}") for l in range(LN)]
        act_rd = e.sem("s4_bank_read_by_scalar")
        dve = e.sem("s4_dve")
        block = st.enter_context(nc.Block())

        def bank_free(pe, s, j, c):
            n = use_of[s, j, c]
            if n >= 2:
                pe.wait_ge(act_rd if uses[n - 2] == "a" else o_rd, nth[n - 2])
            return n % 2

        @block.sync
        def _(sp):
            for dst, src in ((fwd[:, :, :, :], i["dft_fwd"].rearrange("p (q r k) -> p q r k", q=Q, r=2)),
                             (mid[:, :, :], i["dft_mid"].rearrange("p (m k) -> p m k", m=10)),
                             (inv[:, :, :, :], i["dft_inv"].rearrange("p (q r k) -> p q r k", q=Q, r=2))):
                sp.dma_start(dst, src).then_inc(ld, 16)

            def inputs(j):
                r, o, l = jobs[j]
                ln = LN * r + l
                if o == 0:
                    if r >= 1:
                        sp.wait_ge(z_st[l], 16 * r)
                    src = g.hy_dram[0].rearrange("(p q) c -> p q c", q=Q)[:, :, ln * LANE:(ln + 1) * LANE]
                    sp.dma_start(zr[l][:, :, :], src).then_inc(ld_z[l], 16)
                k = j // LN
                if k >= 1:
                    sp.wait_ge(z_ok[l], 4 * k)
                src = g.hy_dram[o + 1].rearrange("(p q) c -> p q c", q=Q)[:, :, ln * LANE:(ln + 1) * LANE]
                sp.dma_start(gt[l][:, :, :], src).then_inc(ld_g[l], 16)
                src = i["hy_skip"][0, o, ln * LANE:(ln + 1) * LANE].partition_broadcast(P)
                sp.dma_start(skip[:, l, :], src).then_inc(ld_g[l], 16)

            def filt(j):
                r, o, l = jobs[j]
                if j >= LN:
                    sp.wait_ge(x_mm, NC * (j - LN + 1))
                for s in range(4):
                    src = g.filt_dram[o, LN * r + l].rearrange("q r (s g) c -> s (q r) (g c)", s=4)[s]
                    sp.dma_start(yh[l][32 * s:32 * s + 32, :, :].rearrange("p g c -> p (g c)"), src).then_inc(ld_h[l], 16)

            for j in range(LN):
                inputs(j)
            for j in range(LN):
                filt(j)
            for s, j in order:
                r, o, l = jobs[j]
                k = j // LN
                if s == "I":
                    for c in range(4):
                        sp.wait_ge(i_cp[l], 8 * k + 2 * c + 2)
                        dst = y_dram[l, 4 * c:4 * c + 4].rearrange("q r k c -> k (q r) c")
                        sp.dma_start(dst, sp_[l][:, 4 * c:4 * c + 4, :, :].rearrange("p q r c -> p (q r) c"))\
                          .then_inc(y_st[l], 16)
                    sp.wait_ge(y_st[l], 64 * (k + 1))
                    if k >= 1:
                        sp.wait_ge(v_st[l], 128 * k)
                    for c in range(4):
                        src = y_dram[l].rearrange("q r (s g) c -> s (q r) (g c)", s=4)[c]
                        sp.dma_start(yx[l][32 * c:32 * c + 32, :, :].rearrange("p g c -> p (g c)"), src)\
                          .then_inc(y_ld[l], 16)
                if s == "II":
                    for half in range(2):
                        sp.wait_ge(v_cp[l], NC * k + 4 * half + 4)
                        for c in range(4):
                            dst = v_dram[l].rearrange("q r (s g) c -> s (q r) g c", s=4)[c, :, 16 * half:16 * half + 16]
                            sp.dma_start(dst, yx[l][32 * c:32 * c + 32, 16 * half:16 * half + 16, :]).then_inc(v_st[l], 16)
                    sp.wait_ge(v_st[l], 128 * (k + 1))
                    for c in range(4):
                        src = v_dram[l, 4 * c:4 * c + 4].rearrange("q r k c -> k (q r) c")
                        sp.dma_start(sp_[l][:, 4 * c:4 * c + 4, :, :].rearrange("p q r c -> p (q r) c"), src)\
                          .then_inc(v_ld[l][c], 16)
                    if j + LN < NJ:
                        filt(j + LN)
                if s == "V":
                    if o == 1:
                        sp.wait_ge(z_ok[l], 4 * (k + 1))
                        dst = g.hyo_dram.rearrange("(p q) c -> p q c", q=Q)[:, :, (LN * r + l) * LANE:(LN * r + l + 1) * LANE]
                        sp.dma_start(dst, zr[l][:, :, :]).then_inc(z_st[l], 16)
                    if j + LN < NJ:
                        inputs(j + LN)
            for l in range(LN):
                sp.wait_ge(z_st[l], 16 * (NL // LN))

        @block.tensor
        def _(pe):
            pe.wait_ge(ld, 48)
            for s, j in order:
                r, o, l = jobs[j]
                k = j // LN
                if s == "I":
                    if o == 0:
                        pe.wait_ge(ld_z[l], 16 * (r + 1))
                    else:
                        pe.wait_ge(z_ok[l], 4 * k)
                    for c in range(8):
                        b = bank_free(pe, s, j, c)
                        for a in range(4):
                            ins = pe.matmul(ob[:, b, a * LANE:(a + 1) * LANE], fwd[:, 2 * c + a // 2, a % 2, :],
                                            zr[l][:, 2 * c + a // 2, :], start=True, stop=True)
                        ins.then_inc(i_mm, 1)
                if s == "II":
                    pe.wait_ge(y_ld[l], 64 * (k + 1))
                    pe.wait_ge(ld_h[l], 64 * (k + 1))
                    for c in range(NC + 1):
                        if c < NC:
                            n = j * NC + c
                            if n >= 2:
                                pe.wait_ge(ab_ok, n - 1)
                            for m in range(3):
                                src = yx[l] if m == 0 else yh[l]
                                if c == 0:
                                    pe.matmul(prod[:, n % 2, m, 0:LANE], mid[:, 5 + m, :], src[:, 0, :],
                                              start=True, stop=True)
                                    ins = pe.matmul(prod[:, n % 2, m, LANE:512], mid[:, m, :],
                                                    src[:, 1:4, :].rearrange("p g c -> p (g c)"), start=True, stop=True)
                                else:
                                    ins = pe.matmul(prod[:, n % 2, m, :], mid[:, m, :],
                                                    src[:, 4 * c:4 * c + 4, :].rearrange("p g c -> p (g c)"),
                                                    start=True, stop=True)
                            ins.then_inc(x_mm, 1)
                        if c >= 1:
                            cc, n = c - 1, j * NC + c - 1
                            b = bank_free(pe, s, j, cc)
                            pe.wait_ge(ab_ok, n + 1)
                            if cc == 0:
                                for m in range(2):
                                    pe.matmul(ob[:, b, 0:LANE], mid[:, 8 + m, :], ab[:, n % 2, m, 0:LANE],
                                              start=(m == 0), stop=(m == 1))
                                for m in range(2):
                                    ins = pe.matmul(ob[:, b, LANE:512], mid[:, 3 + m, :], ab[:, n % 2, m, LANE:512],
                                                    start=(m == 0), stop=(m == 1))
                            else:
                                for m in range(2):
                                    ins = pe.matmul(ob[:, b, :], mid[:, 3 + m, :], ab[:, n % 2, m, :],
                                                    start=(m == 0), stop=(m == 1))
                            ins.then_inc(v_mm, 1)
                if s == "V":
                    for c in range(4):
                        pe.wait_ge(v_ld[l][c], 16 * (k + 1))
                        b = bank_free(pe, s, j, c)
                        for a in range(4):
                            for ri in range(2):
                                ins = pe.matmul(ob[:, b, a * LANE:(a + 1) * LANE], inv[:, 4 * c + a, ri, :],
                                                sp_[l][:, 4 * c + a, ri, :], start=(ri == 0), stop=(ri == 1))
                        ins.then_inc(o_mm, 1)

        @block.scalar
        def _(act):
            ni = nv = na = 0
            for s, j in order:
                r, o, l = jobs[j]
                k = j // LN
                if s == "I":
                    for c in range(8):
                        ni += 1
                        act.wait_ge(i_mm, ni)
                        if k >= 1 and c == 0:
                            act.wait_ge(o_mm, 4 * (j - LN + 1))
                        act.copy(sp_[l][:, 2 * c:2 * c + 2, :, :].rearrange("p q r c -> p (q r c)"),
                                 ob[:, use_of[s, j, c] % 2, :]).then_inc(act_rd, 1)
                        na += 1
                        act.wait_ge(act_rd, na)
                        act.nop().then_inc(i_cp[l], 1)
                if s == "II":
                    for c in range(NC + 1):
                        if c < NC:
                            n = j * NC + c
                            act.wait_ge(x_mm, n + 1)
                            if n >= 2:
                                act.wait_ge(ab_ok, n - 1)
                            if n >= 2:
                                act.wait_ge(v_mm, n - 1)
                            act.copy(ab[:, n % 2, 0, :], prod[:, n % 2, 0, :]).then_inc(x_cp, 1)
                        if c >= 1:
                            cc = c - 1
                            nv += 1
                            act.wait_ge(v_mm, nv)
                            act.copy(yx[l][:, 4 * cc:4 * cc + 4, :].rearrange("p g c -> p (g c)"),
                                     ob[:, use_of[s, j, cc] % 2, :]).then_inc(act_rd, 1)
                            na += 1
                            act.wait_ge(act_rd, na)
                            act.nop().then_inc(v_cp[l], 1)

        @block.vector
        def _(ve):
            ch = Chain(ve, dve)
            no = 0
            for s, j in order:
                r, o, l = jobs[j]
                k = j // LN
                if s == "II":
                    for c in range(NC):
                        n = j * NC + c
                        ve.wait_ge(x_cp, n + 1)
                        if n >= 2:
                            ve.wait_ge(v_mm, n - 1)
                        ch(ve.tensor_tensor(ab[:, n % 2, 1, :], ab[:, n % 2, 0, :], prod[:, n % 2, 2, :], ALU.mult))
                        ch.wait()
                        ve.tensor_tensor(ab[:, n % 2, 0, :], ab[:, n % 2, 0, :], prod[:, n % 2, 1, :], ALU.mult)\
                            .then_inc(ab_ok, 1)
                if s == "V":
                    sk = skip[:, l, :].unsqueeze(1).broadcast_to([P, 4, LANE])
                    ve.wait_ge(ld_g[l], 32 * (k + 1))
                    for c in range(4):
                        zc = zr[l][:, 4 * c:4 * c + 4, :]
                        ve.wait_ge(i_mm, 8 * (j + 1))
                        ch(ve.tensor_tensor(zc, zc, sk, ALU.mult))
                        ch.wait()
                        no += 1
                        ve.wait_ge(o_mm, no)
                        ve.tensor_tensor(zc, ob[:, use_of[s, j, c] % 2, :].rearrange("p (q c) -> p q c", q=4), zc, ALU.add)\
                            .then_inc(o_rd, 1)
                        ve.wait_ge(o_rd, no)
                        ve.tensor_tensor(zc, zc, gt[l][:, 4 * c:4 * c + 4, :], ALU.mult).then_inc(z_ok[l], 1)


class Tile:

    def __init__(self, half, off):
        self.half, self.par = half + off // 2, off % 2
        self.n = 2 * half + off

    def back(self, k):
        return Tile(self.half, self.par - k)


def wait(eng, sem, value):
    if not (isinstance(value, int) and value <= 0):
        eng.wait_ge(sem, value)


def pipeline(eng, step):
    step(Tile(0, -1), True, False, False, False)
    step(Tile(0, 0), True, True, False, False)
    step(Tile(0, 1), True, True, True, False)
    with eng.Fori(1, NT // 2 - 1) as j:
        for par in range(2):
            step(Tile(j, par), True, True, True, True)
    step(Tile(0, NT - 2), True, True, True, True)
    step(Tile(0, NT - 1), False, True, True, True)
    step(Tile(0, NT), False, False, True, True)
    step(Tile(0, NT + 1), False, False, False, True)


def stage5(e, g):
    nc, i = e.nc, e.i
    KEYS = C + 3 * P
    with e.stage() as st:
        wo = e.sb(st, "wo", [P, KT, D])
        rw = e.sb(st, "rw", [P, KT, NG + NE])
        rb = e.sb(st, "rb", [P, NG + NE])
        g1 = e.sb(st, "g1row", [P, D])
        mask = e.sb(st, "mask", [P, KEYS])
        nsink = e.sb(st, "nsink", [P, NH])
        sink = e.sb(st, "sink", [P, NH])
        upper = e.sb(st, "upper", [P, P])
        ones = e.sb(st, "ones", [P, P])
        rank8 = e.sb(st, "rank8", [P, 8])
        slot0 = e.sb(st, "slot0", [P, NE])
        token = e.sb(st, "token", [P, NT], I32)
        fill = e.sb(st, "fill", [P, (NE * CAP + P) * 2 // P], I32)
        qb = [e.sb(st, f"qb{b}", [HD + 1, NH, P]) for b in range(2)]
        pr = [e.sb(st, f"pr{b}", [P, NH, KEYS]) for b in range(2)]
        mx = e.sb(st, "mx", [P, 2, NH])
        nm = e.sb(st, "nm", [P, 2, NH])
        rsum = e.sb(st, "rsum", [P, 2, NH])
        esk = e.sb(st, "esk", [P, 2, NH])
        pt = e.sb(st, "pt", [P, 2, KEYS])
        mix = [e.sb(st, f"mix{b}", [P, 2, HW]) for b in range(2)]
        sqs = e.sb(st, "sqs", [P, D])
        ms = e.sb(st, "ms", [P, 2, 2])
        nw = e.sb(st, "nw", [P, 3, 2])
        n2 = e.sb(st, "n2", [P, 4])
        mixn = e.sb(st, "mixn", [P, 2, HW])
        mixT = e.sb(st, "mixT", [P, KT, P])
        xr = [e.sb(st, f"xres{b}", [P, D]) for b in range(2)]
        x2 = [e.sb(st, f"x2_{b}", [P, D]) for b in range(2)]
        xn = [e.sb(st, f"xn2_{b}", [P, D]) for b in range(2)]
        h2T = e.sb(st, "h2T", [P, KT, P])
        lg = e.sb(st, "lg", [P, 2, NG + NE])
        gexp = e.sb(st, "gexp", [P, 2, NG])
        r4 = e.sb(st, "r4", [P, 2, 16])
        oh = e.sb(st, "oh", [P, 4, 8])
        selg = e.sb(st, "selg", [P, NG, EPG])
        pick = e.sb(st, "pick", [P, 2, 3, NE])
        pos = e.sb(st, "pos", [P, 2, NE])
        idx = e.sb(st, "idx", [P, 2, 2], I32)
        rec = e.sb(st, "rec", [P, 2, 2, 2], I32)
        S = e.ps(st, "S", [P, 2, 512])
        PT = e.ps(st, "PT", [P, 2, 512])
        O = e.ps(st, "O", [P, NH, HD])
        M = e.ps(st, "M", [P, 2, 512])
        R = e.ps(st, "R", [P, 512])

        ld = e.sem("s5_tables_loaded")
        setup = e.sem("s5_set_up")
        filled = e.sem("s5_table_filled")
        ld_q = [e.sem(f"s5_queries_loaded{b}") for b in range(2)]
        ld_x = [e.sem(f"s5_rows_loaded{b}") for b in range(2)]
        qk = e.sem("s5_scores")
        sm = e.sem("s5_scores_masked")
        nmx = e.sem("s5_maximum")
        ex = e.sem("s5_exponentials")
        esn = e.sem("s5_sink_argument")
        eso = e.sem("s5_sink_exponential")
        tp = e.sem("s5_exponentials_turned")
        tc = e.sem("s5_turned_copied")
        pv = e.sem("s5_head_values")
        att = e.sem("s5_attention_scaled")
        sqa = e.sem("s5_mixer_squares")
        mxn = e.sem("s5_mixer_normalised")
        t1 = e.sem("s5_mixer_turned")
        t1v = e.sem("s5_mixer_turned_copied_v")
        t1a = e.sem("s5_mixer_turned_copied_a")
        op = e.sem("s5_projected")
        res = e.sem("s5_residual_added")
        sq2 = e.sem("s5_residual_squares")
        xnd = e.sem("s5_residual_normalised")
        t2 = e.sem("s5_residual_turned")
        t2v = e.sem("s5_residual_turned_copied_v")
        t2a = e.sem("s5_residual_turned_copied_a")
        rt = e.sem("s5_router_product")
        lgd = e.sem("s5_logits_copied")
        rt1 = e.sem("s5_experts_picked")
        gex = e.sem("s5_gate_exponentials")
        px = e.sem("s5_prefix_product")
        pxr = e.sem("s5_prefix_read")
        rec_ok = e.sem("s5_records_ready")
        sc = [e.sem(f"s5_records_scattered{b}") for b in range(2)]
        st_x = [e.sem(f"s5_rows_stored{b}") for b in range(2)]
        dve = e.sem("s5_dve")
        passed = e.sem("s5_waits_passed_v")
        passed_p = e.sem("s5_waits_passed_p")
        block = st.enter_context(nc.Block())

        tables = [(mask[:, :], i["mask"]), (sink[:, :], i["attn_sink"][0].partition_broadcast(P)),
                  (upper[:, :], i["upper"]), (rank8[:, :], i["rank8"]), (slot0[:, :], i["slot0"]),
                  (token[:, :], i["token"]),
                  (rb[:, 0:NG], i["router_g_b"][0].partition_broadcast(P)),
                  (rb[:, NG:], i["router_e_b"][0].partition_broadcast(P)),
                  (rw[:, :, 0:NG], i["router_g_w"][0].rearrange("(k p) n -> p k n", p=P)),
                  (rw[:, :, NG:], i["router_e_w"][0].rearrange("(k p) n -> p k n", p=P)),
                  (g1[:, :], g.gate_dram[0:D].partition_broadcast(P)),
                  (wo[:, :, :], i["w_out"][0].rearrange("(k p) n -> p k n", p=P))]

        @block.sync
        def _(sp):
            for dst, src in tables:
                sp.dma_start(dst, src).then_inc(ld, 16)

            def step(t, scores, values, project, place):
                if scores:
                    b = t.back(-1)
                    wait(sp, qk, 8 * (b.n - 1))
                    sp.dma_start(qb[b.par][0:HD, :, :], g.q_dram[bass.ds(b.n, 1)].rearrange("a d h t -> (a d) h t"))\
                      .then_inc(ld_q[b.par], 16)
                    wait(sp, mxn, b.n - 1)
                    sp.dma_start(mix[b.par][:, 1, :], g.hyo_dram[bass.ds(b.n * P, P), :]).then_inc(ld_x[b.par], 16)
                    wait(sp, res, b.n - 1)
                    sp.dma_start(xr[b.par][:, :], i["x"][0, bass.ds(b.n * P, P), :]).then_inc(ld_x[b.par], 16)
                if project:
                    b = t.back(1)
                    sp.wait_ge(res, b.n + 1)
                    sp.dma_start(e.out[0, bass.ds(b.n * P, P), :], x2[b.par][:, :]).then_inc(st_x[b.par], 16)
                    sp.wait_ge(xnd, b.n + 1)
                    sp.dma_start(g.xn_dram[bass.ds(b.n * P, P), :], xn[b.par][:, :]).then_inc(st_x[b.par], 16)
            pipeline(sp, step)
            for b in range(2):
                sp.wait_ge(st_x[b], 32 * (NT // 2))

        @block.gpsimd
        def _(pool):
            pool.memset(fill[:, :], NOWHERE).then_inc(setup, 1)
            pool.wait_ge(setup, 6)
            pool.dma_start(g.table.rearrange("(p a) c -> p (a c)", p=P), fill[:, :]).then_inc(filled, 16)
            pool.wait_ge(filled, 16)

            def step(t, scores, values, project, place):
                if place:
                    b = t.back(2)
                    pool.wait_ge(rec_ok, b.n + 1)
                    pool.sem_inc(passed_p, 1)
                    for k in range(2):
                        pool.indirect_dma_start(g.table[0:NE * CAP, :],
                                                bass.IndirectOffsetOnAxis(ap=idx[:, b.par, k:k + 1], axis=0),
                                                rec[:, b.par, k, :], None, bounds_check=NE * CAP - 1,
                                                oob_is_err=True).then_inc(sc[b.par], 16)
            pipeline(pool, step)
            for b in range(2):
                pool.wait_ge(sc[b], 32 * (NT // 2))

        @block.tensor
        def _(pe):
            pe.wait_ge(ld, 16 * len(tables))
            pe.wait_ge(setup, 6)

            def step(t, scores, values, project, place):
                nx, pj, pl = t.back(-1), t.back(1), t.back(2)

                def head(h):
                    if scores:
                        if h == 0:
                            pe.wait_ge(ld_q[nx.par], 16 * (nx.half + 1))
                        wait(pe, sm, 8 * nx.n + h)
                        q = qb[nx.par][:, h, :]
                        kv = h // 4
                        pe.matmul(S[:, 0, 0:C], q, g.kT[:, kv, 0:C], start=True, stop=True)
                        pe.matmul(S[:, 0, C:512], q, g.kT[:, kv, bass.ds(nx.n * P + C, 2 * P)], start=True, stop=True)
                        pe.matmul(S[:, 1, 0:P], q, g.kT[:, kv, bass.ds(nx.n * P + C + 2 * P, P)],
                                  start=True, stop=True).then_inc(qk, 1)
                    if values:
                        pe.wait_ge(ex, 8 * t.n + h + 1)
                        wait(pe, tc, 8 * t.n + h)
                        for a in range(5):
                            ins = pe.transpose(PT[:, a // 4, (a % 4) * P:(a % 4 + 1) * P],
                                               pr[t.par][:, h, a * P:(a + 1) * P], g.ident[:, :])
                        ins.then_inc(tp, 1)

                def head_values(h):
                    if values:
                        kv = h // 4
                        pe.wait_ge(tc, 8 * t.n + h + 1)
                        if h == 0:
                            wait(pe, att, t.n)
                        for a in range(5):
                            v = g.v[:, a, kv * HD:(kv + 1) * HD] if a < 2 else \
                                g.v[:, bass.ds(t.n + a, 1), kv * HD:(kv + 1) * HD].rearrange("p a d -> p (a d)")
                            ins = pe.matmul(O[:, h, :], pt[:, h % 2, a * P:(a + 1) * P], v,
                                            start=(a == 0), stop=(a == 4), skip_group_check=True)
                        ins.then_inc(pv, 1)

                head(0)
                if place:
                    pe.wait_ge(rt1, pl.n + 1)
                    pe.matmul(R[:, 64:64 + NE], upper[:, :], pick[:, pl.par, 2, :], start=True, stop=True)
                    pe.matmul(R[:, 128:128 + NE], ones[:, :], pick[:, pl.par, 2, :], start=True, stop=True).then_inc(px, 1)
                if project:
                    pe.wait_ge(mxn, pj.n + 1)
                    wait(pe, t2v, pj.n)
                    wait(pe, t2a, pj.n)
                    for k in range(KT):
                        ins = pe.transpose(M[:, k // 4, (k % 4) * P:(k % 4 + 1) * P],
                                           mixn[:, k // 4, (k % 4) * P:(k % 4 + 1) * P], g.ident[:, :])
                    ins.then_inc(t1, 1)
                head(1)
                head_values(0)
                head(2)
                head_values(1)
                if project:
                    pe.wait_ge(t1v, pj.n + 1)
                    pe.wait_ge(t1a, pj.n + 1)
                    for half in range(2):
                        for k in range(KT):
                            ins = pe.matmul(M[:, half, :], mixT[:, k, :], wo[:, k, half * 512:(half + 1) * 512],
                                            start=(k == 0), stop=(k == KT - 1))
                        ins.then_inc(op, 1)
                for h in range(3, 6):
                    head(h)
                    head_values(h - 1)
                if project:
                    pe.wait_ge(xnd, pj.n + 1)
                    for k in range(KT):
                        ins = pe.transpose(M[:, k // 4, (k % 4) * P:(k % 4 + 1) * P],
                                           xn[pj.par][:, k * P:(k + 1) * P], g.ident[:, :])
                    ins.then_inc(t2, 1)
                for h in range(6, 8):
                    head(h)
                    head_values(h - 1)
                head_values(7)
                if project:
                    pe.wait_ge(t2v, pj.n + 1)
                    pe.wait_ge(t2a, pj.n + 1)
                    if place:
                        pe.wait_ge(pxr, pl.n + 1)
                    for k in range(KT):
                        ins = pe.matmul(R[:, 0:NG + NE], h2T[:, k, :], rw[:, k, :], start=(k == 0), stop=(k == KT - 1))
                    ins.then_inc(rt, 1)
            pipeline(pe, step)

        @block.scalar
        def _(act):
            act.wait_ge(ld, 16 * len(tables))

            def step(t, scores, values, project, place):
                nx, pj = t.back(-1), t.back(1)

                def head(h):
                    if scores:
                        act.wait_ge(nmx, 8 * nx.n + h + 1)
                        act.activation(pr[nx.par][:, h, :], pr[nx.par][:, h, :], ACT.Exp, bias=nm[:, nx.par, h:h + 1],
                                       scale=SCALE, accum_out=rsum[:, nx.par, h:h + 1]).then_inc(ex, 1)
                    if values:
                        act.wait_ge(tp, 8 * t.n + h + 1)
                        wait(act, pv, 8 * t.n + h - 1)
                        act.copy(pt[:, h % 2, 0:512], PT[:, 0, :])
                        act.copy(pt[:, h % 2, 512:KEYS], PT[:, 1, 0:P]).then_inc(tc, 1)

                head(0)
                if place:
                    b = t.back(2)
                    act.wait_ge(rt1, b.n + 1)
                    act.activation(gexp[:, b.par, :], lg[:, b.par, 0:NG], ACT.Exp, bias=r4[:, b.par, 0:1],
                                   accum_out=r4[:, b.par, 4:5])
                    act.activation(r4[:, b.par, 5:6], r4[:, b.par, 3:4], ACT.Exp).then_inc(gex, 1)
                head(1)
                if project:
                    act.wait_ge(t1, pj.n + 1)
                    wait(act, op, 2 * pj.n)
                    for k in range(4, KT):
                        ins = act.activation(mixT[:, k, :], M[:, 1, (k % 4) * P:(k % 4 + 1) * P], ACT.Copy,
                                             scale=g.cols[:, C_GN + k:C_GN + k + 1])
                    ins.then_inc(t1a, 1)
                for h in range(2, 5):
                    head(h)
                if project:
                    act.wait_ge(res, pj.n + 1)
                    wait(act, sqa, pj.n + 1)
                    act.activation(sqs[:, :], x2[pj.par][:, :], ACT.Square, accum_out=n2[:, 3:4]).then_inc(sq2, 1)
                for h in range(5, 7):
                    head(h)
                if project:
                    act.wait_ge(t2, pj.n + 1)
                    wait(act, rt, pj.n)
                    for k in range(4, KT):
                        ins = act.activation(h2T[:, k, :], M[:, 1, (k % 4) * P:(k % 4 + 1) * P], ACT.Identity,
                                             bias=g.mods[:, 0, 24 + k:25 + k], scale=g.scale2[:, k:k + 1])
                    ins.then_inc(t2a, 1)
                head(7)
                if scores:
                    act.wait_ge(esn, nx.n + 1)
                    act.activation(esk[:, nx.par, :], esk[:, nx.par, :], ACT.Exp).then_inc(eso, 1)
                if values:
                    act.wait_ge(att, t.n + 1)
                    act.wait_ge(ld_x[t.par], 32 * (t.half + 1))
                    if project:
                        act.wait_ge(sq2, pj.n + 1)
                    act.activation(sqs[:, 0:HW], mix[t.par][:, 0, :], ACT.Square, accum_out=ms[:, t.par, 0:1])
                    act.activation(sqs[:, HW:], mix[t.par][:, 1, :], ACT.Square, accum_out=ms[:, t.par, 1:2]).then_inc(sqa, 1)
            pipeline(act, step)

        @block.vector
        def _(ve):
            carry = g.carry
            ve.wait_ge(ld, 16 * len(tables))
            ve.memset(carry[:, :], 0.0).then_inc(setup, 1)
            ve.memset(ones[:, :], 1.0).then_inc(setup, 1)
            for b in range(2):
                ve.memset(qb[b][HD:HD + 1, :, :], 1.0).then_inc(setup, 1)
            ve.tensor_scalar(nsink[:, :], sink[:, :], -1.0, None, ALU.mult).then_inc(setup, 1)
            ve.wait_ge(setup, 6)

            def do(ins):
                ins.then_inc(dve, 1)
                ve.wait_ge(dve, 1)
                ve.sem_clear(dve)

            def rsqrt(y, c, v):
                do(ve.tensor_scalar(y.bitcast(I32), v.bitcast(I32), 1, None, ALU.arith_shift_right))
                do(ve.tensor_scalar(y.bitcast(I32), y.bitcast(I32), -1.0, float(0x5F3759DF), ALU.mult, ALU.add))
                for _ in range(3):
                    do(ve.tensor_tensor(c, y, y, ALU.mult))
                    do(ve.tensor_tensor(c, c, v, ALU.mult))
                    do(ve.tensor_scalar(c, c, -0.5, 1.5, ALU.mult, ALU.add))
                    do(ve.tensor_tensor(y, y, c, ALU.mult))

            def one_hot(out, x, m, n, col, b):
                do(ve.scalar_tensor_tensor(out=out, in0=x, scalar=m, in1=rank8[:, 0:n], op0=ALU.is_ge, op1=ALU.mult))
                do(ve.reduce_max(col, out, AX.X))
                do(ve.tensor_scalar(out, out, col, None, ALU.is_equal))

            def step(t, scores, values, project, place):
                nx, pj, pl = t.back(-1), t.back(1), t.back(2)

                def head(h):
                    if scores:
                        ve.wait_ge(qk, 8 * nx.n + h + 1)
                        wait(ve, tp, 8 * (nx.n - 2) + h + 1)
                        ve.sem_inc(passed, 1)
                        ve.tensor_tensor_reduce(out=pr[nx.par][:, h, :], in0=S[:, :, :].rearrange("p a b -> p (a b)")[:, 0:KEYS],
                                                in1=mask[:, :], scale=1.0, scalar=-3e38, op0=ALU.add, op1=ALU.max,
                                                accum_out=mx[:, nx.par, h:h + 1]).then_inc(sm, 1)
                        ve.wait_ge(sm, 8 * nx.n + h + 1)
                        ve.tensor_scalar(nm[:, nx.par, h:h + 1], mx[:, nx.par, h:h + 1], -SCALE, nsink[:, h:h + 1],
                                         ALU.mult, ALU.min).then_inc(nmx, 1)

                head(0)
                if place:
                    b = pl.par
                    ve.wait_ge(px, pl.n + 1)
                    do(ve.tensor_tensor(pos[:, 0, :], R[:, 64:64 + NE], carry[:, :], ALU.add))
                    ve.tensor_tensor(carry[:, :], R[:, 128:128 + NE], carry[:, :], ALU.add).then_inc(pxr, 1)
                    ve.wait_ge(pxr, pl.n + 1)
                    do(ve.tensor_tensor(pos[:, 0, :], pos[:, 0, :], slot0[:, :], ALU.add))
                    wait(ve, sc[b], 32 * pl.half)
                    for k in range(2):
                        do(ve.tensor_tensor(pos[:, 1, :], pos[:, 0, :], pick[:, b, k, :], ALU.mult))
                        do(ve.reduce_sum(r4[:, b, 6 + k:7 + k], pos[:, 1, :], AX.X))
                        do(ve.tensor_copy(idx[:, b, k:k + 1], r4[:, b, 6 + k:7 + k]))
                        do(ve.tensor_copy(rec[:, b, k, 0:1], token[:, bass.ds(pl.n, 1)]))
                    ve.wait_ge(gex, pl.n + 1)
                    do(ve.tensor_scalar(r4[:, b, 8:9], r4[:, b, 5:6], 1.0, None, ALU.add))
                    do(ve.tensor_tensor(r4[:, b, 8:9], r4[:, b, 8:9], r4[:, b, 4:5], ALU.mult))
                    do(ve.reciprocal(rec[:, b, 0, 1:2].bitcast(F32), r4[:, b, 8:9]))
                    ve.tensor_tensor(rec[:, b, 1, 1:2].bitcast(F32), rec[:, b, 0, 1:2].bitcast(F32), r4[:, b, 5:6],
                                     ALU.mult).then_inc(rec_ok, 1)
                head(1)
                if project:
                    ve.wait_ge(t1, pj.n + 1)
                    wait(ve, op, 2 * pj.n)
                    for k in range(4):
                        ins = ve.tensor_scalar(mixT[:, k, :], M[:, 0, k * P:(k + 1) * P],
                                               g.cols[:, C_GN + k:C_GN + k + 1], None, ALU.mult)
                    ins.then_inc(t1v, 1)
                for h in range(2, 4):
                    head(h)
                if project:
                    ve.wait_ge(ld_x[pj.par], 32 * (pj.half + 1))
                    wait(ve, st_x[pj.par], 32 * pj.half)
                    for half in range(2):
                        ve.wait_ge(op, 2 * pj.n + half + 1)
                        cs = slice(half * 512, (half + 1) * 512)
                        do(ve.tensor_tensor(x2[pj.par][:, cs], M[:, half, :], g1[:, cs], ALU.mult))
                    ve.tensor_tensor(x2[pj.par][:, :], x2[pj.par][:, :], xr[pj.par][:, :], ALU.add).then_inc(res, 1)
                head(4)
                if project:
                    ve.wait_ge(sq2, pj.n + 1)
                    do(ve.tensor_scalar(n2[:, 2:3], n2[:, 3:4], 1.0 / D, EPS, ALU.mult, ALU.add))
                    rsqrt(n2[:, 0:1], n2[:, 1:2], n2[:, 2:3])
                    ve.tensor_scalar(xn[pj.par][:, :], x2[pj.par][:, :], n2[:, 0:1], None, ALU.mult).then_inc(xnd, 1)
                for h in range(5, 7):
                    head(h)
                if project:
                    ve.wait_ge(t2, pj.n + 1)
                    wait(ve, rt, pj.n)
                    for k in range(4):
                        ins = ve.tensor_scalar(h2T[:, k, :], M[:, 0, k * P:(k + 1) * P], g.scale2[:, k:k + 1],
                                               g.mods[:, 0, 24 + k:25 + k], ALU.mult, ALU.add)
                    ins.then_inc(t2v, 1)
                head(7)
                if scores:
                    wait(ve, att, nx.n - 1)
                    ve.wait_ge(nmx, 8 * nx.n + 8)
                    ve.tensor_tensor(esk[:, nx.par, :], sink[:, :], nm[:, nx.par, :], ALU.add).then_inc(esn, 1)
                if values:
                    ve.wait_ge(eso, t.n + 1)
                    ve.wait_ge(pv, 8 * t.n + 8)
                    wait(ve, mxn, t.n - 1)
                    do(ve.tensor_tensor(rsum[:, t.par, :], rsum[:, t.par, :], esk[:, t.par, :], ALU.add))
                    do(ve.reciprocal(rsum[:, t.par, :], rsum[:, t.par, :]))
                    ve.tensor_tensor(mix[t.par][:, 0, :].rearrange("p (h d) -> p h d", h=NH), O[:, :, :],
                                     rsum[:, t.par, :].unsqueeze(2).broadcast_to([P, NH, HD]), ALU.mult).then_inc(att, 1)
                    ve.wait_ge(sqa, t.n + 1)
                    do(ve.tensor_scalar(nw[:, 2, :], ms[:, t.par, :], 1.0 / HW, EPS, ALU.mult, ALU.add))
                    rsqrt(nw[:, 0, :], nw[:, 1, :], nw[:, 2, :])
                    wait(ve, t1, t.n)
                    ve.tensor_scalar(mixn[:, 0, :], mix[t.par][:, 0, :], nw[:, 0, 0:1], None, ALU.mult)
                    ve.tensor_scalar(mixn[:, 1, :], mix[t.par][:, 1, :], nw[:, 0, 1:2], None, ALU.mult).then_inc(mxn, 1)
                if project:
                    b = pj.par
                    ve.wait_ge(rt, pj.n + 1)
                    if not (isinstance(pj.n, int) and pj.n < 2):
                        ve.wait_ge(rec_ok, pj.n - 1)
                        ve.wait_ge(px, pj.n - 1)
                    ve.tensor_tensor(lg[:, b, :], R[:, 0:NG + NE], rb[:, :], ALU.add).then_inc(lgd, 1)
                    ve.wait_ge(lgd, pj.n + 1)
                    c = r4[:, b, :]
                    do(ve.reduce_max(c[:, 1:2], lg[:, b, 0:NG], AX.X))
                    do(ve.tensor_scalar(c[:, 0:1], c[:, 1:2], -1.0, None, ALU.mult))
                    one_hot(oh[:, 0, 0:NG], lg[:, b, 0:NG], c[:, 1:2], NG, c[:, 9:10], b)
                    do(ve.tensor_tensor(selg[:, :, :], lg[:, b, NG:].rearrange("p (a c) -> p a c", a=NG),
                                        oh[:, 0, 0:NG].unsqueeze(2).broadcast_to([P, NG, EPG]), ALU.mult))
                    do(ve.reduce_sum(oh[:, 3, :], selg[:, :, :].rearrange("p a c -> p c a"), AX.X))
                    do(ve.reduce_max(c[:, 1:2], oh[:, 3, :], AX.X))
                    one_hot(oh[:, 1, :], oh[:, 3, :], c[:, 1:2], EPG, c[:, 9:10], b)
                    do(ve.scalar_tensor_tensor(out=oh[:, 3, :], in0=oh[:, 1, :], scalar=-3e38, in1=oh[:, 3, :],
                                               op0=ALU.mult, op1=ALU.add))
                    do(ve.reduce_max(c[:, 2:3], oh[:, 3, :], AX.X))
                    one_hot(oh[:, 2, :], oh[:, 3, :], c[:, 2:3], EPG, c[:, 9:10], b)
                    do(ve.tensor_tensor(c[:, 3:4], c[:, 2:3], c[:, 1:2], ALU.subtract))
                    for k in range(2):
                        do(ve.tensor_tensor(pick[:, b, k, :].rearrange("p (a c) -> p a c", a=NG),
                                            oh[:, 0, 0:NG].unsqueeze(2).broadcast_to([P, NG, EPG]),
                                            oh[:, 1 + k, :].unsqueeze(1).broadcast_to([P, NG, EPG]), ALU.mult))
                    ve.tensor_tensor(pick[:, b, 2, :], pick[:, b, 0, :], pick[:, b, 1, :], ALU.add).then_inc(rt1, 1)
            pipeline(ve, step)


def stage6(e, g):
    nc, i = e.nc, e.i
    FT = FH // P
    with e.stage() as st:
        w13 = [e.sb(st, f"w13_{b}", [P, 2, KT, FH]) for b in range(2)]
        w2 = [e.sb(st, f"w2_{b}", [P, FT, D]) for b in range(2)]
        g2 = e.sb(st, "g2row", [P, D])
        info = e.sb(st, "info", [P, 3, NE], I32)
        inf = e.sb(st, "inf", [P, 2, NE])
        rec = e.sb(st, "brec", [P, 2 * NE + T // P + 2, 2], I32)
        rows_in = e.sb(st, "rows_in", [P, 1], I32)
        rows_out = e.sb(st, "rows_out", [P, 1], I32)
        xg = e.sb(st, "xg", [P, D])
        xT = e.sb(st, "bxT", [P, KT, P])
        sg = e.sb(st, "sg", [P, 2, P])
        gT = e.sb(st, "gT", [P, FT, P])
        y = e.sb(st, "by", [P, D])
        tpp = e.ps(st, "btp", [P, 2, 4, P])
        hp = e.ps(st, "bh", [P, 2, 512])
        yp = e.ps(st, "byp", [P, 2, 512])
        cnt = e.sem("s6_counts_ready")
        ld = e.sem("s6_gate_row_loaded")
        ldw13 = [e.sem(f"s6_w13_loaded{b}") for b in range(2)]
        ldw2 = [e.sem(f"s6_w2_loaded{b}") for b in range(2)]
        rl = e.sem("s6_records_loaded")
        gat = e.sem("s6_rows_gathered")
        scat = e.sem("s6_rows_added")
        tt = e.sem("s6_rows_turned")
        gd = e.sem("s6_hidden_gated")
        ym = e.sem("s6_output_product")
        y_ok = e.sem("s6_output_ready")
        xc_v = e.sem("s6_turned_copied_v")
        xc_a = e.sem("s6_turned_copied_a")
        hm = e.sem("s6_hidden_product")
        sgd = e.sem("s6_silu")
        picked_in = e.sem("s6_rows_in_picked")
        picked_out = e.sem("s6_rows_out_picked")
        clean = e.sem("s6_buffers_cleared")
        blank = e.sem("s6_records_cleared")
        passed_a = e.sem("s6_waits_passed_by_scalar")
        passed = e.sem("s6_waits_passed")
        passed_t = e.sem("s6_waits_passed_by_tensor")
        cnt0 = e.sem("s6_counts_step")
        ahead = ((tt, 1), (gd, 2), (ym, 1))
        out_rows, xn_rows = e.out[0], g.xn_dram
        block = st.enter_context(nc.Block())

        def span(eng, ex):
            many = eng.value_load(info[0:1, 0, bass.ds(ex, 1)], min_val=1, max_val=T // P)
            base = eng.value_load(info[0:1, 1, bass.ds(ex, 1)], min_val=0, max_val=2 * NE)
            return many, base

        def blocks(eng, body, before=None, first=None):
            eng.wait_ge(cnt, 1)
            with eng.Fori(0, NE // 2) as pair:
                for par in range(2):
                    ex = 2 * pair + par
                    many, base = span(eng, ex)
                    if before is not None:
                        before(pair, par)
                    with eng.Fori(0, many) as b:
                        body(base + b, ex, b, par)

        @block.vector
        def _(ve):
            ve.memset(rec[:, :, :], NOWHERE).then_inc(blank, 1)
            ve.memset(xg[:, :], 0.0).then_inc(clean, 1)

            def do(ins):
                ins.then_inc(cnt0, 1)
                ve.wait_ge(cnt0, 1)
                ve.sem_clear(cnt0)
            do(ve.tensor_copy(info[:, 0, :], g.carry[:, :]))
            do(ve.tensor_scalar(info[:, 0, :], info[:, 0, :], P - 1, None, ALU.add))
            do(ve.tensor_scalar(info[:, 0, :], info[:, 0, :], P.bit_length() - 1, None, ALU.arith_shift_right))
            do(ve.tensor_scalar(info[:, 0, :], info[:, 0, :], 1, None, ALU.max))
            do(ve.tensor_copy(inf[:, 0, :], info[:, 0, :]))
            do(ve.memset(inf[:, 1, :], 0.0))
            do(ve.tensor_tensor_scan(inf[:, 1, :], inf[:, 0, :], inf[:, 1, :], 0.0, ALU.add, ALU.add))
            do(ve.tensor_copy(info[:, 2, :], inf[:, 1, :]))
            do(ve.tensor_tensor(inf[:, 1, :], inf[:, 1, :], inf[:, 0, :], ALU.subtract))
            ve.tensor_copy(info[:, 1, :], inf[:, 1, :]).then_inc(cnt, 1)
            ve.memset(y[:, :], 0.0).then_inc(y_ok, 1)
            for s, k in ahead:
                ve.sem_inc(s, k)
            ve.wait_ge(ld, 16)

            def turned(n):
                ve.wait_ge(tt, n + 2)
                for k in range(4):
                    ins = ve.tensor_scalar(xT[:, k, :], tpp[:, 0, k, :], g.scale2[:, k:k + 1],
                                           g.mods[:, 0, 24 + k:25 + k], ALU.mult, ALU.add)
                ins.then_inc(xc_v, 1)

            def body(n, ex, b, par):
                ve.wait_ge(ym, 2 * n + 1)
                for f in range(FT):
                    ve.wait_ge(sgd, 4 * n + f + 1)
                    ve.tensor_tensor(gT[:, f, :], sg[:, f % 2, :], hp[:, f % 2, P:2 * P], ALU.mult).then_inc(gd, 1)
                turned(n + 1)
                ve.wait_ge(scat, 16 * (n + 1))
                for half in range(2):
                    cs = slice(half * 512, (half + 1) * 512)
                    ve.wait_ge(ym, 2 * n + half + 2)
                    ins = ve.scalar_tensor_tensor(out=y[:, cs], in0=yp[:, half, :], scalar=rec[:, bass.ds(n + 1, 1), 1:2].rearrange("p a b -> p (a b)").bitcast(F32),
                                                  in1=g2[:, cs], op0=ALU.mult, op1=ALU.mult)
                ins.then_inc(y_ok, 1)
            turned(0)
            blocks(ve, body)

        @block.scalar
        def _(act):
            def turned(n):
                act.wait_ge(tt, n + 2)
                for k in range(4):
                    ins = act.activation(xT[:, 4 + k, :], tpp[:, 1, k, :], ACT.Identity,
                                         bias=g.mods[:, 0, 28 + k:29 + k], scale=g.scale2[:, 4 + k:5 + k])
                ins.then_inc(xc_a, 1)

            def body(n, ex, b, par):
                for f in range(FT):
                    act.wait_ge(hm, 4 * n + f + 1)
                    act.wait_ge(gd, 4 * n + f + 1)
                    act.activation(sg[:, f % 2, :], hp[:, f % 2, 0:P], ACT.Silu).then_inc(sgd, 1)
                turned(n + 1)

            def load(ex, par):
                for m, name in enumerate(("exp_w1", "exp_w3")):
                    act.dma_start(w13[par][:, m, :, :], i[name][0, bass.ds(ex, 1)].rearrange("a (k p) f -> p (a k) f", p=P))\
                       .then_inc(ldw13[par], 16)
                act.dma_start(w2[par][:, :, :], i["exp_w2"][0, bass.ds(ex, 1)].rearrange("a (k p) f -> p (a k) f", p=P))\
                   .then_inc(ldw2[par], 16)

            def expert(ex, par, more):
                many, base = span(act, ex)
                if more:
                    act.wait_ge(ym, 2 * base + 1)
                    act.sem_inc(passed_a, 1)
                    load(ex + 1, 1 - par)
                with act.Fori(0, many) as b:
                    body(base + b, ex, b, par)
            load(0, 0)
            load(1, 1)
            turned(0)
            act.wait_ge(cnt, 1)
            expert(0, 0, False)
            with act.Fori(0, NE // 2 - 1) as pair:
                expert(2 * pair + 1, 1, True)
                expert(2 * pair + 2, 0, True)
            expert(NE - 1, 1, False)

        @block.gpsimd
        def _(pool):
            pool.wait_ge(clean, 1)

            def gather(n):
                pool.wait_ge(rl, 16 * (n + 1))
                pool.wait_ge(tt, n + 1)
                pool.sem_inc(passed, 1)
                pool.tensor_copy(rows_in[:, :], rec[:, bass.ds(n + 1, 1), 0:1].rearrange("p a b -> p (a b)")).then_inc(picked_in, 1)
                pool.wait_ge(picked_in, n + 1)
                pool.sem_inc(passed, 1)
                pool.indirect_dma_start(xg[:, :], None, xn_rows, bass.IndirectOffsetOnAxis(ap=rows_in[:, :], axis=0),
                                        bounds_check=T - 1, oob_is_err=False).then_inc(gat, 16)

            def scatter(n):
                pool.wait_ge(y_ok, n + 1)
                pool.wait_ge(scat, 16 * n)
                pool.sem_inc(passed, 1)
                pool.tensor_copy(rows_out[:, :], rec[:, bass.ds(n, 1), 0:1].rearrange("p a b -> p (a b)")).then_inc(picked_out, 1)
                pool.wait_ge(picked_out, n + 1)
                pool.sem_inc(passed, 1)
                pool.indirect_dma_start(out_rows, bass.IndirectOffsetOnAxis(ap=rows_out[:, :], axis=0), y[:, :], None,
                                        bounds_check=T - 1, oob_is_err=False, compute_op=ALU.add).then_inc(scat, 16)

            gather(0)
            pool.wait_ge(cnt, 1)
            total = pool.value_load(info[0:1, 2, NE - 1:NE], min_val=1, max_val=2 * NE)
            with pool.Fori(0, total) as n:
                gather(n + 1)
                scatter(n)
            scatter(total)
            pool.wait_ge(scat, 16 * (total + 1))
            pool.wait_ge(gat, 16 * (total + 1))
            pool.sem_inc(passed, 1)

        @block.sync
        def _(sp):
            sp.dma_start(g2[:, :], g.gate_dram[D:2 * D].partition_broadcast(P)).then_inc(ld, 16)
            sp.wait_ge(blank, 1)

            def body(n, ex, b, par):
                sp.wait_ge(rl, 16 * n)
                sp.dma_start(rec[:, bass.ds(n + 1, 1), :], g.table[bass.ds(ex * CAP + b * P, P), :].unsqueeze(1)).then_inc(rl, 16)
            blocks(sp, body)
            total = sp.value_load(info[0:1, 2, NE - 1:NE], min_val=1, max_val=2 * NE)
            body(total, NE, 0, 0)

        @block.tensor
        def _(pe):
            def turn(n):
                pe.wait_ge(gat, 16 * (n + 1))
                for k in range(KT):
                    ins = pe.transpose(tpp[:, k // 4, k % 4, :], xg[:, k * P:(k + 1) * P], g.ident[:, :])
                ins.then_inc(tt, 1)

            def weights(pair, par):
                pe.wait_ge(ldw13[par], 32 * (pair + 1))
                pe.wait_ge(ldw2[par], 16 * (pair + 1))
                pe.sem_inc(passed_t, 1)

            def body(n, ex, b, par):
                pe.wait_ge(xc_v, n + 1)
                pe.wait_ge(xc_a, n + 1)
                for f in range(FT):
                    pe.wait_ge(gd, 4 * n + f + 1)
                    for m in range(2):
                        for k in range(KT):
                            ins = pe.matmul(hp[:, f % 2, m * P:(m + 1) * P], w13[par][:, m, k, f * P:(f + 1) * P],
                                            xT[:, k, :], start=(k == 0), stop=(k == KT - 1))
                    ins.then_inc(hm, 1)
                turn(n + 1)
                pe.wait_ge(gd, 4 * n + 6)
                pe.wait_ge(y_ok, n + 1)
                for half in range(2):
                    for f in range(FT):
                        ins = pe.matmul(yp[:, half, :], gT[:, f, :], w2[par][:, f, half * 512:(half + 1) * 512],
                                        start=(f == 0), stop=(f == FT - 1))
                    ins.then_inc(ym, 1)
            turn(0)
            blocks(pe, body, before=weights)


class Shared:
    pass


def program(nc, inputs, out, debug=False, stages=(1, 2, 3, 4, 5, 6)):
    with ExitStack() as stack:
        e = Env(nc, stack, inputs, debug)
        e.out = out
        g = Shared()
        g.cols = e.sb(stack, "cols", [P, P])
        g.mods = e.sb(stack, "mods", [P, 2, 48])
        g.scale1 = e.sb(stack, "scale1", [P, 2, KT])
        g.scale2 = e.sb(stack, "scale2", [P, KT])
        g.ident = e.sb(stack, "ident", [P, P])
        g.filt_dram = e.dram("filt", [2, NL, Q, 2, P, LANE])
        g.gate_dram = e.dram("gate", [2 * D])
        g.hy_dram = e.dram("hy_in", [3, T, HW])
        if 1 in stages:
            stage1(e, g)
        g.q_dram = e.dram("q", [NT + 1, HD, NH, P])
        g.kT = e.sb(stack, "kT", [HD + 1, NKV, C + T + 2 * P])
        g.v = e.sb(stack, "v", [P, NT + 4, NKV * HD])
        with ExitStack() as mid:
            g.hT = e.sb(mid, "hT", [P, KT, T])
            g.hcT = e.sb(mid, "hcT", [P, KT, C])
            if 2 in stages:
                stage2(e, g)
            if 3 in stages:
                stage3(e, g)
            if debug and max(stages)<=3:
                e.dump(g)
        g.hyo_dram = e.dram("hy_out", [T, HW])
        if 4 in stages:
            stage4(e, g)
        g.xn_dram = e.dram("xn", [T, D])
        g.table = e.dram("table", [NE * CAP + P, 2], I32)
        g.carry = e.sb(stack, "carry", [P, NE])
        if 5 in stages:
            stage5(e, g)
        if 6 in stages:
            stage6(e, g)
        if debug and max(stages) >= 4:
            e.dump(g)


INPUTS = ["x", "c", "ctx", "c_ctx", "ada_w", "ada_b", "norm1_w", "w_in", "q_norm_w", "k_norm_w", "attn_sink",
          "hy_conv_w", "hy_conv_b", "hy_w1", "hy_b1", "hy_w2", "hy_b2", "hy_w3", "hy_sin_freq", "hy_skip",
          "group_norm_w", "w_out", "norm2_w", "router_g_w", "router_g_b", "router_e_w", "router_e_b",
          "exp_w1", "exp_w3", "exp_w2"]


def kernel(**inputs):
    import concourse.bacc as bacc
    from concourse.bass_utils import run_bass_kernel_spmd

    nc = bacc.Bacc("TRN2", target_bir_lowering=False, num_devices=1)
    arrays, aps = {}, {}
    for name, a in [(n, inputs[n]) for n in INPUTS] + list(constants().items()):
        a = np.ascontiguousarray(a)
        arrays[f"in_{name}"] = a
        aps[name] = nc.dram_tensor(f"in_{name}", a.shape, mybir.dt.from_np(a.dtype), kind="ExternalInput").ap()
    out = nc.dram_tensor("out_0", (1, T, D), F32, kind="ExternalOutput").ap()
    program(nc, aps, out)
    r = run_bass_kernel_spmd(nc, [arrays], core_ids=[0])
    return r.results[0]["out_0"]
```

```python
from contextlib import ExitStack, contextmanager

import numpy as np

import concourse.bass as bass
from concourse import mybir

F32 = mybir.dt.float32
I32 = mybir.dt.int32
U32 = mybir.dt.uint32
ALU = mybir.AluOpType
ACT = mybir.ActivationFunctionType
AX = mybir.AxisListType

P = 128
D = 1024
T = 2048
C = 256
KT = D // P
NT = T // P
HD = 64
NH, NKV = 8, 2
AW = 512
HW = 512
Q = 16
NE = 32
NG, EPG = 4, 8
FH = 512
EPS = 1e-6
SCALE = HD ** -0.5
NEG = -1e30
LANE = 128
NL = HW // LANE
NOWHERE = 4095
CAP = T

C_ADAB, C_N1, C_N2, C_GN, C_CW, C_CB, C_QN, C_KN, C_B1, C_B2, C_SF = 0, 48, 56, 64, 72, 108, 120, 121, 122, 123, 124


def constants():
    k = {}
    p = np.arange(P)[:, None, None]
    q = np.arange(Q)[None, :, None]
    k2 = np.arange(P)[None, None, :]
    th = 2 * np.pi * (((16 * p + q) * k2) % 4096) / 4096
    fre, fim = np.cos(th), -np.sin(th)
    fim[:, :, 0] = np.where(np.arange(P) % 2, -1.0, 1.0)[:, None]
    k["dft_fwd"] = np.concatenate([fre, fim], axis=2).reshape(P, Q * 256)
    ire = 2 / 4096 * np.cos(th).transpose(2, 1, 0)
    iim = -2 / 4096 * np.sin(th).transpose(2, 1, 0)
    ire[0] = 1 / 4096
    iim[0] = np.where(np.arange(P) % 2, -1.0, 1.0)[None, :] / 4096
    k["dft_inv"] = np.stack([ire, iim], axis=2).reshape(P, Q * 256)
    w = np.exp(-2j * np.pi * np.outer(np.arange(16), np.arange(16)) / 16)
    x = np.zeros((4, 16, 2, 4, 16, 2))
    for s in range(4):
        x[s, :, 0, s, :, 0] = w.real
        x[s, :, 0, s, :, 1] = w.imag
        x[s, :, 1, s, :, 0] = -w.imag
        x[s, :, 1, s, :, 1] = w.real
    xs = x.copy()
    xs[0, :, :, 0] = 0
    qq = np.arange(16)
    xs[0, :, 0, 0, 0, 0] = 1
    xs[0, :, 0, 0, 0, 1] = (-1.0) ** qq
    for k1 in range(1, 8):
        xs[0, :, 0, 0, k1, 0] = w[:, k1].real
        xs[0, :, 0, 0, k1, 1] = w[:, k1].imag
    for k1 in range(8):
        v = np.exp(-2j * np.pi * qq * (k1 + 0.5) / 16)
        xs[0, :, 1, 0, 8 + k1, 0] = v.real
        xs[0, :, 1, 0, 8 + k1, 1] = v.imag

    def spectra(m, special):
        h1, h2 = m.copy(), m.copy()
        h1[..., 1] = m[..., 0]
        h2[..., 0] = m[..., 1]
        h2[..., 1] = -m[..., 1]
        if special:
            h1[:, :, :, 0, 0, 1] = m[:, :, :, 0, 0, 1]
            h2[:, :, :, 0, 0, :] = 0
        return h1, h2

    inv = np.zeros((4, 16, 2, 4, 16, 2))
    wi = np.conj(w).T
    for s in range(4):
        inv[s, :, 0, s, :, 0] = wi.real
        inv[s, :, 0, s, :, 1] = wi.imag
        inv[s, :, 1, s, :, 0] = -wi.imag
        inv[s, :, 1, s, :, 1] = wi.real
    invs = inv.copy()
    invs[0, :, :, 0] = 0
    invs[0, 0, 0, 0, :, 0] = 1
    invs[0, 0, 1, 0, :, 0] = (-1.0) ** qq
    for k1 in range(1, 8):
        invs[0, k1, 0, 0, :, 0] = 2 * wi[k1].real
        invs[0, k1, 1, 0, :, 0] = -2 * wi[k1].imag
    for k1 in range(8):
        v = np.exp(2j * np.pi * qq * (k1 + 0.5) / 16)
        invs[0, 8 + k1, 0, 0, :, 1] = 2 * v.real
        invs[0, 8 + k1, 1, 0, :, 1] = -2 * v.imag
    mats = []
    for m, n, special in ((x, inv, False), (xs, invs, True)):
        h1, h2 = spectra(m, special)
        mats += [m, h1, h2, n, n[:, :, ::-1]]
    k["dft_mid"] = np.stack([m.reshape(P, P) for m in mats], axis=1).reshape(P, 10 * P)
    tf = (16 * np.arange(P)[None, :] + np.arange(Q)[:, None]).reshape(-1)
    pos = np.concatenate([tf, T - tf]).astype(np.float64)
    bands = np.linspace(1e-4, 15, 16).astype(np.float32).astype(np.float64)
    ang = 2 * np.pi / T * pos[None, :] * bands[:, None]
    k["feat"] = np.concatenate([pos[None] / T, np.cos(ang), -np.sin(ang)], axis=0)
    k["tneg"] = -(np.stack([tf.reshape(Q, P).T, (T - tf).reshape(Q, P).T], axis=1) / T).reshape(P, 2 * Q)
    deltas = np.abs(np.linspace(np.log(1e-2) / 1.5, np.log(1e-2) / 0.3, HW))
    k["deltas"] = np.broadcast_to(deltas[None], (P, HW))
    tok = np.arange(T)
    inv_freq = 10000.0 ** (-np.arange(16) / 16)
    a = np.concatenate([np.outer(inv_freq, tok // 64), np.outer(inv_freq, tok // 64),
                        np.outer(inv_freq, tok % 64), np.outer(inv_freq, tok % 64)])
    sign = np.where(np.arange(64) % 32 < 16, -1.0, 1.0)[:, None]
    k["rope_cos"] = np.concatenate([np.cos(a)] * 2)
    k["rope_sin"] = np.concatenate([np.sin(a) * sign] * 2)
    c = np.arange(P)
    k["head_ones"] = (c[:, None] // 64 == c[None, :] // 64) * 1.0
    k["pair_swap"] = (c[:, None] == (c[None, :] ^ 16)) * 1.0
    k["ident"] = np.eye(P)
    k["upper"] = (c[:, None] < c[None, :]) * 1.0
    qi, kj = np.arange(P)[:, None], np.arange(3 * P)[None, :] - P
    band = np.where(np.abs(kj - qi) <= P, 0.0, NEG)
    k["mask"] = np.concatenate([np.zeros((P, C)), band], axis=1)
    kb = np.zeros((1, NKV, C + T + 2 * P))
    kb[:, :, C:C + P] = NEG
    kb[:, :, C + P + T:] = NEG
    k["key_bias"] = kb.reshape(1, -1)
    k["rank8"] = np.broadcast_to(8.0 - np.arange(8)[None], (P, 8))
    k["slot0"] = np.broadcast_to(float(CAP) * np.arange(NE)[None], (P, NE))
    out = {n: np.ascontiguousarray(v, dtype=np.float32) for n, v in k.items()}
    out["token"] = (np.arange(P)[:, None] + P * np.arange(NT)[None]).astype(np.int32)
    return out


class Env:

    def __init__(self, nc, stack, inputs, debug=False):
        self.nc, self.stack, self.i, self.debug = nc, stack, inputs, debug
        self.sems = {}

    def sem(self, name):
        assert name not in self.sems
        self.sems[name] = self.nc.alloc_semaphore(name=name)
        return self.sems[name]

    def stage(self):
        @contextmanager
        def scope():
            with ExitStack() as st:
                yield st
            self.nc.clear_and_free_semaphores(list(self.sems.values()))
            self.nc.all_engine_barrier()
            self.sems = {}
        return scope()

    def sb(self, stack, name, shape, dt=F32):
        return stack.enter_context(self.nc.sbuf_tensor("sb_" + name, shape, dt))

    def ps(self, stack, name, shape, dt=F32):
        return stack.enter_context(self.nc.psum_tensor("ps_" + name, shape, dt))

    def dram(self, name, shape, dt=F32):
        kw = {"kind": "ExternalOutput"} if self.debug else {}
        return self.nc.dram_tensor("scr_" + name, shape, dt, **kw).ap()


class Chain:

    def __init__(self, eng, sem):
        self.eng, self.sem, self.n = eng, sem, 0

    def __call__(self, ins):
        ins.then_inc(self.sem, 1)
        self.n += 1
        return self.n

    def wait(self, n=None):
        self.eng.wait_ge(self.sem, self.n if n is None else n)


def stage1(e, g):
    nc = e.nc
    steps = [(o, q) for o in range(2) for q in range(Q)]
    TWO_PI_HI = float(np.float32(6.28125))
    TWO_PI_LO = float(np.float32(2 * np.pi - 6.28125))
    ROUND = 12582912.0
    with e.stage() as st:
        rows = e.sb(st, "rows", [P, P])
        crow = e.sb(st, "crow", [16, P])
        sil = e.sb(st, "sil", [P, KT, 32])
        mrow = e.sb(st, "mrow", [P, 3, 512])
        csb = e.sb(st, "csb", [P, 16])
        ada = e.sb(st, "ada", [P, 2, 3 * D])
        feat = e.sb(st, "feat", [33, 2 * T])
        w1 = e.sb(st, "fw1", [33, 64])
        w2 = e.sb(st, "fw2", [64, 64])
        w3 = e.sb(st, "fw3", [64, 4 * HW])
        hid = e.sb(st, "hid", [64, 2, 2 * T])
        ang = e.sb(st, "ang", [64, 4, 512])
        fwd = e.sb(st, "fwd1", [P, Q, 2, P])
        dl = e.sb(st, "dl", [P, HW])
        tneg = e.sb(st, "tneg", [P, 2, Q])
        dec = e.sb(st, "dec", [P, 2, Q, HW])
        fb = e.sb(st, "fb", [P, 2, HW])
        eo = e.sb(st, "eo", [P, 3, 2, HW])
        out = e.sb(st, "fout", [P, 4, HW])
        gr = e.sb(st, "gr", [16, P])
        gcol = e.sb(st, "gcol", [P, 16])
        gen = e.ps(st, "gen", [P, 4, 512])
        spec = e.ps(st, "spec", [P, 2, 512])
        modp = e.ps(st, "modp", [P, 512])
        misc = e.ps(st, "misc", [P, 512])

        ld_small = e.sem("s1_small_loaded")
        ld_dec = e.sem("s1_decay_loaded")
        ld_feat = e.sem("s1_feat_loaded")
        ld_filt = e.sem("s1_filter_tables_loaded")
        ld_ada = [e.sem(f"s1_ada_loaded{i}") for i in range(2)]
        rows_zero = e.sem("s1_rows_zeroed")
        turned = e.sem("s1_params_turned")
        cols_ok = e.sem("s1_cols_copied")
        sil_ok = e.sem("s1_silu_done")
        mlp_mm = e.sem("s1_mlp_product")
        mlp_arg = e.sem("s1_mlp_argument")
        mlp_sin = e.sem("s1_mlp_sine")
        dec_ok = e.sem("s1_decay_done")
        gen_mm = e.sem("s1_filter_generated")
        eo_ok = e.sem("s1_sum_difference")
        spec_mm = e.sem("s1_spectrum_product")
        spec_cp = e.sem("s1_spectrum_copied")
        stored = [e.sem(f"s1_spectrum_stored{i}") for i in range(4)]
        ada_mm = e.sem("s1_ada_product")
        mod_cp = e.sem("s1_modulation_copied")
        mod_t = e.sem("s1_modulation_turned")
        mod_rd = e.sem("s1_modulation_read")
        sil_z = e.sem("s1_silu_zeroed")
        dve = e.sem("s1_dve")
        g_cols = e.sem("s1_gate_cols")
        g_turn = e.sem("s1_gate_turned")
        g_copy = e.sem("s1_gate_copied")
        g_out = e.sem("s1_gate_stored")
        i = e.i
        small = [
            (rows[C_ADAB:C_ADAB + 48, :], i["ada_b"].rearrange("a (r p) -> (a r) p", p=P)),
            (rows[C_N1:C_N1 + 8, :], i["norm1_w"].rearrange("a (r p) -> (a r) p", p=P)),
            (rows[C_N2:C_N2 + 8, :], i["norm2_w"].rearrange("a (r p) -> (a r) p", p=P)),
            (rows[C_GN:C_GN + 8, :], i["group_norm_w"].rearrange("a (r p) -> (a r) p", p=P)),
            (rows[C_CW:C_CW + 36, :], i["hy_conv_w"].rearrange("a j (r p) -> (a j r) p", p=P)),
            (rows[C_CB:C_CB + 12, :], i["hy_conv_b"].rearrange("a (r p) -> (a r) p", p=P)),
            (rows[C_QN:C_QN + 1, 0:HD], i["q_norm_w"]), (rows[C_QN:C_QN + 1, HD:], i["q_norm_w"]),
            (rows[C_KN:C_KN + 1, 0:HD], i["k_norm_w"]), (rows[C_KN:C_KN + 1, HD:], i["k_norm_w"]),
            (rows[C_B1:C_B1 + 1, 0:64], i["hy_b1"]), (rows[C_B2:C_B2 + 1, 0:64], i["hy_b2"]),
            (rows[C_SF:C_SF + 2, 0:64], i["hy_sin_freq"].rearrange("a b c -> (a b) c")),
            (crow[0:8, :], i["c"].rearrange("a (r p) -> (a r) p", p=P)),
            (crow[8:16, :], i["c_ctx"].rearrange("(r p) -> r p", p=P)),
            (g.ident[:, :], i["ident"]),
        ]
        early = [
            (w1[:, :], i["hy_w1"][0]), (w2[:, :], i["hy_w2"][0]), (feat[:, :], i["feat"]),
        ]
        decay = [(dl[:, :], i["deltas"]), (tneg[:, :, :], i["tneg"].rearrange("p (d q) -> p d q", d=2))]
        tables = [
            (w3[:, :], i["hy_w3"][0]), (fwd[:, :, :, :], i["dft_fwd"].rearrange("p (q r k) -> p q r k", q=Q, r=2)),
        ]
        block = st.enter_context(nc.Block())

        @block.sync
        def _(sp):
            for dst, src in decay:
                sp.dma_start(dst, src).then_inc(ld_dec, 16)
            sp.wait_ge(rows_zero, 1)
            for dst, src in small:
                sp.dma_start(dst, src).then_inc(ld_small, 16)
            for dst, src in early:
                sp.dma_start(dst, src).then_inc(ld_feat, 16)
            for dst, src in tables:
                sp.dma_start(dst, src).then_inc(ld_filt, 16)
            for u in range(2 * KT):
                k, half = u // 2, u % 2
                if u >= 2:
                    sp.wait_ge(ada_mm, u - 1)
                sp.dma_start(ada[:, half, :], i["ada_w"][0, k * P:(k + 1) * P, half * 3 * D:(half + 1) * 3 * D])\
                    .then_inc(ld_ada[half], 16)

        @block.tensor
        def _(pe):
            pe.wait_ge(ld_small, 16 * len(small))
            pe.transpose(misc[:, 0:P], rows[:, :], g.ident[:, :]).then_inc(turned, 1)
            pe.transpose(misc[:, P:P + 16], crow[:, :], g.ident[0:16, 0:16]).then_inc(turned, 1)
            pe.wait_ge(ld_feat, 16 * len(early))
            def bank(b):
                return spec[:, b, :] if b < 2 else modp[:, :]

            def modulation(u):
                k, half = u // 2, u % 2
                if u == 0:
                    pe.wait_ge(sil_ok, 1)
                pe.wait_ge(ld_ada[half], 16 * (k + 1))
                for c in range(6):
                    at = 6 * half + c
                    mm = pe.matmul(bank(at // 4)[32 * (at % 4):32 * (at % 4) + 32, :], sil[:, k, :],
                                   ada[:, half, c * 512:(c + 1) * 512], start=(k == 0), stop=(k == KT - 1),
                                   skip_group_check=True)
                mm.then_inc(ada_mm, 1)

            for layer in range(2):
                for n in range(8):
                    at = 8 * layer + n
                    if at >= 4:
                        pe.wait_ge(mlp_arg, at - 3)
                    if layer == 1:
                        pe.wait_ge(mlp_sin, n + 1)
                    w, x = (w1[:, :], feat[:, n * 512:(n + 1) * 512]) if layer == 0 else \
                        (w2[:, :], hid[:, 0, n * 512:(n + 1) * 512])
                    pe.matmul(gen[0:64, at % 4, :], w, x, start=True, stop=True).then_inc(mlp_mm, 1)
                    if at % 2 == 1:
                        modulation(at - 1)
                        modulation(at)
            pe.wait_ge(mlp_sin, 16)

            def spectra(n):
                q = steps[n][1]
                pe.wait_ge(eo_ok, n + 1)
                for par in range(2):
                    if n >= 1:
                        pe.wait_ge(spec_cp, 2 * n + par - 1)
                    m = fwd[:, q, :, par::2]
                    pe.matmul(spec[:, par, :], m, eo[:, n % 3, par, :], start=True, stop=True).then_inc(spec_mm, 1)

            for n, (o, q) in enumerate(steps):
                if n >= 2:
                    pe.wait_ge(eo_ok, n - 1)
                elif n == 0:
                    pe.wait_ge(mlp_arg, 16)
                    pe.wait_ge(ld_filt, 16 * len(tables))
                for d in range(2):
                    pe.matmul(gen[:, 2 * (n % 2) + d, :], hid[:, 1, d * T + q * P:d * T + (q + 1) * P],
                              w3[:, (2 * o + d) * HW:(2 * o + d + 1) * HW], start=True, stop=True).then_inc(gen_mm, 1)
                if n == 2:
                    pe.wait_ge(mod_cp, 3)
                if n >= 2:
                    spectra(n - 2)
                if 3 <= n < 6:
                    pe.wait_ge(cols_ok, 2)
                    if n > 3:
                        pe.wait_ge(mod_rd, 2 * (n - 3))
                    for c in range(4):
                        mt = pe.transpose(misc[:, c * P:(c + 1) * P], mrow[:, n - 3, c * P:(c + 1) * P], g.ident[:, :])
                    mt.then_inc(mod_t, 1)
            spectra(len(steps) - 2)
            spectra(len(steps) - 1)
            pe.wait_ge(g_cols, 1)
            pe.transpose(misc[0:16, 256:256 + P], gcol[:, :], g.ident[:, :]).then_inc(g_turn, 1)

        @block.scalar
        def _(act):
            act.wait_ge(turned, 2)
            act.wait_ge(cols_ok, 2)
            act.wait_ge(sil_z, 1)
            act.activation(sil[:, :, 0:2].rearrange("p k a -> p a k"), csb[:, :].rearrange("p (a k) -> p a k", a=2),
                           ACT.Silu).then_inc(sil_ok, 1)
            act.wait_ge(ld_dec, 16 * len(decay))
            for d in range(2):
                for q in range(Q):
                    act.activation(dec[:, d, q, :], dl[:, :], ACT.Exp, scale=tneg[:, d, q:q + 1]).then_inc(dec_ok, 1)
            for n in range(16):
                act.wait_ge(mlp_arg, n + 1)
                act.activation(hid[:, n // 8, (n % 8) * 512:(n % 8 + 1) * 512], ang[:, n % 4, :], ACT.Sin)\
                    .then_inc(mlp_sin, 1)

            act.wait_ge(ada_mm, 2 * KT)
            for b in range(3):
                act.copy(mrow[:, b, :], spec[:, b, :] if b < 2 else modp[:, :]).then_inc(mod_cp, 1)

            def store(n):
                o, q = steps[n // 2]
                act.wait_ge(spec_cp, n + 1)
                for ri in range(2):
                    dst = g.filt_dram[o, :, q, ri].rearrange("l (j two) c -> two j l c", two=2)[n % 2]
                    act.dma_start(dst, out[64 * ri:64 * ri + 64, n % 4, :].rearrange("p (l c) -> p l c", c=LANE))\
                       .then_inc(stored[n % 4], 16)

            for n in range(2 * len(steps)):
                act.wait_ge(spec_mm, n + 1)
                if n >= 4:
                    act.wait_ge(stored[n % 4], 32 * (n // 4))
                act.copy(out[:, n % 4, :], spec[:, n % 2, :]).then_inc(spec_cp, 1)
                if n >= 1:
                    store(n - 1)
            store(2 * len(steps) - 1)
            act.wait_ge(g_turn, 1)
            act.copy(gr[:, :], misc[0:16, 256:256 + P]).then_inc(g_copy, 1)
            act.wait_ge(g_copy, 1)
            act.dma_start(g.gate_dram.rearrange("(r p) -> r p", p=P), gr[:, :]).then_inc(g_out, 16)
            act.wait_ge(g_out, 16)
            for b in range(4):
                act.wait_ge(stored[b], 32 * (2 * len(steps) // 4))

        @block.vector
        def _(ve):
            ch = Chain(ve, dve)
            ve.memset(rows[:, :], 0.0).then_inc(rows_zero, 1)
            ve.memset(sil[:, :, :], 0.0).then_inc(sil_z, 1)
            ve.wait_ge(turned, 2)
            ve.tensor_copy(g.cols[:, :], misc[:, 0:P]).then_inc(cols_ok, 1)
            ve.tensor_copy(csb[:, :], misc[:, P:P + 16]).then_inc(cols_ok, 1)
            ve.wait_ge(cols_ok, 2)
            tmp = eo
            for first in range(0, 16, 2):
                pair, layer = (first, first + 1), first // 8
                for n in pair:
                    ve.wait_ge(mlp_mm, n + 1)
                    ch(ve.tensor_scalar(tmp[0:64, n % 2, 0, :], gen[0:64, n % 4, :], g.cols[0:64, C_B1 + layer:C_B1 + layer + 1],
                                        g.cols[0:64, C_SF + layer:C_SF + layer + 1], ALU.add, ALU.mult))
                for n in pair:
                    ch.wait(ch.n - 1)
                    ch(ve.tensor_scalar(tmp[0:64, n % 2, 1, :], tmp[0:64, n % 2, 0, :], float(1 / (2 * np.pi)), ROUND, ALU.mult, ALU.add))
                for n in pair:
                    ch.wait(ch.n - 1)
                    ch(ve.tensor_scalar(tmp[0:64, n % 2, 1, :], tmp[0:64, n % 2, 1, :], ROUND, None, ALU.subtract))
                for n in pair:
                    ch.wait(ch.n - 1)
                    ch(ve.scalar_tensor_tensor(out=tmp[0:64, n % 2, 0, :], in0=tmp[0:64, n % 2, 1, :], scalar=-TWO_PI_HI,
                                               in1=tmp[0:64, n % 2, 0, :], op0=ALU.mult, op1=ALU.add))
                for n in pair:
                    if n >= 4:
                        ve.wait_ge(mlp_sin, n - 3)
                    ch.wait(ch.n - 1)
                    ch(ve.scalar_tensor_tensor(out=ang[:, n % 4, :], in0=tmp[0:64, n % 2, 1, :], scalar=-TWO_PI_LO,
                                               in1=tmp[0:64, n % 2, 0, :], op0=ALU.mult, op1=ALU.add))
                for n in pair:
                    ch.wait(ch.n - 1 + n % 2)
                    ve.tensor_scalar(ang[:, n % 4, :], ang[:, n % 4, :], 3.1415925, -3.1415925, ALU.min, ALU.max)\
                        .then_inc(mlp_arg, 1)
            ve.wait_ge(dec_ok, 2 * Q)
            ve.wait_ge(ld_small, 16 * len(small))
            ch(ve.memset(dec[0:1, 1, 0, :], 0.0))
            ch.wait()
            for n, (o, q) in enumerate(steps):
                ve.wait_ge(gen_mm, 2 * n + 2)
                if n >= 3:
                    ve.wait_ge(spec_mm, 2 * n - 4)
                for d in range(2):
                    ch(ve.tensor_tensor(fb[:, d, :], gen[:, 2 * (n % 2) + d, :], dec[:, d, q, :], ALU.mult))
                ch.wait()
                ch(ve.tensor_tensor(eo[:, n % 3, 0, :], fb[:, 0, :], fb[:, 1, :], ALU.add))
                ve.tensor_tensor(eo[:, n % 3, 1, :], fb[:, 0, :], fb[:, 1, :], ALU.subtract).then_inc(eo_ok, 1)
                ve.wait_ge(eo_ok, n + 1)
                ch.wait()
                if 3 <= n < 6:
                    ve.wait_ge(mod_t, n - 2)
                    b = n - 3
                    for a in range(2):
                        ve.tensor_tensor(g.mods[:, a, 16 * b:16 * b + 16].rearrange("p (j c) -> p c j", j=4),
                                         misc[:, :].rearrange("p (c j r) -> p c j r", c=4, j=4)[:, :, :, a],
                                         g.cols[:, C_ADAB + 16 * b:C_ADAB + 16 * b + 16].rearrange("p (j c) -> p c j", j=4),
                                         ALU.add).then_inc(mod_rd, 1)
                if n == 5:
                    ve.wait_ge(mod_rd, 6)
                    for a in range(2):
                        ch(ve.scalar_tensor_tensor(out=g.scale1[:, a, :], in0=g.mods[:, a, 8:16], scalar=1.0,
                                                   in1=g.cols[:, C_N1:C_N1 + 8], op0=ALU.add, op1=ALU.mult))
                    ch(ve.scalar_tensor_tensor(out=g.scale2[:, :], in0=g.mods[:, 0, 32:40], scalar=1.0,
                                               in1=g.cols[:, C_N2:C_N2 + 8], op0=ALU.add, op1=ALU.mult))
                    ch(ve.tensor_copy(gcol[:, 0:8], g.mods[:, 0, 16:24]))
                    ve.tensor_copy(gcol[:, 8:16], g.mods[:, 0, 40:48]).then_inc(g_cols, 1)
                    ve.wait_ge(g_cols, 1)
                    ch.wait()


def stage2(e, g):
    nc, i = e.nc, e.i
    with e.stage() as st:
        xr = e.sb(st, "xr", [P, 2, D])
        sq = e.sb(st, "sq", [P, D])
        ss = e.sb(st, "ss", [P, 2, 1])
        rs = e.sb(st, "rs", [P, 2, 1])
        xn = e.sb(st, "xn", [P, 2, D])
        tp = e.ps(st, "tp", [P, 2, KT, P])
        loaded = [e.sem(f"s2_rows_loaded{b}") for b in range(2)]
        summed = e.sem("s2_squares_summed")
        inv = e.sem("s2_variance_inverted")
        root = e.sem("s2_rstd")
        scaled = e.sem("s2_rows_scaled")
        turned = e.sem("s2_rows_turned")
        out_v = e.sem("s2_written_by_vector")
        out_a = e.sem("s2_written_by_scalar")
        dve = e.sem("s2_dve")
        NS = NT + 2
        block = st.enter_context(nc.Block())

        def tiles(eng, body):
            for n in range(2):
                body(n, n, n, g.hT, 0)
            with eng.Fori(1, NT // 2) as j:
                for b in range(2):
                    body(2 * j + b, 2 * j + b, b, g.hT, 0)
            for n in range(2):
                body(NT + n, n, n, g.hcT, 1)

        def write_last(write, n, at, b, s):
            if isinstance(n, int) and n == 0:
                return
            if s == 1 and at == 0:
                write(n - 1, NT - 1, 1 - b, g.hT, 0)
            else:
                write(n - 1, at - 1, 1 - b, g.hT if s == 0 else g.hcT, s)

        @block.sync
        def _(sp):
            def load(n, at, b, hT, s):
                if not (isinstance(n, int) and n < 2):
                    sp.wait_ge(scaled, n - 1)
                src = i["x"][0] if s == 0 else i["ctx"][0]
                sp.dma_start(xr[:, b, :], src[bass.ds(at * P, P), :]).then_inc(loaded[b], 16)
            tiles(sp, load)

        @block.scalar
        def _(act):
            def half(n, at, b, hT, s):
                act.wait_ge(turned, n + 1)
                for k in range(4, KT):
                    ins = act.activation(hT[:, k, bass.ds(at * P, P)], tp[:, b, k, :], ACT.Identity,
                                         bias=g.mods[:, s, k:k + 1], scale=g.scale1[:, s, k:k + 1])
                ins.then_inc(out_a, 1)

            def tile(n, at, b, hT, s):
                act.wait_ge(loaded[b], (n - b) * 8 + 16)
                if not (isinstance(n, int) and n == 0):
                    act.wait_ge(summed, n)
                if not (isinstance(n, int) and n < 2):
                    act.wait_ge(inv, n - 1)
                act.activation(sq[:, :], xr[:, b, :], ACT.Square, accum_out=ss[:, b, :]).then_inc(summed, 1)
                act.wait_ge(inv, n + 1)
                if not (isinstance(n, int) and n < 2):
                    act.wait_ge(scaled, n - 1)
                act.activation(rs[:, b, :], ss[:, b, :], ACT.Sqrt).then_inc(root, 1)
                write_last(half, n, at, b, s)
            tiles(act, tile)
            half(NS - 1, 1, 1, g.hcT, 1)

        @block.vector
        def _(ve):
            def tile(n, at, b, hT, s):
                ve.wait_ge(summed, n + 1)
                ve.tensor_scalar(ss[:, b, :], ss[:, b, :], 1.0 / D, EPS, ALU.mult, ALU.add).then_inc(dve, 1)
                ve.wait_ge(dve, n + 1)
                ve.reciprocal(ss[:, b, :], ss[:, b, :]).then_inc(inv, 1)
                ve.wait_ge(root, n + 1)
                if not (isinstance(n, int) and n < 2):
                    ve.wait_ge(turned, n - 1)
                ve.tensor_scalar(xn[:, b, :], xr[:, b, :], rs[:, b, :], None, ALU.mult).then_inc(scaled, 1)
                write_last(half, n, at, b, s)

            def half(n, at, b, hT, s):
                ve.wait_ge(turned, n + 1)
                for k in range(4):
                    ins = ve.tensor_scalar(hT[:, k, bass.ds(at * P, P)], tp[:, b, k, :], g.scale1[:, s, k:k + 1],
                                           g.mods[:, s, k:k + 1], ALU.mult, ALU.add)
                ins.then_inc(out_v, 1)
            tiles(ve, tile)
            half(NS - 1, 1, 1, g.hcT, 1)
            ve.wait_ge(out_a, NS)

        @block.tensor
        def _(pe):
            def turn(n, at, b, hT, s):
                pe.wait_ge(scaled, n + 1)
                if not (isinstance(n, int) and n < 2):
                    pe.wait_ge(out_v, n - 1)
                    pe.wait_ge(out_a, n - 1)
                for k in range(KT):
                    ins = pe.transpose(tp[:, b, k, :], xn[:, b, k * P:(k + 1) * P], g.ident[:, :])
                ins.then_inc(turned, 1)
            tiles(pe, turn)
            pe.wait_ge(out_v, NS)
            pe.wait_ge(out_a, NS)


def stage3(e, g):
    nc, i = e.nc, e.i
    PW = 256
    order = [2, 0, 1] + list(range(3, 9))
    CH = T // 512
    qk = [("k", 4, n) for n in range(CH)] + [("kc", 4, 0)] + [("q", ct, n) for ct in range(4) for n in range(CH)]
    hy = [(ct, n) for ct in range(12) for n in range(CH)]
    with e.stage() as st:
        w = e.sb(st, "win", [P, 3, KT, PW])
        cos = e.sb(st, "cos", [P, T])
        sin = e.sb(st, "sin", [P, T])
        ones = e.sb(st, "head_ones", [P, P])
        swap = e.sb(st, "pair_swap", [P, P])
        qw = e.sb(st, "qw", [P, 2, 512])
        sq = e.sb(st, "qsq", [P, 2, 512])
        rs = e.sb(st, "qrs", [P, 2, 512])
        rot = e.sb(st, "rot", [P, 2, 512])
        u = e.sb(st, "hu", [P, 2, T + 2])
        y = e.sb(st, "hyv", [P, 2, T])
        z = [m[:, :].rearrange("p (q c) -> p q c", q=Q) for m in (cos, sin)]
        mp = e.ps(st, "proj", [P, 4, 512])
        ap = e.ps(st, "paux", [P, 4, 512])
        ld = e.sem("s3_tables_loaded")
        ldw = [e.sem(f"s3_weights_loaded{b}") for b in range(3)]
        wdone = e.sem("s3_piece_used")
        mm = e.sem("s3_qk_product")
        w_qw = e.sem("s3_weighted")
        aux = e.sem("s3_norm_and_swap_product")
        inv = e.sem("s3_norm_inverted")
        root = e.sem("s3_rstd")
        auxr = e.sem("s3_swap_read")
        rotd = e.sem("s3_rotated")
        st_q = [e.sem(f"s3_stored{b}") for b in range(2)]
        v_mm = e.sem("s3_value_product")
        v_cp = e.sem("s3_value_copied")
        h_mm = e.sem("s3_hyena_product")
        h_cp = e.sem("s3_hyena_copied")
        conv = e.sem("s3_convolved")
        h_tr = e.sem("s3_hyena_turned")
        z_cp = e.sem("s3_hyena_turned_copied")
        st_z = [e.sem(f"s3_hyena_stored{b}") for b in range(2)]
        dve = e.sem("s3_dve")
        zeroed = e.sem("s3_zeroed")
        NV, NQ = NT + 2, len(qk)
        kpos = {"k": lambda n: C + P + 512 * n, "kc": lambda n: 0}
        block = st.enter_context(nc.Block())

        @block.sync
        def _(sp):
            for n, pc in enumerate(order):
                if n >= 3:
                    sp.wait_ge(wdone, n - 2)
                src = i["w_in"][0, :, pc * PW:(pc + 1) * PW].rearrange("(k p) c -> p k c", p=P)
                sp.dma_start(w[:, n % 3, :, :], src).then_inc(ldw[n % 3], 16)
                if n == 0:
                    for dst, src in ((ones, "head_ones"), (swap, "pair_swap"), (cos, "rope_cos"), (sin, "rope_sin")):
                        sp.dma_start(dst[:, :], i[src]).then_inc(ld, 16)
                    sp.dma_start(g.kT[HD:HD + 1, :, :].rearrange("p a t -> p (a t)"), i["key_bias"]).then_inc(ld, 16)

        @block.tensor
        def _(pe):
            def product(n, kind, ct, c):
                pc = order.index(ct // 2)
                pe.wait_ge(ldw[pc % 3], 16 * (pc // 3 + 1))
                if n >= 4:
                    pe.wait_ge(w_qw, n - 3)
                N = C if kind == "kc" else 512
                for k in range(KT):
                    rhs = g.hcT[:, k, :] if kind == "kc" else g.hT[:, k, c * 512:(c + 1) * 512]
                    ins = pe.matmul(mp[:, n % 4, 0:N], w[:, pc % 3, k, (ct % 2) * P:(ct % 2 + 1) * P], rhs,
                                    start=(k == 0), stop=(k == KT - 1))
                ins.then_inc(mm, 1)

            def norm(n, kind):
                N = C if kind == "kc" else 512
                pe.wait_ge(w_qw, n + 1)
                if n >= 2:
                    pe.wait_ge(auxr, n - 1)
                b = 2 * (n % 2)
                pe.matmul(ap[:, b, 0:N], ones[:, :], sq[:, n % 2, 0:N], start=True, stop=True)
                pe.matmul(ap[:, b + 1, 0:N], swap[:, :], qw[:, n % 2, 0:N], start=True, stop=True).then_inc(aux, 1)

            for n, (kind, ct, c) in enumerate(qk):
                product(n, kind, ct, c)
                if n == 1:
                    pe.wait_ge(ld, 16 * 5)
                if n >= 1:
                    norm(n - 1, qk[n - 1][0])
                if n == 4:
                    for t in range(NV):
                        if t >= 4:
                            pe.wait_ge(v_cp, t - 3)
                        else:
                            pe.wait_ge(w_qw, n + 1)
                        for k in range(KT):
                            x = g.hT[:, k, t * P:(t + 1) * P] if t < NT else g.hcT[:, k, (t - NT) * P:(t - NT + 1) * P]
                            ins = pe.matmul(mp[:, (t + 1) % 4, 0:P], x, w[:, 0, k, P:2 * P],
                                            start=(k == 0), stop=(k == KT - 1))
                        ins.then_inc(v_mm, 1)
                    pe.wait_ge(v_cp, NV)
                    pe.nop().then_inc(wdone, 1)
                if kind == "q" and ct % 2 == 1 and c == CH - 1:
                    pe.wait_ge(mm, n + 1)
                    pe.nop().then_inc(wdone, 1)
            def turn(ct):
                pe.wait_ge(conv, ct + 1)
                for b in range(4):
                    if ct >= 1:
                        pe.wait_ge(z_cp, 4 * ct + b - 3)
                    for a in range(4):
                        ins = pe.transpose(ap[:, b, a * P:(a + 1) * P], y[:, ct % 2, 4 * b + a::Q], g.ident[:, :])
                    ins.then_inc(h_tr, 1)

            for n, (ct, c) in enumerate(hy):
                pc = 3 + ct // 2
                pe.wait_ge(ldw[pc % 3], 16 * (pc // 3 + 1))
                if n >= 4:
                    pe.wait_ge(h_cp, n - 3)
                else:
                    pe.wait_ge(w_qw, NQ + n - 3)
                for k in range(KT):
                    ins = pe.matmul(mp[:, (NQ + n) % 4, :], w[:, pc % 3, k, (ct % 2) * P:(ct % 2 + 1) * P],
                                    g.hT[:, k, c * 512:(c + 1) * 512], start=(k == 0), stop=(k == KT - 1))
                ins.then_inc(h_mm, 1)
                if n == 0:
                    norm(NQ - 1, "q")
                    pe.wait_ge(auxr, NQ)
                if ct % 2 == 1 and c == CH - 1:
                    pe.wait_ge(h_mm, n + 1)
                    pe.nop().then_inc(wdone, 1)
                if ct >= 1 and c == 1:
                    turn(ct - 1)
            turn(11)

        @block.scalar
        def _(act):
            def weigh(n, kind, ct):
                N = C if kind == "kc" else 512
                col = C_QN if kind == "q" else C_KN
                act.wait_ge(mm, n + 1)
                if n >= 2:
                    act.wait_ge(aux, n - 1)
                    act.wait_ge(rotd, n - 1)
                act.activation(qw[:, n % 2, 0:N], mp[:, n % 4, 0:N], ACT.Identity, scale=g.cols[:, col:col + 1])
                act.activation(sq[:, n % 2, 0:N], mp[:, n % 4, 0:N], ACT.Square).then_inc(w_qw, 1)

            def rstd(n, kind):
                N = C if kind == "kc" else 512
                act.wait_ge(inv, n + 1)
                act.activation(rs[:, n % 2, 0:N], rs[:, n % 2, 0:N], ACT.Sqrt).then_inc(root, 1)

            for n, (kind, ct, c) in enumerate(qk):
                weigh(n, kind, ct)
                if n >= 1:
                    rstd(n - 1, qk[n - 1][0])
                if n == 4:
                    for t in range(NV):
                        act.wait_ge(v_mm, t + 1)
                        at = 3 + t if t < NT else t - NT
                        act.copy(g.v[:, at, :], mp[:, (t + 1) % 4, 0:P]).then_inc(v_cp, 1)
            rstd(len(qk) - 1, "q")
            act.wait_ge(zeroed, 5)

            def turned(ct):
                for b in range(4):
                    act.wait_ge(h_tr, 4 * ct + b + 1)
                    if ct >= 2 and b == 0:
                        act.wait_ge(st_z[ct % 2], 16 * (ct // 2))
                    if ct == 0 and b == 0:
                        act.wait_ge(rotd, NQ)
                    act.copy(z[ct % 2][:, 4 * b:4 * b + 4, :].rearrange("p q c -> p (q c)"), ap[:, b, :]).then_inc(z_cp, 1)
                act.wait_ge(z_cp, 4 * ct + 4)
                dst = g.hy_dram[ct // 4].rearrange("(p q) c -> p q c", q=Q)[:, :, (ct % 4) * P:(ct % 4 + 1) * P]
                act.dma_start(dst, z[ct % 2]).then_inc(st_z[ct % 2], 16)

            for n, (ct, c) in enumerate(hy):
                act.wait_ge(h_mm, n + 1)
                if ct >= 2 and c == 0:
                    act.wait_ge(conv, ct - 1)
                act.copy(u[:, ct % 2, 1 + c * 512:1 + (c + 1) * 512], mp[:, (NQ + n) % 4, :]).then_inc(h_cp, 1)
                if ct >= 1 and c == 2:
                    turned(ct - 1)
            turned(11)
            for b in range(2):
                act.wait_ge(st_z[b], 16 * 6)

        @block.vector
        def _(ve):
            ch = Chain(ve, dve)
            ve.memset(u[:, :, 0:1], 0.0).then_inc(zeroed, 1)
            ve.memset(u[:, :, T + 1:T + 2], 0.0).then_inc(zeroed, 1)
            ve.memset(g.v[:, 2:20:17, :], 0.0).then_inc(zeroed, 1)
            for n, (kind, ct, c) in enumerate(qk):
                N = C if kind == "kc" else 512
                b = n % 2
                ve.wait_ge(aux, n + 1)
                if n >= 2:
                    ve.wait_ge(st_q[b], 32 * (n // 2))
                ch(ve.tensor_scalar(rs[:, b, 0:N], ap[:, 2 * b, 0:N], 1.0 / HD, EPS, ALU.mult, ALU.add))
                ch.wait()
                ve.reciprocal(rs[:, b, 0:N], rs[:, b, 0:N]).then_inc(inv, 1)
                if kind == "kc":
                    ve.wait_ge(root, n + 1)
                    ve.tensor_tensor(rot[:, b, 0:N], qw[:, b, 0:N], rs[:, b, 0:N], ALU.mult).then_inc(rotd, 1)
                    ve.nop().then_inc(auxr, 1)
                    continue
                ch(ve.tensor_tensor(rot[:, b, :], ap[:, 2 * b + 1, :], sin[:, c * 512:(c + 1) * 512], ALU.mult))
                ch(ve.tensor_tensor(qw[:, b, :], qw[:, b, :], cos[:, c * 512:(c + 1) * 512], ALU.mult))
                ch.wait()
                ve.tensor_tensor(rot[:, b, :], rot[:, b, :], qw[:, b, :], ALU.add).then_inc(auxr, 1)
                ve.wait_ge(root, n + 1)
                ve.wait_ge(auxr, n + 1)
                ve.tensor_tensor(rot[:, b, :], rot[:, b, :], rs[:, b, :], ALU.mult).then_inc(rotd, 1)
            for ct in range(12):
                b = ct % 2
                ve.wait_ge(h_cp, 4 * ct + 4)
                if ct >= 2:
                    ve.wait_ge(h_tr, 4 * ct - 4)
                wc = [g.cols[:, C_CW + 12 * j + ct:C_CW + 12 * j + ct + 1] for j in range(3)]
                ch(ve.tensor_scalar(y[:, b, :], u[:, b, 1:T + 1], wc[1], g.cols[:, C_CB + ct:C_CB + ct + 1],
                                    ALU.mult, ALU.add))
                ch.wait()
                ch(ve.scalar_tensor_tensor(out=y[:, b, :], in0=u[:, b, 0:T], scalar=wc[0], in1=y[:, b, :],
                                           op0=ALU.mult, op1=ALU.add))
                ch.wait()
                ve.scalar_tensor_tensor(out=y[:, b, :], in0=u[:, b, 2:T + 2], scalar=wc[2], in1=y[:, b, :],
                                        op0=ALU.mult, op1=ALU.add).then_inc(conv, 1)

        @block.gpsimd
        def _(pool):
            pool.memset(g.kT[0:HD, :, C:C + P], 0.0).then_inc(zeroed, 1)
            pool.memset(g.kT[0:HD, :, C + P + T:], 0.0).then_inc(zeroed, 1)
            for n, (kind, ct, c) in enumerate(qk):
                N = C if kind == "kc" else 512
                pool.wait_ge(rotd, n + 1)
                for h in range(2):
                    src = rot[HD * h:HD * h + HD, n % 2, 0:N]
                    if kind == "q":
                        dst = g.q_dram[4 * c:4 * c + 4, :, 2 * ct + h, :].rearrange("b d t -> d b t")
                        src = src.rearrange("p (b t) -> p b t", t=P)
                    else:
                        dst = g.kT[0:HD, h, kpos[kind](c):kpos[kind](c) + N]
                    pool.dma_start(dst, src).then_inc(st_q[n % 2], 16)
            for b in range(2):
                pool.wait_ge(st_q[b], 32 * ((len(qk) - b + 1) // 2))
            pool.wait_ge(zeroed, 5)


def stage4(e, g):
    nc, i = e.nc, e.i
    LN = 2
    jobs = [(r, o, l) for r in range(NL // LN) for o in range(2) for l in range(LN)]
    NJ, NC = len(jobs), 8
    order = []
    for b in range(0, NJ, LN):
        order += [(s, b + l) for s in ("I", "II", "V") for l in range(LN)]
    uses, use_of = [], {}
    for s, j in order:
        for c in range({"I": 8, "II": NC, "V": 4}[s]):
            use_of[s, j, c] = len(uses)
            uses.append("v" if s == "V" else "a")
    nth = [sum(x == uses[n] for x in uses[:n + 1]) for n in range(len(uses))]
    with e.stage() as st:
        fwd = e.sb(st, "fwd4", [P, Q, 2, P])
        inv = e.sb(st, "inv4", [P, Q, 2, P])
        mid = e.sb(st, "mid4", [P, 10, P])
        skip = e.sb(st, "skip", [P, LN, LANE])
        zr = [e.sb(st, f"zr{l}", [P, Q, LANE]) for l in range(LN)]
        gt = [e.sb(st, f"gt{l}", [P, Q, LANE]) for l in range(LN)]
        sp_ = [e.sb(st, f"sp{l}", [P, Q, 2, LANE]) for l in range(LN)]
        yx = [e.sb(st, f"yx{l}", [P, 32, LANE]) for l in range(LN)]
        yh = [e.sb(st, f"yh{l}", [P, 32, LANE]) for l in range(LN)]
        ab = e.sb(st, "ab", [P, 2, 2, 512])
        prod = e.ps(st, "prod", [P, 2, 3, 512])
        ob = e.ps(st, "ob", [P, 2, 512])
        y_dram = e.dram("hy_y", [LN, Q, 2, P, LANE])
        v_dram = e.dram("hy_v", [LN, Q, 2, P, LANE])
        ld = e.sem("s4_tables_loaded")
        ld_mid = e.sem("s4_middle_tables_loaded")
        ld_inv = e.sem("s4_inverse_table_loaded")
        ld_z = [e.sem(f"s4_z_loaded{l}") for l in range(LN)]
        ld_g = [e.sem(f"s4_gate_loaded{l}") for l in range(LN)]
        ld_h = [e.sem(f"s4_filter_loaded{l}") for l in range(LN)]
        i_mm = e.sem("s4_I_product")
        i_cp = [e.sem(f"s4_I_copied{l}") for l in range(LN)]
        y_st = [e.sem(f"s4_Y_stored{l}") for l in range(LN)]
        y_ld = [e.sem(f"s4_Y_loaded{l}") for l in range(LN)]
        x_mm = e.sem("s4_spectra_product")
        x_cp = e.sem("s4_X_copied")
        ab_ok = e.sem("s4_spectra_multiplied")
        v_mm = e.sem("s4_II_inverse_product")
        v_cp = [e.sem(f"s4_II_inverse_copied{l}") for l in range(LN)]
        v_st = [e.sem(f"s4_V_stored{l}") for l in range(LN)]
        v_ld = [[e.sem(f"s4_V_loaded{l}_{c}") for c in range(4)] for l in range(LN)]
        o_mm = e.sem("s4_conv_product")
        o_rd = e.sem("s4_conv_read")
        z_ok = [e.sem(f"s4_z_ready{l}") for l in range(LN)]
        z_st = [e.sem(f"s4_z_stored{l}") for l in range(LN)]
        act_rd = e.sem("s4_bank_read_by_scalar")
        dve = e.sem("s4_dve")
        block = st.enter_context(nc.Block())

        def bank_free(pe, s, j, c):
            n = use_of[s, j, c]
            if n >= 2:
                pe.wait_ge(act_rd if uses[n - 2] == "a" else o_rd, nth[n - 2])
            return n % 2

        @block.sync
        def _(sp):
            def part0(j):
                r, o, l = jobs[j]
                ln = LN * r + l
                if o == 0:
                    if r >= 1:
                        sp.wait_ge(z_st[l], 16 * r)
                    src = g.hy_dram[0].rearrange("(p q) c -> p q c", q=Q)[:, :, ln * LANE:(ln + 1) * LANE]
                    sp.dma_start(zr[l][:, :, :], src).then_inc(ld_z[l], 16)

            def inputs(j):
                r, o, l = jobs[j]
                ln = LN * r + l
                k = j // LN
                if k >= 1:
                    sp.wait_ge(z_ok[l], 4 * k)
                src = g.hy_dram[o + 1].rearrange("(p q) c -> p q c", q=Q)[:, :, ln * LANE:(ln + 1) * LANE]
                sp.dma_start(gt[l][:, :, :], src).then_inc(ld_g[l], 16)
                src = i["hy_skip"][0, o, ln * LANE:(ln + 1) * LANE].partition_broadcast(P)
                sp.dma_start(skip[:, l, :], src).then_inc(ld_g[l], 16)

            def filt(j):
                r, o, l = jobs[j]
                if j >= LN:
                    sp.wait_ge(x_mm, NC * (j - LN + 1))
                for s in range(4):
                    src = g.filt_dram[o, LN * r + l].rearrange("q r (s g) c -> s (q r) (g c)", s=4)[s]
                    sp.dma_start(yh[l][32 * s:32 * s + 32, :, :].rearrange("p g c -> p (g c)"), src).then_inc(ld_h[l], 16)

            sp.dma_start(fwd[:, :, :, :], i["dft_fwd"].rearrange("p (q r k) -> p q r k", q=Q, r=2)).then_inc(ld, 16)
            for j in range(LN):
                part0(j)
            sp.dma_start(mid[:, :, :], i["dft_mid"].rearrange("p (m k) -> p m k", m=10)).then_inc(ld_mid, 16)
            filt(0)
            for s, j in order:
                r, o, l = jobs[j]
                k = j // LN
                if s == "I":
                    for c in range(4):
                        sp.wait_ge(i_cp[l], 8 * k + 2 * c + 2)
                        dst = y_dram[l, 4 * c:4 * c + 4].rearrange("q r k c -> k (q r) c")
                        sp.dma_start(dst, sp_[l][:, 4 * c:4 * c + 4, :, :].rearrange("p q r c -> p (q r) c"))\
                          .then_inc(y_st[l], 16)
                    sp.wait_ge(y_st[l], 64 * (k + 1))
                    if k >= 1:
                        sp.wait_ge(v_st[l], 128 * k)
                    for c in range(4):
                        src = y_dram[l].rearrange("q r (s g) c -> s (q r) (g c)", s=4)[c]
                        sp.dma_start(yx[l][32 * c:32 * c + 32, :, :].rearrange("p g c -> p (g c)"), src)\
                          .then_inc(y_ld[l], 16)
                if j == 0 and s == "I":
                    filt(1)
                if j == 1 and s == "I":
                    sp.dma_start(inv[:, :, :, :], i["dft_inv"].rearrange("p (q r k) -> p q r k", q=Q, r=2)).then_inc(ld_inv, 16)
                    for first in range(LN):
                        inputs(first)
                if s == "II":
                    for half in range(2):
                        sp.wait_ge(v_cp[l], NC * k + 4 * half + 4)
                        for c in range(4):
                            dst = v_dram[l].rearrange("q r (s g) c -> s (q r) g c", s=4)[c, :, 16 * half:16 * half + 16]
                            sp.dma_start(dst, yx[l][32 * c:32 * c + 32, 16 * half:16 * half + 16, :]).then_inc(v_st[l], 16)
                    sp.wait_ge(v_st[l], 128 * (k + 1))
                    for c in range(4):
                        src = v_dram[l, 4 * c:4 * c + 4].rearrange("q r k c -> k (q r) c")
                        sp.dma_start(sp_[l][:, 4 * c:4 * c + 4, :, :].rearrange("p q r c -> p (q r) c"), src)\
                          .then_inc(v_ld[l][c], 16)
                    if j + LN < NJ:
                        filt(j + LN)
                if s == "V":
                    if o == 1:
                        sp.wait_ge(z_ok[l], 4 * (k + 1))
                        dst = g.hyo_dram.rearrange("(p q) c -> p q c", q=Q)[:, :, (LN * r + l) * LANE:(LN * r + l + 1) * LANE]
                        sp.dma_start(dst, zr[l][:, :, :]).then_inc(z_st[l], 16)
                    if j + LN < NJ:
                        part0(j + LN)
                        inputs(j + LN)
            for l in range(LN):
                sp.wait_ge(z_st[l], 16 * (NL // LN))

        @block.tensor
        def _(pe):
            pe.wait_ge(ld, 16)
            for s, j in order:
                r, o, l = jobs[j]
                k = j // LN
                if s == "I":
                    if o == 0:
                        pe.wait_ge(ld_z[l], 16 * (r + 1))
                    else:
                        pe.wait_ge(z_ok[l], 4 * k)
                    for c in range(8):
                        b = bank_free(pe, s, j, c)
                        for a in range(4):
                            ins = pe.matmul(ob[:, b, a * LANE:(a + 1) * LANE], fwd[:, 2 * c + a // 2, a % 2, :],
                                            zr[l][:, 2 * c + a // 2, :], start=True, stop=True)
                        ins.then_inc(i_mm, 1)
                if s == "II":
                    if j == 0:
                        pe.wait_ge(ld_mid, 16)
                    pe.wait_ge(y_ld[l], 64 * (k + 1))
                    pe.wait_ge(ld_h[l], 64 * (k + 1))
                    for c in range(NC + 1):
                        if c < NC:
                            n = j * NC + c
                            if n >= 2:
                                pe.wait_ge(ab_ok, n - 1)
                            for m in range(3):
                                src = yx[l] if m == 0 else yh[l]
                                if c == 0:
                                    pe.matmul(prod[:, n % 2, m, 0:LANE], mid[:, 5 + m, :], src[:, 0, :],
                                              start=True, stop=True)
                                    ins = pe.matmul(prod[:, n % 2, m, LANE:512], mid[:, m, :],
                                                    src[:, 1:4, :].rearrange("p g c -> p (g c)"), start=True, stop=True)
                                else:
                                    ins = pe.matmul(prod[:, n % 2, m, :], mid[:, m, :],
                                                    src[:, 4 * c:4 * c + 4, :].rearrange("p g c -> p (g c)"),
                                                    start=True, stop=True)
                            ins.then_inc(x_mm, 1)
                        if c >= 1:
                            cc, n = c - 1, j * NC + c - 1
                            b = bank_free(pe, s, j, cc)
                            pe.wait_ge(ab_ok, n + 1)
                            if cc == 0:
                                for m in range(2):
                                    pe.matmul(ob[:, b, 0:LANE], mid[:, 8 + m, :], ab[:, n % 2, m, 0:LANE],
                                              start=(m == 0), stop=(m == 1))
                                for m in range(2):
                                    ins = pe.matmul(ob[:, b, LANE:512], mid[:, 3 + m, :], ab[:, n % 2, m, LANE:512],
                                                    start=(m == 0), stop=(m == 1))
                            else:
                                for m in range(2):
                                    ins = pe.matmul(ob[:, b, :], mid[:, 3 + m, :], ab[:, n % 2, m, :],
                                                    start=(m == 0), stop=(m == 1))
                            ins.then_inc(v_mm, 1)
                if s == "V":
                    if j == 0:
                        pe.wait_ge(ld_inv, 16)
                    for c in range(4):
                        pe.wait_ge(v_ld[l][c], 16 * (k + 1))
                        b = bank_free(pe, s, j, c)
                        for a in range(4):
                            for ri in range(2):
                                ins = pe.matmul(ob[:, b, a * LANE:(a + 1) * LANE], inv[:, 4 * c + a, ri, :],
                                                sp_[l][:, 4 * c + a, ri, :], start=(ri == 0), stop=(ri == 1))
                        ins.then_inc(o_mm, 1)

        @block.scalar
        def _(act):
            ni = nv = na = 0
            for s, j in order:
                r, o, l = jobs[j]
                k = j // LN
                if s == "I":
                    for c in range(8):
                        ni += 1
                        act.wait_ge(i_mm, ni)
                        if k >= 1 and c == 0:
                            act.wait_ge(o_mm, 4 * (j - LN + 1))
                        act.copy(sp_[l][:, 2 * c:2 * c + 2, :, :].rearrange("p q r c -> p (q r c)"),
                                 ob[:, use_of[s, j, c] % 2, :]).then_inc(act_rd, 1)
                        na += 1
                        act.wait_ge(act_rd, na)
                        act.nop().then_inc(i_cp[l], 1)
                if s == "II":
                    for c in range(NC + 1):
                        if c < NC:
                            n = j * NC + c
                            act.wait_ge(x_mm, n + 1)
                            if n >= 2:
                                act.wait_ge(ab_ok, n - 1)
                            if n >= 2:
                                act.wait_ge(v_mm, n - 1)
                            act.copy(ab[:, n % 2, 0, :], prod[:, n % 2, 0, :]).then_inc(x_cp, 1)
                        if c >= 1:
                            cc = c - 1
                            nv += 1
                            act.wait_ge(v_mm, nv)
                            act.copy(yx[l][:, 4 * cc:4 * cc + 4, :].rearrange("p g c -> p (g c)"),
                                     ob[:, use_of[s, j, cc] % 2, :]).then_inc(act_rd, 1)
                            na += 1
                            act.wait_ge(act_rd, na)
                            act.nop().then_inc(v_cp[l], 1)

        @block.vector
        def _(ve):
            ch = Chain(ve, dve)
            no = 0
            for s, j in order:
                r, o, l = jobs[j]
                k = j // LN
                if s == "II":
                    for c in range(NC):
                        n = j * NC + c
                        ve.wait_ge(x_cp, n + 1)
                        if n >= 2:
                            ve.wait_ge(v_mm, n - 1)
                        ch(ve.tensor_tensor(ab[:, n % 2, 1, :], ab[:, n % 2, 0, :], prod[:, n % 2, 2, :], ALU.mult))
                        ch.wait()
                        ve.tensor_tensor(ab[:, n % 2, 0, :], ab[:, n % 2, 0, :], prod[:, n % 2, 1, :], ALU.mult)\
                            .then_inc(ab_ok, 1)
                if s == "V":
                    sk = skip[:, l, :].unsqueeze(1).broadcast_to([P, 4, LANE])
                    ve.wait_ge(ld_g[l], 32 * (k + 1))
                    for c in range(4):
                        zc = zr[l][:, 4 * c:4 * c + 4, :]
                        ve.wait_ge(i_mm, 8 * (j + 1))
                        ch(ve.tensor_tensor(zc, zc, sk, ALU.mult))
                        ch.wait()
                        no += 1
                        ve.wait_ge(o_mm, no)
                        ve.tensor_tensor(zc, ob[:, use_of[s, j, c] % 2, :].rearrange("p (q c) -> p q c", q=4), zc, ALU.add)\
                            .then_inc(o_rd, 1)
                        ve.wait_ge(o_rd, no)
                        ve.tensor_tensor(zc, zc, gt[l][:, 4 * c:4 * c + 4, :], ALU.mult).then_inc(z_ok[l], 1)


class Tile:

    def __init__(self, half, off):
        self.half, self.par = half + off // 2, off % 2
        self.n = 2 * half + off

    def back(self, k):
        return Tile(self.half, self.par - k)


def wait(eng, sem, value):
    if not (isinstance(value, int) and value <= 0):
        eng.wait_ge(sem, value)


def pipeline(eng, step):
    step(Tile(0, -1), True, False, False, False, False)
    step(Tile(0, 0), True, True, False, False, False)
    step(Tile(0, 1), True, True, True, False, False)
    step(Tile(0, 2), True, True, True, True, False)
    with eng.Fori(1, NT // 2 - 1) as j:
        for off in (1, 2):
            step(Tile(j, off), True, True, True, True, True)
    step(Tile(0, NT - 1), False, True, True, True, True)
    step(Tile(0, NT), False, False, True, True, True)
    step(Tile(0, NT + 1), False, False, False, True, True)
    step(Tile(0, NT + 2), False, False, False, False, True)


def stage5(e, g):
    nc, i = e.nc, e.i
    KEYS = C + 3 * P
    with e.stage() as st:
        wo = e.sb(st, "wo", [P, KT, D])
        rw = e.sb(st, "rw", [P, KT, NG + NE])
        rb = e.sb(st, "rb", [P, NG + NE])
        g1 = e.sb(st, "g1row", [P, D])
        mask = e.sb(st, "mask", [P, KEYS])
        nsink = e.sb(st, "nsink", [P, NH])
        sink = e.sb(st, "sink", [P, NH])
        upper = e.sb(st, "upper", [P, P])
        ones = e.sb(st, "ones", [P, P])
        rank8 = e.sb(st, "rank8", [P, 8])
        slot0 = e.sb(st, "slot0", [P, NE])
        token = e.sb(st, "token", [P, NT], I32)
        fill = e.sb(st, "fill", [P, (NE * CAP + P) * 2 // P], I32)
        qb = [e.sb(st, f"qb{b}", [HD + 1, NH, P]) for b in range(2)]
        pr = [e.sb(st, f"pr{b}", [P, NH, KEYS]) for b in range(2)]
        mx = e.sb(st, "mx", [P, 2, NH])
        nm = e.sb(st, "nm", [P, 2, NH])
        rsum = e.sb(st, "rsum", [P, 2, NH])
        esk = e.sb(st, "esk", [P, 2, NH])
        pt = e.sb(st, "pt", [P, 2, KEYS])
        mix = [e.sb(st, f"mix{b}", [P, 2, HW]) for b in range(2)]
        sqs = e.sb(st, "sqs", [P, D])
        ms = e.sb(st, "ms", [P, 2, 2])
        nw = e.sb(st, "nw", [P, 3, 2])
        n2 = e.sb(st, "n2", [P, 4])
        mixn = e.sb(st, "mixn", [P, 2, HW])
        mixT = e.sb(st, "mixT", [P, KT, P])
        xr = [e.sb(st, f"xres{b}", [P, D]) for b in range(2)]
        x2 = [e.sb(st, f"x2_{b}", [P, D]) for b in range(2)]
        xn = [e.sb(st, f"xn2_{b}", [P, D]) for b in range(2)]
        h2T = e.sb(st, "h2T", [P, KT, P])
        lg = e.sb(st, "lg", [P, 2, NG + NE])
        gexp = e.sb(st, "gexp", [P, 2, NG])
        r4 = e.sb(st, "r4", [P, 2, 16])
        oh = e.sb(st, "oh", [P, 4, 8])
        powers = e.sb(st, "powers", [P, 3])
        selg = e.sb(st, "selg", [P, NG, EPG])
        pick = e.sb(st, "pick", [P, 2, 3, NE])
        pos = e.sb(st, "pos", [P, 2, NE])
        pxs = e.sb(st, "pxs", [P, 2, NE])
        idx = e.sb(st, "idx", [P, 2, 2], I32)
        rec = e.sb(st, "rec", [P, 2, 2, 2], I32)
        S = e.ps(st, "S", [P, 2, 512])
        PT = e.ps(st, "PT", [P, 2, 512])
        O = e.ps(st, "O", [P, NH, HD])
        M = e.ps(st, "M", [P, 2, 512])
        R = e.ps(st, "R", [P, 512])

        ld = e.sem("s5_tables_loaded")
        ld_later = e.sem("s5_later_tables_loaded")
        setup = e.sem("s5_set_up")
        filled = e.sem("s5_table_filled")
        ld_q = [e.sem(f"s5_queries_loaded{b}") for b in range(2)]
        ld_x = [e.sem(f"s5_rows_loaded{b}") for b in range(2)]
        qk = e.sem("s5_scores")
        sm = e.sem("s5_scores_masked")
        nmx = e.sem("s5_maximum")
        ex = e.sem("s5_exponentials")
        esn = e.sem("s5_sink_argument")
        eso = e.sem("s5_sink_exponential")
        tp = e.sem("s5_exponentials_turned")
        tc = e.sem("s5_turned_copied")
        pv = e.sem("s5_head_values")
        att = e.sem("s5_attention_scaled")
        sqa = e.sem("s5_mixer_squares")
        mxn = e.sem("s5_mixer_normalised")
        t1 = e.sem("s5_mixer_turned")
        t1v = e.sem("s5_mixer_turned_copied_v")
        t1a = e.sem("s5_mixer_turned_copied_a")
        op = e.sem("s5_projected")
        res = e.sem("s5_residual_added")
        sq2 = e.sem("s5_residual_squares")
        xnd = e.sem("s5_residual_normalised")
        t2 = e.sem("s5_residual_turned")
        t2v = e.sem("s5_residual_turned_copied_v")
        t2a = e.sem("s5_residual_turned_copied_a")
        rt = e.sem("s5_router_product")
        lgd = e.sem("s5_logits_copied")
        rt1 = e.sem("s5_experts_picked")
        gex = e.sem("s5_gate_exponentials")
        px = e.sem("s5_prefix_product")
        pxr = e.sem("s5_prefix_read")
        rec_ok = e.sem("s5_records_ready")
        sc = [e.sem(f"s5_records_scattered{b}") for b in range(2)]
        st_x = [e.sem(f"s5_rows_stored{b}") for b in range(2)]
        dve = e.sem("s5_dve")
        ps = e.sem("s5_pool")
        ld_h = [e.sem(f"s5_hyena_rows_loaded{b}") for b in range(2)]
        nwd = e.sem("s5_mixer_variance_inverted")
        n2d = e.sem("s5_residual_variance_inverted")
        passed = e.sem("s5_waits_passed_v")
        passed_p = e.sem("s5_waits_passed_p")
        block = st.enter_context(nc.Block())

        tables = [(mask[:, :], i["mask"]), (sink[:, :], i["attn_sink"][0].partition_broadcast(P))]
        later = [
                  (upper[:, :], i["upper"]), (rank8[:, :], i["rank8"]), (slot0[:, :], i["slot0"]),
                  (token[:, :], i["token"]),
                  (rb[:, 0:NG], i["router_g_b"][0].partition_broadcast(P)),
                  (rb[:, NG:], i["router_e_b"][0].partition_broadcast(P)),
                  (rw[:, :, 0:NG], i["router_g_w"][0].rearrange("(k p) n -> p k n", p=P)),
                  (rw[:, :, NG:], i["router_e_w"][0].rearrange("(k p) n -> p k n", p=P)),
                  (g1[:, :], g.gate_dram[0:D].partition_broadcast(P)),
                  (wo[:, :, :], i["w_out"][0].rearrange("(k p) n -> p k n", p=P))]

        @block.sync
        def _(sp):
            for dst, src in tables:
                sp.dma_start(dst, src).then_inc(ld, 16)

            def step(t, scores, values, project, route, place):
                if scores:
                    b = t.back(-1)
                    wait(sp, qk, 8 * (b.n - 1))
                    sp.dma_start(qb[b.par][0:HD, :, :], g.q_dram[bass.ds(b.n, 1)].rearrange("a d h t -> (a d) h t"))\
                      .then_inc(ld_q[b.par], 16)
                    wait(sp, mxn, b.n - 1)
                    if isinstance(b.n, int) and b.n == 0:
                        for dst, src in later:
                            sp.dma_start(dst, src).then_inc(ld_later, 16)
                    sp.dma_start(mix[b.par][:, 1, :], g.hyo_dram[bass.ds(b.n * P, P), :]).then_inc(ld_h[b.par], 16)
                if values:
                    wait(sp, res, t.n - 1)
                    sp.dma_start(xr[t.par][:, :], i["x"][0, bass.ds(t.n * P, P), :]).then_inc(ld_x[t.par], 16)
                if route:
                    b = t.back(2)
                    sp.wait_ge(res, b.n + 1)
                    sp.dma_start(e.out[0, bass.ds(b.n * P, P), :], x2[b.par][:, :]).then_inc(st_x[b.par], 16)
                    sp.wait_ge(xnd, b.n + 1)
                    sp.dma_start(g.xn_dram[bass.ds(b.n * P, P), :], xn[b.par][:, :]).then_inc(st_x[b.par], 16)
            pipeline(sp, step)
            for b in range(2):
                sp.wait_ge(st_x[b], 32 * (NT // 2))

        @block.gpsimd
        def _(pool):
            carry = g.carry
            pool.memset(fill[:, :], NOWHERE).then_inc(setup, 1)
            pool.memset(carry[:, :], 0.0).then_inc(setup, 1)
            pool.memset(powers[:, 0:1], -1.0).then_inc(setup, 1)
            pool.memset(powers[:, 1:3], -0.5).then_inc(setup, 1)
            pool.wait_ge(setup, 8)
            pool.dma_start(g.table.rearrange("(p a) c -> p (a c)", p=P), fill[:, :]).then_inc(filled, 16)
            pool.wait_ge(filled, 16)
            pool.wait_ge(ld_later, 16 * len(later))

            def do(ins):
                ins.then_inc(ps, 1)
                pool.wait_ge(ps, 1)
                pool.sem_clear(ps)

            def rsqrt(y, v, n):
                return pool.tensor_tensor(y, v, powers[:, 1:1 + n], ALU.pow)

            def largest(out, x, n):
                do(pool.tensor_scalar(out, x[:, 0:1], x[:, 1:2], x[:, 2:3], ALU.max, ALU.max))
                for k in range(3, n - 1, 2):
                    do(pool.tensor_scalar(out, out, x[:, k:k + 1], x[:, k + 1:k + 2], ALU.max, ALU.max))
                do(pool.tensor_scalar(out, out, x[:, n - 1:n], None, ALU.max))

            def one_hot(out, x, m, n, col):
                do(pool.tensor_scalar(out, x, m, None, ALU.is_equal))
                do(pool.tensor_tensor(out, out, rank8[:, 0:n], ALU.mult))
                largest(col, out, n)
                do(pool.tensor_scalar(out, out, col, None, ALU.is_equal))

            def step(t, scores, values, project, route, place):
                if route:
                    b = t.back(2)
                    pool.wait_ge(sq2, b.n + 1)
                    pool.sem_inc(passed_p, 1)
                    do(pool.tensor_scalar(n2[:, 2:3], n2[:, 3:4], 1.0 / D, EPS, ALU.mult, ALU.add))
                    rsqrt(n2[:, 0:1], n2[:, 2:3], 1).then_inc(n2d, 1)
                if place:
                    pl = t.back(3)
                    b = pl.par
                    pool.wait_ge(pxr, pl.n + 1)
                    wait(pool, sc[b], 32 * pl.half)
                    pool.wait_ge(gex, pl.n + 1)
                    pool.sem_inc(passed_p, 1)
                    do(pool.tensor_tensor(pxs[:, 0, :], pxs[:, 0, :], carry[:, :], ALU.add))
                    do(pool.tensor_tensor(carry[:, :], pxs[:, 1, :], carry[:, :], ALU.add))
                    do(pool.tensor_tensor(pxs[:, 0, :], pxs[:, 0, :], slot0[:, :], ALU.add))
                    do(pool.tensor_tensor(pos[:, :, :], pick[:, b, 0:2, :],
                                          pxs[:, 0:1, :].broadcast_to([P, 2, NE]), ALU.mult))
                    n = NE
                    while n > 1:
                        n //= 2
                        do(pool.tensor_tensor(pos[:, :, 0:n], pos[:, :, 0:n], pos[:, :, n:2 * n], ALU.add))
                    do(pool.tensor_copy(idx[:, b, :], pos[:, :, 0:1].rearrange("p a b -> p (a b)")))
                    for k in range(2):
                        do(pool.tensor_copy(rec[:, b, k, 0:1], token[:, bass.ds(pl.n, 1)]))
                    do(pool.tensor_scalar(r4[:, b, 8:9], r4[:, b, 5:6], 1.0, None, ALU.add))
                    do(pool.tensor_tensor(r4[:, b, 8:9], r4[:, b, 8:9], r4[:, b, 4:5], ALU.mult))
                    do(pool.tensor_tensor(rec[:, b, 0, 1:2].bitcast(F32), r4[:, b, 8:9], powers[:, 0:1], ALU.pow))
                    pool.tensor_tensor(rec[:, b, 1, 1:2].bitcast(F32), rec[:, b, 0, 1:2].bitcast(F32), r4[:, b, 5:6],
                                       ALU.mult).then_inc(rec_ok, 1)
                    pool.wait_ge(rec_ok, pl.n + 1)
                    pool.sem_inc(passed_p, 1)
                    for k in range(2):
                        pool.indirect_dma_start(g.table[0:NE * CAP, :],
                                                bass.IndirectOffsetOnAxis(ap=idx[:, b, k:k + 1], axis=0),
                                                rec[:, b, k, :], None, bounds_check=NE * CAP - 1,
                                                oob_is_err=True).then_inc(sc[b], 16)
                if route:
                    rb_ = t.back(2)
                    b = rb_.par
                    pool.wait_ge(lgd, rb_.n + 1)
                    pool.sem_inc(passed_p, 1)
                    c = r4[:, b, :]
                    largest(c[:, 1:2], lg[:, b, 0:NG], NG)
                    do(pool.tensor_scalar(c[:, 0:1], c[:, 1:2], -1.0, None, ALU.mult))
                    one_hot(oh[:, 0, 0:NG], lg[:, b, 0:NG], c[:, 1:2], NG, c[:, 9:10])
                    do(pool.tensor_tensor(selg[:, :, :], lg[:, b, NG:].rearrange("p (a c) -> p a c", a=NG),
                                          oh[:, 0, 0:NG].unsqueeze(2).broadcast_to([P, NG, EPG]), ALU.mult))
                    do(pool.tensor_tensor(selg[:, 0:2, :], selg[:, 0:2, :], selg[:, 2:4, :], ALU.add))
                    do(pool.tensor_tensor(oh[:, 3, :], selg[:, 0, :], selg[:, 1, :], ALU.add))
                    largest(c[:, 1:2], oh[:, 3, :], EPG)
                    one_hot(oh[:, 1, :], oh[:, 3, :], c[:, 1:2], EPG, c[:, 9:10])
                    do(pool.tensor_scalar(oh[:, 2, :], oh[:, 1, :], -3e38, None, ALU.mult))
                    do(pool.tensor_tensor(oh[:, 3, :], oh[:, 2, :], oh[:, 3, :], ALU.add))
                    largest(c[:, 2:3], oh[:, 3, :], EPG)
                    one_hot(oh[:, 2, :], oh[:, 3, :], c[:, 2:3], EPG, c[:, 9:10])
                    do(pool.tensor_tensor(c[:, 3:4], c[:, 2:3], c[:, 1:2], ALU.subtract))
                    for k in range(2):
                        do(pool.tensor_tensor(pick[:, b, k, :].rearrange("p (a c) -> p a c", a=NG),
                                              oh[:, 0, 0:NG].unsqueeze(2).broadcast_to([P, NG, EPG]),
                                              oh[:, 1 + k, :].unsqueeze(1).broadcast_to([P, NG, EPG]), ALU.mult))
                    pool.tensor_tensor(pick[:, b, 2, :], pick[:, b, 0, :], pick[:, b, 1, :], ALU.add).then_inc(rt1, 1)
                if values:
                    pool.wait_ge(sqa, t.n + 1)
                    wait(pool, mxn, t.n)
                    pool.sem_inc(passed_p, 1)
                    do(pool.tensor_scalar(nw[:, 2, :], ms[:, t.par, :], 1.0 / HW, EPS, ALU.mult, ALU.add))
                    rsqrt(nw[:, 0, :], nw[:, 2, :], 2).then_inc(nwd, 1)
            pipeline(pool, step)
            for b in range(2):
                pool.wait_ge(sc[b], 32 * (NT // 2))

        @block.tensor
        def _(pe):
            pe.wait_ge(setup, 8)

            def step(t, scores, values, project, route, place):
                nx, pj, ro, pl = t.back(-1), t.back(1), t.back(2), t.back(3)

                def head(h):
                    if scores:
                        if h == 0:
                            pe.wait_ge(ld_q[nx.par], 16 * (nx.half + 1))
                        wait(pe, sm, 8 * nx.n + h)
                        q = qb[nx.par][:, h, :]
                        kv = h // 4
                        pe.matmul(S[:, 0, 0:C], q, g.kT[:, kv, 0:C], start=True, stop=True)
                        pe.matmul(S[:, 0, C:512], q, g.kT[:, kv, bass.ds(nx.n * P + C, 2 * P)], start=True, stop=True)
                        pe.matmul(S[:, 1, 0:P], q, g.kT[:, kv, bass.ds(nx.n * P + C + 2 * P, P)],
                                  start=True, stop=True).then_inc(qk, 1)
                    if values:
                        pe.wait_ge(ex, 8 * t.n + h + 1)
                        wait(pe, tc, 8 * t.n + h)
                        for a in range(5):
                            ins = pe.transpose(PT[:, a // 4, (a % 4) * P:(a % 4 + 1) * P],
                                               pr[t.par][:, h, a * P:(a + 1) * P], g.ident[:, :])
                        ins.then_inc(tp, 1)
                        if h > 0:
                            head_values(h - 1)

                def head_values(h):
                    kv = h // 4
                    pe.wait_ge(tc, 8 * t.n + h + 1)
                    if h == 0:
                        wait(pe, att, t.n)
                    for a in range(5):
                        v = g.v[:, a, kv * HD:(kv + 1) * HD] if a < 2 else \
                            g.v[:, bass.ds(t.n + a, 1), kv * HD:(kv + 1) * HD].rearrange("p a d -> p (a d)")
                        ins = pe.matmul(O[:, h, :], pt[:, h % 2, a * P:(a + 1) * P], v,
                                        start=(a == 0), stop=(a == 4), skip_group_check=True)
                    ins.then_inc(pv, 1)

                for h in range(5):
                    head(h)
                if route:
                    pe.wait_ge(xnd, ro.n + 1)
                    for k in range(KT):
                        ins = pe.transpose(M[:, k // 4, (k % 4) * P:(k % 4 + 1) * P],
                                           xn[ro.par][:, k * P:(k + 1) * P], g.ident[:, :])
                    ins.then_inc(t2, 1)
                if place:
                    pe.wait_ge(rt1, pl.n + 1)
                    pe.matmul(R[:, 64:64 + NE], upper[:, :], pick[:, pl.par, 2, :], start=True, stop=True)
                    pe.matmul(R[:, 128:128 + NE], ones[:, :], pick[:, pl.par, 2, :], start=True, stop=True).then_inc(px, 1)
                for h in range(5, 7):
                    head(h)
                if route:
                    pe.wait_ge(t2v, ro.n + 1)
                    pe.wait_ge(t2a, ro.n + 1)
                if project:
                    pe.wait_ge(mxn, pj.n + 1)
                    for k in range(KT):
                        ins = pe.transpose(M[:, k // 4, (k % 4) * P:(k % 4 + 1) * P],
                                           mixn[:, k // 4, (k % 4) * P:(k % 4 + 1) * P], g.ident[:, :])
                    ins.then_inc(t1, 1)
                if route:
                    if place:
                        pe.wait_ge(pxr, pl.n + 1)
                    for k in range(KT):
                        ins = pe.matmul(R[:, 0:NG + NE], h2T[:, k, :], rw[:, k, :], start=(k == 0), stop=(k == KT - 1))
                    ins.then_inc(rt, 1)
                head(7)
                if values:
                    head_values(7)
                if project and isinstance(t.n, int) and t.n == 1:
                    pe.wait_ge(ld_later, 16 * len(later))
                if project:
                    pe.wait_ge(t1v, pj.n + 1)
                    pe.wait_ge(t1a, pj.n + 1)
                    for half in range(2):
                        for k in range(KT):
                            ins = pe.matmul(M[:, half, :], mixT[:, k, :], wo[:, k, half * 512:(half + 1) * 512],
                                            start=(k == 0), stop=(k == KT - 1))
                        ins.then_inc(op, 1)
            pipeline(pe, step)

        @block.scalar
        def _(act):
            def step(t, scores, values, project, route, place):
                nx, pj, ro, pl = t.back(-1), t.back(1), t.back(2), t.back(3)

                def head(h):
                    if values:
                        act.wait_ge(tp, 8 * t.n + h + 1)
                        wait(act, pv, 8 * t.n + h - 1)
                        act.copy(pt[:, h % 2, 0:512], PT[:, 0, :])
                        act.copy(pt[:, h % 2, 512:KEYS], PT[:, 1, 0:P]).then_inc(tc, 1)
                    if scores:
                        act.wait_ge(nmx, 8 * nx.n + h + 1)
                        act.activation(pr[nx.par][:, h, :], pr[nx.par][:, h, :], ACT.Exp, bias=nm[:, nx.par, h:h + 1],
                                       scale=SCALE, accum_out=rsum[:, nx.par, h:h + 1]).then_inc(ex, 1)

                head(0)
                if route:
                    act.wait_ge(res, ro.n + 1)
                    wait(act, sqa, min(ro.n + 2, NT) if isinstance(ro.n, int) else ro.n + 2)
                    wait(act, xnd, ro.n)
                    act.activation(sqs[:, :], x2[ro.par][:, :], ACT.Square, accum_out=n2[:, 3:4]).then_inc(sq2, 1)
                head(1)
                head(2)
                if place:
                    act.wait_ge(rt1, pl.n + 1)
                    act.activation(gexp[:, pl.par, :], lg[:, pl.par, 0:NG], ACT.Exp, bias=r4[:, pl.par, 0:1],
                                   accum_out=r4[:, pl.par, 4:5])
                    act.activation(r4[:, pl.par, 5:6], r4[:, pl.par, 3:4], ACT.Exp).then_inc(gex, 1)
                head(3)
                head(4)
                if route:
                    act.wait_ge(t2, ro.n + 1)
                    wait(act, rt, ro.n)
                    for k in range(4, KT):
                        ins = act.activation(h2T[:, k, :], M[:, 1, (k % 4) * P:(k % 4 + 1) * P], ACT.Identity,
                                             bias=g.mods[:, 0, 24 + k:25 + k], scale=g.scale2[:, k:k + 1])
                    ins.then_inc(t2a, 1)
                head(5)
                head(6)
                if project:
                    act.wait_ge(t1, pj.n + 1)
                    wait(act, op, 2 * pj.n)
                    for k in range(4, KT):
                        ins = act.activation(mixT[:, k, :], M[:, 1, (k % 4) * P:(k % 4 + 1) * P], ACT.Copy,
                                             scale=g.cols[:, C_GN + k:C_GN + k + 1])
                    ins.then_inc(t1a, 1)
                head(7)
                if scores:
                    act.wait_ge(esn, nx.n + 1)
                    act.activation(esk[:, nx.par, :], esk[:, nx.par, :], ACT.Exp).then_inc(eso, 1)
                if values:
                    act.wait_ge(att, t.n + 1)
                    act.wait_ge(ld_h[t.par], 16 * (t.half + 1))
                    if route:
                        act.wait_ge(sq2, ro.n + 1)
                    act.activation(sqs[:, 0:HW], mix[t.par][:, 0, :], ACT.Square, accum_out=ms[:, t.par, 0:1])
                    act.activation(sqs[:, HW:], mix[t.par][:, 1, :], ACT.Square, accum_out=ms[:, t.par, 1:2]).then_inc(sqa, 1)
            pipeline(act, step)

        @block.vector
        def _(ve):
            ve.wait_ge(ld, 16 * len(tables))
            ve.memset(ones[:, :], 1.0).then_inc(setup, 1)
            for b in range(2):
                ve.memset(qb[b][HD:HD + 1, :, :], 1.0).then_inc(setup, 1)
            ve.tensor_scalar(nsink[:, :], sink[:, :], -1.0, None, ALU.mult).then_inc(setup, 1)
            ve.wait_ge(setup, 8)

            def do(ins):
                ins.then_inc(dve, 1)
                ve.wait_ge(dve, 1)
                ve.sem_clear(dve)

            def step(t, scores, values, project, route, place):
                nx, pj, ro, pl = t.back(-1), t.back(1), t.back(2), t.back(3)

                def head(h):
                    if scores:
                        ve.wait_ge(qk, 8 * nx.n + h + 1)
                        wait(ve, tp, 8 * (nx.n - 2) + h + 1)
                        ve.sem_inc(passed, 1)
                        ve.tensor_tensor_reduce(out=pr[nx.par][:, h, :], in0=S[:, :, :].rearrange("p a b -> p (a b)")[:, 0:KEYS],
                                                in1=mask[:, :], scale=1.0, scalar=-3e38, op0=ALU.add, op1=ALU.max,
                                                accum_out=mx[:, nx.par, h:h + 1]).then_inc(sm, 1)
                        ve.wait_ge(sm, 8 * nx.n + h + 1)
                        ve.tensor_scalar(nm[:, nx.par, h:h + 1], mx[:, nx.par, h:h + 1], -SCALE, nsink[:, h:h + 1],
                                         ALU.mult, ALU.min).then_inc(nmx, 1)

                def residual(tile, half):
                    cs = slice(half * 512, (half + 1) * 512)
                    ve.wait_ge(op, 2 * tile.n + half + 1)
                    do(ve.tensor_tensor(x2[tile.par][:, cs], M[:, half, :], g1[:, cs], ALU.mult))
                    return ve.tensor_tensor(x2[tile.par][:, cs], x2[tile.par][:, cs], xr[tile.par][:, cs], ALU.add)

                if values and isinstance(t.n, int) and t.n == 1:
                    ve.wait_ge(ld_later, 16 * len(later))
                head(0)
                if route:
                    residual(ro, 1).then_inc(res, 1)
                for h in range(1, 4):
                    head(h)
                if route:
                    ve.wait_ge(n2d, ro.n + 1)
                    ve.tensor_scalar(xn[ro.par][:, :], x2[ro.par][:, :], n2[:, 0:1], None, ALU.mult).then_inc(xnd, 1)
                head(4)
                if route:
                    ve.wait_ge(t2, ro.n + 1)
                    wait(ve, rt, ro.n)
                    for k in range(4):
                        ins = ve.tensor_scalar(h2T[:, k, :], M[:, 0, k * P:(k + 1) * P], g.scale2[:, k:k + 1],
                                               g.mods[:, 0, 24 + k:25 + k], ALU.mult, ALU.add)
                    ins.then_inc(t2v, 1)
                if place:
                    ve.wait_ge(px, pl.n + 1)
                    wait(ve, rec_ok, pl.n)
                    ve.tensor_copy(pxs[:, :, :], R[:, 64:192].rearrange("p (a b) -> p a b", a=2)[:, :, 0:NE]).then_inc(pxr, 1)
                head(5)
                head(6)
                if project:
                    ve.wait_ge(t1, pj.n + 1)
                    wait(ve, op, 2 * pj.n)
                    for k in range(4):
                        ins = ve.tensor_scalar(mixT[:, k, :], M[:, 0, k * P:(k + 1) * P],
                                               g.cols[:, C_GN + k:C_GN + k + 1], None, ALU.mult)
                    ins.then_inc(t1v, 1)
                if route:
                    ve.wait_ge(rt, ro.n + 1)
                    wait(ve, rec_ok, ro.n - 1)
                    ve.tensor_tensor(lg[:, ro.par, :], R[:, 0:NG + NE], rb[:, :], ALU.add).then_inc(lgd, 1)
                head(7)
                if scores:
                    wait(ve, att, nx.n - 1)
                    ve.wait_ge(nmx, 8 * nx.n + 8)
                    ve.tensor_tensor(esk[:, nx.par, :], sink[:, :], nm[:, nx.par, :], ALU.add).then_inc(esn, 1)
                if values:
                    ve.wait_ge(eso, t.n + 1)
                    ve.wait_ge(pv, 8 * t.n + 8)
                    wait(ve, mxn, t.n - 1)
                    do(ve.tensor_tensor(rsum[:, t.par, :], rsum[:, t.par, :], esk[:, t.par, :], ALU.add))
                    do(ve.reciprocal(rsum[:, t.par, :], rsum[:, t.par, :]))
                    ve.tensor_tensor(mix[t.par][:, 0, :].rearrange("p (h d) -> p h d", h=NH), O[:, :, :],
                                     rsum[:, t.par, :].unsqueeze(2).broadcast_to([P, NH, HD]), ALU.mult).then_inc(att, 1)
                if project:
                    ve.wait_ge(ld_x[pj.par], 16 * (pj.half + 1))
                    wait(ve, st_x[pj.par], 32 * pj.half)
                    do(residual(pj, 0))
                if values:
                    ve.wait_ge(nwd, t.n + 1)
                    wait(ve, t1, t.n)
                    ve.tensor_scalar(mixn[:, 0, :], mix[t.par][:, 0, :], nw[:, 0, 0:1], None, ALU.mult)
                    ve.tensor_scalar(mixn[:, 1, :], mix[t.par][:, 1, :], nw[:, 0, 1:2], None, ALU.mult).then_inc(mxn, 1)
            pipeline(ve, step)


def stage6(e, g):
    nc, i = e.nc, e.i
    FT = FH // P
    with e.stage() as st:
        w13 = [e.sb(st, f"w13_{b}", [P, 2, KT, FH]) for b in range(2)]
        w2 = [e.sb(st, f"w2_{b}", [P, FT, D]) for b in range(2)]
        g2 = e.sb(st, "g2row", [P, D])
        info = e.sb(st, "info", [P, 3, NE], I32)
        inf = e.sb(st, "inf", [P, 2, NE])
        rec = e.sb(st, "brec", [P, 2 * NE + T // P + 2, 2], I32)
        rows_in = e.sb(st, "rows_in", [P, 1], I32)
        rows_out = e.sb(st, "rows_out", [P, 1], I32)
        xg = e.sb(st, "xg", [P, D])
        xT = e.sb(st, "bxT", [P, KT, P])
        sg = e.sb(st, "sg", [P, 2, P])
        gT = e.sb(st, "gT", [P, FT, P])
        y = e.sb(st, "by", [P, D])
        tpp = e.ps(st, "btp", [P, 2, 4, P])
        hp = e.ps(st, "bh", [P, 2, 512])
        yp = e.ps(st, "byp", [P, 2, 512])
        cnt = e.sem("s6_counts_ready")
        ld = e.sem("s6_gate_row_loaded")
        ldw13 = [e.sem(f"s6_w13_loaded{b}") for b in range(2)]
        ldw2 = [e.sem(f"s6_w2_loaded{b}") for b in range(2)]
        rl = e.sem("s6_records_loaded")
        gat = e.sem("s6_rows_gathered")
        scat = e.sem("s6_rows_added")
        tt = e.sem("s6_rows_turned")
        gd = e.sem("s6_hidden_gated")
        ym = e.sem("s6_output_product")
        y_ok = e.sem("s6_output_ready")
        xc_v = e.sem("s6_turned_copied_v")
        xc_a = e.sem("s6_turned_copied_a")
        hm = e.sem("s6_hidden_product")
        sgd = e.sem("s6_silu")
        picked_in = e.sem("s6_rows_in_picked")
        picked_out = e.sem("s6_rows_out_picked")
        clean = e.sem("s6_buffers_cleared")
        blank = e.sem("s6_records_cleared")
        passed_a = e.sem("s6_waits_passed_by_scalar")
        passed = e.sem("s6_waits_passed")
        passed_t = e.sem("s6_waits_passed_by_tensor")
        cnt0 = e.sem("s6_counts_step")
        ahead = ((tt, 1), (gd, 2), (ym, 1))
        out_rows, xn_rows = e.out[0], g.xn_dram
        block = st.enter_context(nc.Block())

        def span(eng, ex):
            many = eng.value_load(info[0:1, 0, bass.ds(ex, 1)], min_val=1, max_val=T // P)
            base = eng.value_load(info[0:1, 1, bass.ds(ex, 1)], min_val=0, max_val=2 * NE)
            return many, base

        def blocks(eng, body, before=None, first=None):
            eng.wait_ge(cnt, 1)
            with eng.Fori(0, NE // 2) as pair:
                for par in range(2):
                    ex = 2 * pair + par
                    many, base = span(eng, ex)
                    if before is not None:
                        before(pair, par)
                    with eng.Fori(0, many) as b:
                        body(base + b, ex, b, par)

        @block.vector
        def _(ve):
            ve.memset(rec[:, :, :], NOWHERE).then_inc(blank, 1)
            ve.memset(xg[:, :], 0.0).then_inc(clean, 1)

            def do(ins):
                ins.then_inc(cnt0, 1)
                ve.wait_ge(cnt0, 1)
                ve.sem_clear(cnt0)
            do(ve.tensor_copy(info[:, 0, :], g.carry[:, :]))
            do(ve.tensor_scalar(info[:, 0, :], info[:, 0, :], P - 1, None, ALU.add))
            do(ve.tensor_scalar(info[:, 0, :], info[:, 0, :], P.bit_length() - 1, None, ALU.arith_shift_right))
            do(ve.tensor_scalar(info[:, 0, :], info[:, 0, :], 1, None, ALU.max))
            do(ve.tensor_copy(inf[:, 0, :], info[:, 0, :]))
            do(ve.memset(inf[:, 1, :], 0.0))
            do(ve.tensor_tensor_scan(inf[:, 1, :], inf[:, 0, :], inf[:, 1, :], 0.0, ALU.add, ALU.add))
            do(ve.tensor_copy(info[:, 2, :], inf[:, 1, :]))
            do(ve.tensor_tensor(inf[:, 1, :], inf[:, 1, :], inf[:, 0, :], ALU.subtract))
            ve.tensor_copy(info[:, 1, :], inf[:, 1, :]).then_inc(cnt, 1)
            ve.memset(y[:, :], 0.0).then_inc(y_ok, 1)
            for s, k in ahead:
                ve.sem_inc(s, k)
            ve.wait_ge(ld, 16)

            def turned(n):
                ve.wait_ge(tt, n + 2)
                for k in range(4):
                    ins = ve.tensor_scalar(xT[:, k, :], tpp[:, 0, k, :], g.scale2[:, k:k + 1],
                                           g.mods[:, 0, 24 + k:25 + k], ALU.mult, ALU.add)
                ins.then_inc(xc_v, 1)

            def body(n, ex, b, par):
                ve.wait_ge(ym, 2 * n + 1)
                for f in range(FT):
                    ve.wait_ge(sgd, 4 * n + f + 1)
                    ve.tensor_tensor(gT[:, f, :], sg[:, f % 2, :], hp[:, f % 2, P:2 * P], ALU.mult).then_inc(gd, 1)
                turned(n + 1)
                ve.wait_ge(scat, 16 * (n + 1))
                for half in range(2):
                    cs = slice(half * 512, (half + 1) * 512)
                    ve.wait_ge(ym, 2 * n + half + 2)
                    ins = ve.scalar_tensor_tensor(out=y[:, cs], in0=yp[:, half, :], scalar=rec[:, bass.ds(n + 1, 1), 1:2].rearrange("p a b -> p (a b)").bitcast(F32),
                                                  in1=g2[:, cs], op0=ALU.mult, op1=ALU.mult)
                ins.then_inc(y_ok, 1)
            turned(0)
            blocks(ve, body)

        @block.scalar
        def _(act):
            def turned(n):
                act.wait_ge(tt, n + 2)
                for k in range(4):
                    ins = act.activation(xT[:, 4 + k, :], tpp[:, 1, k, :], ACT.Identity,
                                         bias=g.mods[:, 0, 28 + k:29 + k], scale=g.scale2[:, 4 + k:5 + k])
                ins.then_inc(xc_a, 1)

            def body(n, ex, b, par):
                for f in range(FT):
                    act.wait_ge(hm, 4 * n + f + 1)
                    act.wait_ge(gd, 4 * n + f + 1)
                    act.activation(sg[:, f % 2, :], hp[:, f % 2, 0:P], ACT.Silu).then_inc(sgd, 1)
                turned(n + 1)

            def load(ex, par):
                for m, name in enumerate(("exp_w1", "exp_w3")):
                    act.dma_start(w13[par][:, m, :, :], i[name][0, bass.ds(ex, 1)].rearrange("a (k p) f -> p (a k) f", p=P))\
                       .then_inc(ldw13[par], 16)
                act.dma_start(w2[par][:, :, :], i["exp_w2"][0, bass.ds(ex, 1)].rearrange("a (k p) f -> p (a k) f", p=P))\
                   .then_inc(ldw2[par], 16)

            def expert(ex, par, more):
                many, base = span(act, ex)
                if more:
                    act.wait_ge(ym, 2 * base + 1)
                    act.sem_inc(passed_a, 1)
                    load(ex + 1, 1 - par)
                with act.Fori(0, many) as b:
                    body(base + b, ex, b, par)
            load(0, 0)
            load(1, 1)
            turned(0)
            act.wait_ge(cnt, 1)
            expert(0, 0, False)
            with act.Fori(0, NE // 2 - 1) as pair:
                expert(2 * pair + 1, 1, True)
                expert(2 * pair + 2, 0, True)
            expert(NE - 1, 1, False)

        @block.gpsimd
        def _(pool):
            pool.wait_ge(clean, 1)

            def gather(n):
                pool.wait_ge(rl, 16 * (n + 1))
                pool.wait_ge(tt, n + 1)
                pool.sem_inc(passed, 1)
                pool.tensor_copy(rows_in[:, :], rec[:, bass.ds(n + 1, 1), 0:1].rearrange("p a b -> p (a b)")).then_inc(picked_in, 1)
                pool.wait_ge(picked_in, n + 1)
                pool.sem_inc(passed, 1)
                pool.indirect_dma_start(xg[:, :], None, xn_rows, bass.IndirectOffsetOnAxis(ap=rows_in[:, :], axis=0),
                                        bounds_check=T - 1, oob_is_err=False).then_inc(gat, 16)

            def scatter(n):
                pool.wait_ge(y_ok, n + 1)
                pool.wait_ge(scat, 16 * n)
                pool.sem_inc(passed, 1)
                pool.tensor_copy(rows_out[:, :], rec[:, bass.ds(n, 1), 0:1].rearrange("p a b -> p (a b)")).then_inc(picked_out, 1)
                pool.wait_ge(picked_out, n + 1)
                pool.sem_inc(passed, 1)
                pool.indirect_dma_start(out_rows, bass.IndirectOffsetOnAxis(ap=rows_out[:, :], axis=0), y[:, :], None,
                                        bounds_check=T - 1, oob_is_err=False, compute_op=ALU.add).then_inc(scat, 16)

            gather(0)
            pool.wait_ge(cnt, 1)
            total = pool.value_load(info[0:1, 2, NE - 1:NE], min_val=1, max_val=2 * NE)
            with pool.Fori(0, total) as n:
                gather(n + 1)
                scatter(n)
            scatter(total)
            pool.wait_ge(scat, 16 * (total + 1))
            pool.wait_ge(gat, 16 * (total + 1))
            pool.sem_inc(passed, 1)

        @block.sync
        def _(sp):
            sp.dma_start(g2[:, :], g.gate_dram[D:2 * D].partition_broadcast(P)).then_inc(ld, 16)
            sp.wait_ge(blank, 1)

            def body(n, ex, b, par):
                sp.wait_ge(rl, 16 * n)
                sp.dma_start(rec[:, bass.ds(n + 1, 1), :], g.table[bass.ds(ex * CAP + b * P, P), :].unsqueeze(1)).then_inc(rl, 16)
            blocks(sp, body)
            total = sp.value_load(info[0:1, 2, NE - 1:NE], min_val=1, max_val=2 * NE)
            body(total, NE, 0, 0)

        @block.tensor
        def _(pe):
            def turn(n):
                pe.wait_ge(gat, 16 * (n + 1))
                for k in range(KT):
                    ins = pe.transpose(tpp[:, k // 4, k % 4, :], xg[:, k * P:(k + 1) * P], g.ident[:, :])
                ins.then_inc(tt, 1)

            def weights(pair, par):
                pe.wait_ge(ldw13[par], 32 * (pair + 1))
                pe.wait_ge(ldw2[par], 16 * (pair + 1))
                pe.sem_inc(passed_t, 1)

            def body(n, ex, b, par):
                pe.wait_ge(xc_v, n + 1)
                pe.wait_ge(xc_a, n + 1)
                for f in range(FT):
                    pe.wait_ge(gd, 4 * n + f + 1)
                    for m in range(2):
                        for k in range(KT):
                            ins = pe.matmul(hp[:, f % 2, m * P:(m + 1) * P], w13[par][:, m, k, f * P:(f + 1) * P],
                                            xT[:, k, :], start=(k == 0), stop=(k == KT - 1))
                    ins.then_inc(hm, 1)
                turn(n + 1)
                pe.wait_ge(gd, 4 * n + 6)
                pe.wait_ge(y_ok, n + 1)
                for half in range(2):
                    for f in range(FT):
                        ins = pe.matmul(yp[:, half, :], gT[:, f, :], w2[par][:, f, half * 512:(half + 1) * 512],
                                        start=(f == 0), stop=(f == FT - 1))
                    ins.then_inc(ym, 1)
            turn(0)
            blocks(pe, body, before=weights)


class Shared:
    pass


def program(nc, inputs, out, debug=False, stages=(1, 2, 3, 4, 5, 6)):
    with ExitStack() as stack:
        e = Env(nc, stack, inputs, debug)
        e.out = out
        g = Shared()
        g.cols = e.sb(stack, "cols", [P, P])
        g.mods = e.sb(stack, "mods", [P, 2, 48])
        g.scale1 = e.sb(stack, "scale1", [P, 2, KT])
        g.scale2 = e.sb(stack, "scale2", [P, KT])
        g.ident = e.sb(stack, "ident", [P, P])
        g.filt_dram = e.dram("filt", [2, NL, Q, 2, P, LANE])
        g.gate_dram = e.dram("gate", [2 * D])
        g.hy_dram = e.dram("hy_in", [3, T, HW])
        if 1 in stages:
            stage1(e, g)
        g.q_dram = e.dram("q", [NT + 1, HD, NH, P])
        g.kT = e.sb(stack, "kT", [HD + 1, NKV, C + T + 2 * P])
        g.v = e.sb(stack, "v", [P, NT + 4, NKV * HD])
        with ExitStack() as mid:
            g.hT = e.sb(mid, "hT", [P, KT, T])
            g.hcT = e.sb(mid, "hcT", [P, KT, C])
            if 2 in stages:
                stage2(e, g)
            if 3 in stages:
                stage3(e, g)
            if debug and max(stages)<=3:
                e.dump(g)
        g.hyo_dram = e.dram("hy_out", [T, HW])
        if 4 in stages:
            stage4(e, g)
        g.xn_dram = e.dram("xn", [T, D])
        g.table = e.dram("table", [NE * CAP + P, 2], I32)
        g.carry = e.sb(stack, "carry", [P, NE])
        if 5 in stages:
            stage5(e, g)
        if 6 in stages:
            stage6(e, g)
        if debug and max(stages) >= 4:
            e.dump(g)


INPUTS = ["x", "c", "ctx", "c_ctx", "ada_w", "ada_b", "norm1_w", "w_in", "q_norm_w", "k_norm_w", "attn_sink",
          "hy_conv_w", "hy_conv_b", "hy_w1", "hy_b1", "hy_w2", "hy_b2", "hy_w3", "hy_sin_freq", "hy_skip",
          "group_norm_w", "w_out", "norm2_w", "router_g_w", "router_g_b", "router_e_w", "router_e_b",
          "exp_w1", "exp_w3", "exp_w2"]


def kernel(**inputs):
    import concourse.bacc as bacc
    from concourse.bass_utils import run_bass_kernel_spmd

    nc = bacc.Bacc("TRN2", target_bir_lowering=False, num_devices=1)
    arrays, aps = {}, {}
    for name, a in [(n, inputs[n]) for n in INPUTS] + list(constants().items()):
        a = np.ascontiguousarray(a)
        arrays[f"in_{name}"] = a
        aps[name] = nc.dram_tensor(f"in_{name}", a.shape, mybir.dt.from_np(a.dtype), kind="ExternalInput").ap()
    out = nc.dram_tensor("out_0", (1, T, D), F32, kind="ExternalOutput").ap()
    program(nc, aps, out)
    r = run_bass_kernel_spmd(nc, [arrays], core_ids=[0])
    return r.results[0]["out_0"]
```

```python
from contextlib import ExitStack, contextmanager

import numpy as np

import concourse.bass as bass
from concourse import mybir

F32 = mybir.dt.float32
F32R = mybir.dt.float32r
I32 = mybir.dt.int32
U32 = mybir.dt.uint32
ALU = mybir.AluOpType
ACT = mybir.ActivationFunctionType
AX = mybir.AxisListType

P = 128
D = 1024
T = 2048
C = 256
KT = D // P
NT = T // P
HD = 64
NH, NKV = 8, 2
AW = 512
HW = 512
Q = 16
NE = 32
NG, EPG = 4, 8
FH = 512
EPS = 1e-6
SCALE = HD ** -0.5
NEG = -1e30
LANE = 128
NL = HW // LANE
NOWHERE = 4095
CAP = T

C_ADAB, C_N1, C_N2, C_GN, C_CW, C_CB, C_QN, C_KN, C_B1, C_B2, C_SF = 0, 48, 56, 64, 72, 108, 120, 121, 122, 123, 124


def constants():
    k = {}
    p = np.arange(P)[:, None, None]
    q = np.arange(Q)[None, :, None]
    k2 = np.arange(P)[None, None, :]
    th = 2 * np.pi * (((16 * p + q) * k2) % 4096) / 4096
    fre, fim = np.cos(th), -np.sin(th)
    fim[:, :, 0] = np.where(np.arange(P) % 2, -1.0, 1.0)[:, None]
    k["dft_fwd"] = np.concatenate([fre, fim], axis=2).reshape(P, Q * 256)
    ire = 2 / 4096 * np.cos(th).transpose(2, 1, 0)
    iim = -2 / 4096 * np.sin(th).transpose(2, 1, 0)
    ire[0] = 1 / 4096
    iim[0] = np.where(np.arange(P) % 2, -1.0, 1.0)[None, :] / 4096
    k["dft_inv"] = np.stack([ire, iim], axis=2).reshape(P, Q * 256)
    w = np.exp(-2j * np.pi * np.outer(np.arange(16), np.arange(16)) / 16)
    x = np.zeros((4, 16, 2, 4, 16, 2))
    for s in range(4):
        x[s, :, 0, s, :, 0] = w.real
        x[s, :, 0, s, :, 1] = w.imag
        x[s, :, 1, s, :, 0] = -w.imag
        x[s, :, 1, s, :, 1] = w.real
    xs = x.copy()
    xs[0, :, :, 0] = 0
    qq = np.arange(16)
    xs[0, :, 0, 0, 0, 0] = 1
    xs[0, :, 0, 0, 0, 1] = (-1.0) ** qq
    for k1 in range(1, 8):
        xs[0, :, 0, 0, k1, 0] = w[:, k1].real
        xs[0, :, 0, 0, k1, 1] = w[:, k1].imag
    for k1 in range(8):
        v = np.exp(-2j * np.pi * qq * (k1 + 0.5) / 16)
        xs[0, :, 1, 0, 8 + k1, 0] = v.real
        xs[0, :, 1, 0, 8 + k1, 1] = v.imag

    def spectra(m, special):
        h1, h2 = m.copy(), m.copy()
        h1[..., 1] = m[..., 0]
        h2[..., 0] = m[..., 1]
        h2[..., 1] = -m[..., 1]
        if special:
            h1[:, :, :, 0, 0, 1] = m[:, :, :, 0, 0, 1]
            h2[:, :, :, 0, 0, :] = 0
        return h1, h2

    inv = np.zeros((4, 16, 2, 4, 16, 2))
    wi = np.conj(w).T
    for s in range(4):
        inv[s, :, 0, s, :, 0] = wi.real
        inv[s, :, 0, s, :, 1] = wi.imag
        inv[s, :, 1, s, :, 0] = -wi.imag
        inv[s, :, 1, s, :, 1] = wi.real
    invs = inv.copy()
    invs[0, :, :, 0] = 0
    invs[0, 0, 0, 0, :, 0] = 1
    invs[0, 0, 1, 0, :, 0] = (-1.0) ** qq
    for k1 in range(1, 8):
        invs[0, k1, 0, 0, :, 0] = 2 * wi[k1].real
        invs[0, k1, 1, 0, :, 0] = -2 * wi[k1].imag
    for k1 in range(8):
        v = np.exp(2j * np.pi * qq * (k1 + 0.5) / 16)
        invs[0, 8 + k1, 0, 0, :, 1] = 2 * v.real
        invs[0, 8 + k1, 1, 0, :, 1] = -2 * v.imag
    mats = []
    for m, n, special in ((x, inv, False), (xs, invs, True)):
        h1, h2 = spectra(m, special)
        mats += [m, h1, h2, n, n[:, :, ::-1]]
    k["dft_mid"] = np.stack([m.reshape(P, P) for m in mats], axis=1).reshape(P, 10 * P)
    tf = (16 * np.arange(P)[None, :] + np.arange(Q)[:, None]).reshape(-1)
    pos = np.concatenate([tf, T - tf]).astype(np.float64)
    bands = np.linspace(1e-4, 15, 16).astype(np.float32).astype(np.float64)
    ang = 2 * np.pi / T * pos[None, :] * bands[:, None]
    k["feat"] = np.concatenate([pos[None] / T, np.cos(ang), -np.sin(ang)], axis=0)
    k["tneg"] = -(np.stack([tf.reshape(Q, P).T, (T - tf).reshape(Q, P).T], axis=1) / T).reshape(P, 2 * Q)
    deltas = np.abs(np.linspace(np.log(1e-2) / 1.5, np.log(1e-2) / 0.3, HW))
    k["deltas"] = np.broadcast_to(deltas[None], (P, HW))
    tok = np.arange(T)
    inv_freq = 10000.0 ** (-np.arange(16) / 16)
    a = np.concatenate([np.outer(inv_freq, tok // 64), np.outer(inv_freq, tok // 64),
                        np.outer(inv_freq, tok % 64), np.outer(inv_freq, tok % 64)])
    sign = np.where(np.arange(64) % 32 < 16, -1.0, 1.0)[:, None]
    k["rope_cos"] = np.concatenate([np.cos(a)] * 2)
    k["rope_sin"] = np.concatenate([np.sin(a) * sign] * 2)
    c = np.arange(P)
    k["head_ones"] = (c[:, None] // 64 == c[None, :] // 64) * 1.0
    k["pair_swap"] = (c[:, None] == (c[None, :] ^ 16)) * 1.0
    k["ident"] = np.eye(P)
    k["upper"] = (c[:, None] < c[None, :]) * 1.0
    qi, kj = np.arange(P)[:, None], np.arange(3 * P)[None, :] - P
    band = np.where(np.abs(kj - qi) <= P, 0.0, NEG)
    k["mask"] = np.concatenate([np.zeros((P, C)), band], axis=1)
    kb = np.zeros((1, NKV, C + T + 2 * P))
    kb[:, :, C:C + P] = NEG
    kb[:, :, C + P + T:] = NEG
    k["key_bias"] = kb.reshape(1, -1)
    k["rank8"] = np.broadcast_to(8.0 - np.arange(8)[None], (P, 8))
    k["slot0"] = np.broadcast_to(float(CAP) * np.arange(NE)[None], (P, NE))
    out = {n: np.ascontiguousarray(v, dtype=np.float32) for n, v in k.items()}
    out["token"] = (np.arange(P)[:, None] + P * np.arange(NT)[None]).astype(np.int32)
    return out


class Env:

    def __init__(self, nc, stack, inputs, debug=False):
        self.nc, self.stack, self.i, self.debug = nc, stack, inputs, debug
        self.sems = {}

    def sem(self, name):
        assert name not in self.sems
        self.sems[name] = self.nc.alloc_semaphore(name=name)
        return self.sems[name]

    def stage(self):
        @contextmanager
        def scope():
            with ExitStack() as st:
                yield st
            self.nc.clear_and_free_semaphores(list(self.sems.values()))
            self.nc.all_engine_barrier()
            self.sems = {}
        return scope()

    def sb(self, stack, name, shape, dt=F32):
        return stack.enter_context(self.nc.sbuf_tensor("sb_" + name, shape, dt))

    def ps(self, stack, name, shape, dt=F32):
        return stack.enter_context(self.nc.psum_tensor("ps_" + name, shape, dt))

    def dram(self, name, shape, dt=F32):
        kw = {"kind": "ExternalOutput"} if self.debug else {}
        return self.nc.dram_tensor("scr_" + name, shape, dt, **kw).ap()


class Chain:

    def __init__(self, eng, sem):
        self.eng, self.sem, self.n = eng, sem, 0

    def __call__(self, ins):
        ins.then_inc(self.sem, 1)
        self.n += 1
        return self.n

    def wait(self, n=None):
        self.eng.wait_ge(self.sem, self.n if n is None else n)


def stage1(e, g):
    nc = e.nc
    steps = [(o, q) for o in range(2) for q in range(Q)]
    TWO_PI_HI = float(np.float32(6.28125))
    TWO_PI_LO = float(np.float32(2 * np.pi - 6.28125))
    ROUND = 12582912.0
    with e.stage() as st:
        rows = e.sb(st, "rows", [P, P])
        crow = e.sb(st, "crow", [16, P])
        sil = e.sb(st, "sil", [P, KT, 32])
        mrow = e.sb(st, "mrow", [P, 3, 512])
        csb = e.sb(st, "csb", [P, 16])
        ada = e.sb(st, "ada", [P, 2, 3 * D])
        feat = e.sb(st, "feat", [33, 2 * T])
        w1 = e.sb(st, "fw1", [33, 64])
        w2 = e.sb(st, "fw2", [64, 64])
        w3 = e.sb(st, "fw3", [64, 4 * HW])
        hid = e.sb(st, "hid", [64, 2, 2 * T])
        ang = e.sb(st, "ang", [64, 4, 512])
        fwd = e.sb(st, "fwd1", [P, Q, 2, P])
        dl = e.sb(st, "dl", [P, HW])
        tneg = e.sb(st, "tneg", [P, 2, Q])
        dec = e.sb(st, "dec", [P, 2, Q, HW])
        fb = e.sb(st, "fb", [P, 2, HW])
        eo = e.sb(st, "eo", [P, 3, 2, HW])
        out = e.sb(st, "fout", [P, 4, HW])
        gr = e.sb(st, "gr", [16, P])
        gcol = e.sb(st, "gcol", [P, 16])
        gen = e.ps(st, "gen", [P, 4, 512])
        spec = e.ps(st, "spec", [P, 2, 512])
        modp = e.ps(st, "modp", [P, 512])
        misc = e.ps(st, "misc", [P, 512])

        ld_small = e.sem("s1_small_loaded")
        ld_dec = e.sem("s1_decay_loaded")
        ld_feat = e.sem("s1_feat_loaded")
        ld_filt = e.sem("s1_filter_tables_loaded")
        ld_ada = [e.sem(f"s1_ada_loaded{i}") for i in range(2)]
        rows_zero = e.sem("s1_rows_zeroed")
        turned = e.sem("s1_params_turned")
        cols_ok = e.sem("s1_cols_copied")
        sil_ok = e.sem("s1_silu_done")
        mlp_mm = e.sem("s1_mlp_product")
        mlp_arg = e.sem("s1_mlp_argument")
        mlp_sin = e.sem("s1_mlp_sine")
        dec_ok = e.sem("s1_decay_done")
        gen_mm = e.sem("s1_filter_generated")
        eo_ok = e.sem("s1_sum_difference")
        spec_mm = e.sem("s1_spectrum_product")
        spec_cp = e.sem("s1_spectrum_copied")
        stored = [e.sem(f"s1_spectrum_stored{i}") for i in range(4)]
        ada_mm = e.sem("s1_ada_product")
        mod_cp = e.sem("s1_modulation_copied")
        mod_t = e.sem("s1_modulation_turned")
        mod_rd = e.sem("s1_modulation_read")
        sil_z = e.sem("s1_silu_zeroed")
        dve = e.sem("s1_dve")
        g_cols = e.sem("s1_gate_cols")
        g_turn = e.sem("s1_gate_turned")
        g_copy = e.sem("s1_gate_copied")
        g_out = e.sem("s1_gate_stored")
        i = e.i
        small = [
            (rows[C_ADAB:C_ADAB + 48, :], i["ada_b"].rearrange("a (r p) -> (a r) p", p=P)),
            (rows[C_N1:C_N1 + 8, :], i["norm1_w"].rearrange("a (r p) -> (a r) p", p=P)),
            (rows[C_N2:C_N2 + 8, :], i["norm2_w"].rearrange("a (r p) -> (a r) p", p=P)),
            (rows[C_GN:C_GN + 8, :], i["group_norm_w"].rearrange("a (r p) -> (a r) p", p=P)),
            (rows[C_CW:C_CW + 36, :], i["hy_conv_w"].rearrange("a j (r p) -> (a j r) p", p=P)),
            (rows[C_CB:C_CB + 12, :], i["hy_conv_b"].rearrange("a (r p) -> (a r) p", p=P)),
            (rows[C_QN:C_QN + 1, 0:HD], i["q_norm_w"]), (rows[C_QN:C_QN + 1, HD:], i["q_norm_w"]),
            (rows[C_KN:C_KN + 1, 0:HD], i["k_norm_w"]), (rows[C_KN:C_KN + 1, HD:], i["k_norm_w"]),
            (rows[C_B1:C_B1 + 1, 0:64], i["hy_b1"]), (rows[C_B2:C_B2 + 1, 0:64], i["hy_b2"]),
            (rows[C_SF:C_SF + 2, 0:64], i["hy_sin_freq"].rearrange("a b c -> (a b) c")),
            (crow[0:8, :], i["c"].rearrange("a (r p) -> (a r) p", p=P)),
            (crow[8:16, :], i["c_ctx"].rearrange("(r p) -> r p", p=P)),
            (g.ident[:, :], i["ident"]),
        ]
        early = [
            (w1[:, :], i["hy_w1"][0]), (w2[:, :], i["hy_w2"][0]), (feat[:, :], i["feat"]),
        ]
        decay = [(dl[:, :], i["deltas"]), (tneg[:, :, :], i["tneg"].rearrange("p (d q) -> p d q", d=2))]
        tables = [
            (w3[:, :], i["hy_w3"][0]), (fwd[:, :, :, :], i["dft_fwd"].rearrange("p (q r k) -> p q r k", q=Q, r=2)),
        ]
        block = st.enter_context(nc.Block())

        @block.sync
        def _(sp):
            for dst, src in decay:
                sp.dma_start(dst, src).then_inc(ld_dec, 16)
            sp.wait_ge(rows_zero, 1)
            for dst, src in small:
                sp.dma_start(dst, src).then_inc(ld_small, 16)
            for dst, src in early:
                sp.dma_start(dst, src).then_inc(ld_feat, 16)
            for dst, src in tables:
                sp.dma_start(dst, src).then_inc(ld_filt, 16)
            for u in range(2 * KT):
                k, half = u // 2, u % 2
                if u >= 2:
                    sp.wait_ge(ada_mm, u - 1)
                sp.dma_start(ada[:, half, :], i["ada_w"][0, k * P:(k + 1) * P, half * 3 * D:(half + 1) * 3 * D])\
                    .then_inc(ld_ada[half], 16)

        @block.tensor
        def _(pe):
            pe.wait_ge(ld_small, 16 * len(small))
            pe.transpose(misc[:, 0:P], rows[:, :], g.ident[:, :]).then_inc(turned, 1)
            pe.transpose(misc[:, P:P + 16], crow[:, :], g.ident[0:16, 0:16]).then_inc(turned, 1)
            pe.wait_ge(ld_feat, 16 * len(early))
            def bank(b):
                return spec[:, b, :] if b < 2 else modp[:, :]

            def modulation(u):
                k, half = u // 2, u % 2
                if u == 0:
                    pe.wait_ge(sil_ok, 1)
                pe.wait_ge(ld_ada[half], 16 * (k + 1))
                for c in range(6):
                    at = 6 * half + c
                    mm = pe.matmul(bank(at // 4)[32 * (at % 4):32 * (at % 4) + 32, :], sil[:, k, :],
                                   ada[:, half, c * 512:(c + 1) * 512], start=(k == 0), stop=(k == KT - 1),
                                   skip_group_check=True)
                mm.then_inc(ada_mm, 1)

            for layer in range(2):
                for n in range(8):
                    at = 8 * layer + n
                    if at >= 4:
                        pe.wait_ge(mlp_arg, at - 3)
                    if layer == 1:
                        pe.wait_ge(mlp_sin, n + 1)
                    w, x = (w1[:, :], feat[:, n * 512:(n + 1) * 512]) if layer == 0 else \
                        (w2[:, :], hid[:, 0, n * 512:(n + 1) * 512])
                    pe.matmul(gen[0:64, at % 4, :], w, x, start=True, stop=True).then_inc(mlp_mm, 1)
                    if at % 2 == 1:
                        modulation(at - 1)
                        modulation(at)
            pe.wait_ge(mlp_sin, 16)

            def spectra(n):
                q = steps[n][1]
                pe.wait_ge(eo_ok, n + 1)
                for par in range(2):
                    if n >= 1:
                        pe.wait_ge(spec_cp, 2 * n + par - 1)
                    m = fwd[:, q, :, par::2]
                    pe.matmul(spec[:, par, :], m, eo[:, n % 3, par, :], start=True, stop=True).then_inc(spec_mm, 1)

            for n, (o, q) in enumerate(steps):
                if n >= 2:
                    pe.wait_ge(eo_ok, n - 1)
                elif n == 0:
                    pe.wait_ge(mlp_arg, 16)
                    pe.wait_ge(ld_filt, 16 * len(tables))
                for d in range(2):
                    pe.matmul(gen[:, 2 * (n % 2) + d, :], hid[:, 1, d * T + q * P:d * T + (q + 1) * P],
                              w3[:, (2 * o + d) * HW:(2 * o + d + 1) * HW], start=True, stop=True).then_inc(gen_mm, 1)
                if n == 2:
                    pe.wait_ge(mod_cp, 3)
                if n >= 2:
                    spectra(n - 2)
                if 3 <= n < 6:
                    pe.wait_ge(cols_ok, 2)
                    if n > 3:
                        pe.wait_ge(mod_rd, 2 * (n - 3))
                    for c in range(4):
                        mt = pe.transpose(misc[:, c * P:(c + 1) * P], mrow[:, n - 3, c * P:(c + 1) * P], g.ident[:, :])
                    mt.then_inc(mod_t, 1)
            spectra(len(steps) - 2)
            spectra(len(steps) - 1)
            pe.wait_ge(g_cols, 1)
            pe.transpose(misc[0:16, 256:256 + P], gcol[:, :], g.ident[:, :]).then_inc(g_turn, 1)

        @block.scalar
        def _(act):
            act.wait_ge(turned, 2)
            act.wait_ge(cols_ok, 2)
            act.wait_ge(sil_z, 1)
            act.activation(sil[:, :, 0:2].rearrange("p k a -> p a k"), csb[:, :].rearrange("p (a k) -> p a k", a=2),
                           ACT.Silu).then_inc(sil_ok, 1)
            act.wait_ge(ld_dec, 16 * len(decay))
            for d in range(2):
                for q in range(Q):
                    act.activation(dec[:, d, q, :], dl[:, :], ACT.Exp, scale=tneg[:, d, q:q + 1]).then_inc(dec_ok, 1)
            for n in range(16):
                act.wait_ge(mlp_arg, n + 1)
                act.activation(hid[:, n // 8, (n % 8) * 512:(n % 8 + 1) * 512], ang[:, n % 4, :], ACT.Sin)\
                    .then_inc(mlp_sin, 1)

            act.wait_ge(ada_mm, 2 * KT)
            for b in range(3):
                act.copy(mrow[:, b, :], spec[:, b, :] if b < 2 else modp[:, :]).then_inc(mod_cp, 1)

            def store(n):
                o, q = steps[n // 2]
                act.wait_ge(spec_cp, n + 1)
                for ri in range(2):
                    dst = g.filt_dram[o, :, q, ri].rearrange("l (j two) c -> two j l c", two=2)[n % 2]
                    act.dma_start(dst, out[64 * ri:64 * ri + 64, n % 4, :].rearrange("p (l c) -> p l c", c=LANE))\
                       .then_inc(stored[n % 4], 16)

            for n in range(2 * len(steps)):
                act.wait_ge(spec_mm, n + 1)
                if n >= 4:
                    act.wait_ge(stored[n % 4], 32 * (n // 4))
                act.copy(out[:, n % 4, :], spec[:, n % 2, :]).then_inc(spec_cp, 1)
                if n >= 1:
                    store(n - 1)
            store(2 * len(steps) - 1)
            act.wait_ge(g_turn, 1)
            act.copy(gr[:, :], misc[0:16, 256:256 + P]).then_inc(g_copy, 1)
            act.wait_ge(g_copy, 1)
            act.dma_start(g.gate_dram.rearrange("(r p) -> r p", p=P), gr[:, :]).then_inc(g_out, 16)
            act.wait_ge(g_out, 16)
            for b in range(4):
                act.wait_ge(stored[b], 32 * (2 * len(steps) // 4))

        @block.vector
        def _(ve):
            ch = Chain(ve, dve)
            ve.memset(rows[:, :], 0.0).then_inc(rows_zero, 1)
            ve.memset(sil[:, :, :], 0.0).then_inc(sil_z, 1)
            ve.wait_ge(turned, 2)
            ve.tensor_copy(g.cols[:, :], misc[:, 0:P]).then_inc(cols_ok, 1)
            ve.tensor_copy(csb[:, :], misc[:, P:P + 16]).then_inc(cols_ok, 1)
            ve.wait_ge(cols_ok, 2)
            tmp = eo
            for first in range(0, 16, 2):
                pair, layer = (first, first + 1), first // 8
                for n in pair:
                    ve.wait_ge(mlp_mm, n + 1)
                    ch(ve.tensor_scalar(tmp[0:64, n % 2, 0, :], gen[0:64, n % 4, :], g.cols[0:64, C_B1 + layer:C_B1 + layer + 1],
                                        g.cols[0:64, C_SF + layer:C_SF + layer + 1], ALU.add, ALU.mult))
                for n in pair:
                    ch.wait(ch.n - 1)
                    ch(ve.tensor_scalar(tmp[0:64, n % 2, 1, :], tmp[0:64, n % 2, 0, :], float(1 / (2 * np.pi)), ROUND, ALU.mult, ALU.add))
                for n in pair:
                    ch.wait(ch.n - 1)
                    ch(ve.tensor_scalar(tmp[0:64, n % 2, 1, :], tmp[0:64, n % 2, 1, :], ROUND, None, ALU.subtract))
                for n in pair:
                    ch.wait(ch.n - 1)
                    ch(ve.scalar_tensor_tensor(out=tmp[0:64, n % 2, 0, :], in0=tmp[0:64, n % 2, 1, :], scalar=-TWO_PI_HI,
                                               in1=tmp[0:64, n % 2, 0, :], op0=ALU.mult, op1=ALU.add))
                for n in pair:
                    if n >= 4:
                        ve.wait_ge(mlp_sin, n - 3)
                    ch.wait(ch.n - 1)
                    ch(ve.scalar_tensor_tensor(out=ang[:, n % 4, :], in0=tmp[0:64, n % 2, 1, :], scalar=-TWO_PI_LO,
                                               in1=tmp[0:64, n % 2, 0, :], op0=ALU.mult, op1=ALU.add))
                for n in pair:
                    ch.wait(ch.n - 1 + n % 2)
                    ve.tensor_scalar(ang[:, n % 4, :], ang[:, n % 4, :], 3.1415925, -3.1415925, ALU.min, ALU.max)\
                        .then_inc(mlp_arg, 1)
            ve.wait_ge(dec_ok, 2 * Q)
            ve.wait_ge(ld_small, 16 * len(small))
            ch(ve.memset(dec[0:1, 1, 0, :], 0.0))
            ch.wait()
            for n, (o, q) in enumerate(steps):
                ve.wait_ge(gen_mm, 2 * n + 2)
                if n >= 3:
                    ve.wait_ge(spec_mm, 2 * n - 4)
                for d in range(2):
                    ch(ve.tensor_tensor(fb[:, d, :], gen[:, 2 * (n % 2) + d, :], dec[:, d, q, :], ALU.mult))
                ch.wait()
                ch(ve.tensor_tensor(eo[:, n % 3, 0, :], fb[:, 0, :], fb[:, 1, :], ALU.add))
                ve.tensor_tensor(eo[:, n % 3, 1, :], fb[:, 0, :], fb[:, 1, :], ALU.subtract).then_inc(eo_ok, 1)
                ve.wait_ge(eo_ok, n + 1)
                ch.wait()
                if 3 <= n < 6:
                    ve.wait_ge(mod_t, n - 2)
                    b = n - 3
                    for a in range(2):
                        ve.tensor_tensor(g.mods[:, a, 16 * b:16 * b + 16].rearrange("p (j c) -> p c j", j=4),
                                         misc[:, :].rearrange("p (c j r) -> p c j r", c=4, j=4)[:, :, :, a],
                                         g.cols[:, C_ADAB + 16 * b:C_ADAB + 16 * b + 16].rearrange("p (j c) -> p c j", j=4),
                                         ALU.add).then_inc(mod_rd, 1)
                if n == 5:
                    ve.wait_ge(mod_rd, 6)
                    for a in range(2):
                        ch(ve.scalar_tensor_tensor(out=g.scale1[:, a, :], in0=g.mods[:, a, 8:16], scalar=1.0,
                                                   in1=g.cols[:, C_N1:C_N1 + 8], op0=ALU.add, op1=ALU.mult))
                    ch(ve.scalar_tensor_tensor(out=g.scale2[:, :], in0=g.mods[:, 0, 32:40], scalar=1.0,
                                               in1=g.cols[:, C_N2:C_N2 + 8], op0=ALU.add, op1=ALU.mult))
                    ch(ve.tensor_copy(gcol[:, 0:8], g.mods[:, 0, 16:24]))
                    ve.tensor_copy(gcol[:, 8:16], g.mods[:, 0, 40:48]).then_inc(g_cols, 1)
                    ve.wait_ge(g_cols, 1)
                    ch.wait()


def stage2(e, g):
    nc, i = e.nc, e.i
    with e.stage() as st:
        xr = e.sb(st, "xr", [P, 2, D])
        sq = e.sb(st, "sq", [P, D])
        ss = e.sb(st, "ss", [P, 2, 1])
        rs = e.sb(st, "rs", [P, 2, 1])
        xn = e.sb(st, "xn", [P, 2, D])
        tp = e.ps(st, "tp", [P, 2, KT, P])
        loaded = [e.sem(f"s2_rows_loaded{b}") for b in range(2)]
        summed = e.sem("s2_squares_summed")
        inv = e.sem("s2_variance_inverted")
        root = e.sem("s2_rstd")
        scaled = e.sem("s2_rows_scaled")
        turned = e.sem("s2_rows_turned")
        out_v = e.sem("s2_written_by_vector")
        out_a = e.sem("s2_written_by_scalar")
        dve = e.sem("s2_dve")
        NS = NT + 2
        block = st.enter_context(nc.Block())

        def tiles(eng, body):
            for n in range(2):
                body(n, n, n, g.hT, 0)
            with eng.Fori(1, NT // 2) as j:
                for b in range(2):
                    body(2 * j + b, 2 * j + b, b, g.hT, 0)
            for n in range(2):
                body(NT + n, n, n, g.hcT, 1)

        def write_last(write, n, at, b, s):
            if isinstance(n, int) and n == 0:
                return
            if s == 1 and at == 0:
                write(n - 1, NT - 1, 1 - b, g.hT, 0)
            else:
                write(n - 1, at - 1, 1 - b, g.hT if s == 0 else g.hcT, s)

        @block.sync
        def _(sp):
            def load(n, at, b, hT, s):
                if not (isinstance(n, int) and n < 2):
                    sp.wait_ge(scaled, n - 1)
                src = i["x"][0] if s == 0 else i["ctx"][0]
                sp.dma_start(xr[:, b, :], src[bass.ds(at * P, P), :]).then_inc(loaded[b], 16)
            tiles(sp, load)

        @block.scalar
        def _(act):
            def half(n, at, b, hT, s):
                act.wait_ge(turned, n + 1)
                for k in range(4, KT):
                    ins = act.activation(hT[:, k, bass.ds(at * P, P)], tp[:, b, k, :], ACT.Identity,
                                         bias=g.mods[:, s, k:k + 1], scale=g.scale1[:, s, k:k + 1])
                ins.then_inc(out_a, 1)

            def tile(n, at, b, hT, s):
                act.wait_ge(loaded[b], (n - b) * 8 + 16)
                if not (isinstance(n, int) and n == 0):
                    act.wait_ge(summed, n)
                if not (isinstance(n, int) and n < 2):
                    act.wait_ge(inv, n - 1)
                act.activation(sq[:, :], xr[:, b, :], ACT.Square, accum_out=ss[:, b, :]).then_inc(summed, 1)
                act.wait_ge(inv, n + 1)
                if not (isinstance(n, int) and n < 2):
                    act.wait_ge(scaled, n - 1)
                act.activation(rs[:, b, :], ss[:, b, :], ACT.Sqrt).then_inc(root, 1)
                write_last(half, n, at, b, s)
            tiles(act, tile)
            half(NS - 1, 1, 1, g.hcT, 1)

        @block.vector
        def _(ve):
            def tile(n, at, b, hT, s):
                ve.wait_ge(summed, n + 1)
                ve.tensor_scalar(ss[:, b, :], ss[:, b, :], 1.0 / D, EPS, ALU.mult, ALU.add).then_inc(dve, 1)
                ve.wait_ge(dve, n + 1)
                ve.reciprocal(ss[:, b, :], ss[:, b, :]).then_inc(inv, 1)
                ve.wait_ge(root, n + 1)
                if not (isinstance(n, int) and n < 2):
                    ve.wait_ge(turned, n - 1)
                ve.tensor_scalar(xn[:, b, :], xr[:, b, :], rs[:, b, :], None, ALU.mult).then_inc(scaled, 1)
                write_last(half, n, at, b, s)

            def half(n, at, b, hT, s):
                ve.wait_ge(turned, n + 1)
                for k in range(4):
                    ins = ve.tensor_scalar(hT[:, k, bass.ds(at * P, P)], tp[:, b, k, :], g.scale1[:, s, k:k + 1],
                                           g.mods[:, s, k:k + 1], ALU.mult, ALU.add)
                ins.then_inc(out_v, 1)
            tiles(ve, tile)
            half(NS - 1, 1, 1, g.hcT, 1)
            ve.wait_ge(out_a, NS)

        @block.tensor
        def _(pe):
            def turn(n, at, b, hT, s):
                pe.wait_ge(scaled, n + 1)
                if not (isinstance(n, int) and n < 2):
                    pe.wait_ge(out_v, n - 1)
                    pe.wait_ge(out_a, n - 1)
                for k in range(KT):
                    ins = pe.transpose(tp[:, b, k, :], xn[:, b, k * P:(k + 1) * P], g.ident[:, :])
                ins.then_inc(turned, 1)
            tiles(pe, turn)
            pe.wait_ge(out_v, NS)
            pe.wait_ge(out_a, NS)


def stage3(e, g):
    nc, i = e.nc, e.i
    PW = 256
    order = [2, 0, 1] + list(range(3, 9))
    CH = T // 512
    qk = [("k", 4, n) for n in range(CH)] + [("kc", 4, 0)] + [("q", ct, n) for ct in range(4) for n in range(CH)]
    hy = [(ct, n) for ct in range(12) for n in range(CH)]
    with e.stage() as st:
        w = e.sb(st, "win", [P, 3, KT, PW])
        cos = e.sb(st, "cos", [P, T])
        sin = e.sb(st, "sin", [P, T])
        ones = e.sb(st, "head_ones", [P, P])
        swap = e.sb(st, "pair_swap", [P, P])
        qw = e.sb(st, "qw", [P, 2, 512])
        sq = e.sb(st, "qsq", [P, 2, 512])
        rs = e.sb(st, "qrs", [P, 2, 512])
        rot = e.sb(st, "rot", [P, 2, 512])
        u = e.sb(st, "hu", [P, 2, T + 2])
        y = e.sb(st, "hyv", [P, 2, T])
        z = [m[:, :].rearrange("p (q c) -> p q c", q=Q) for m in (cos, sin)]
        mp = e.ps(st, "proj", [P, 4, 512])
        ap = e.ps(st, "paux", [P, 4, 512])
        ld = e.sem("s3_tables_loaded")
        ldw = [e.sem(f"s3_weights_loaded{b}") for b in range(3)]
        wdone = e.sem("s3_piece_used")
        mm = e.sem("s3_qk_product")
        w_qw = e.sem("s3_weighted")
        aux = e.sem("s3_norm_and_swap_product")
        inv = e.sem("s3_norm_inverted")
        root = e.sem("s3_rstd")
        auxr = e.sem("s3_swap_read")
        rotd = e.sem("s3_rotated")
        st_q = [e.sem(f"s3_stored{b}") for b in range(2)]
        v_mm = e.sem("s3_value_product")
        v_cp = e.sem("s3_value_copied")
        h_mm = e.sem("s3_hyena_product")
        h_cp = e.sem("s3_hyena_copied")
        conv = e.sem("s3_convolved")
        h_tr = e.sem("s3_hyena_turned")
        z_cp = e.sem("s3_hyena_turned_copied")
        st_z = [e.sem(f"s3_hyena_stored{b}") for b in range(2)]
        dve = e.sem("s3_dve")
        zeroed = e.sem("s3_zeroed")
        NV, NQ = NT + 2, len(qk)
        kpos = {"k": lambda n: C + P + 512 * n, "kc": lambda n: 0}
        block = st.enter_context(nc.Block())

        @block.sync
        def _(sp):
            for n, pc in enumerate(order):
                if n >= 3:
                    sp.wait_ge(wdone, n - 2)
                src = i["w_in"][0, :, pc * PW:(pc + 1) * PW].rearrange("(k p) c -> p k c", p=P)
                sp.dma_start(w[:, n % 3, :, :], src).then_inc(ldw[n % 3], 16)
                if n == 0:
                    for dst, src in ((ones, "head_ones"), (swap, "pair_swap"), (cos, "rope_cos"), (sin, "rope_sin")):
                        sp.dma_start(dst[:, :], i[src]).then_inc(ld, 16)
                    sp.dma_start(g.kT[HD:HD + 1, :, :].rearrange("p a t -> p (a t)"), i["key_bias"]).then_inc(ld, 16)

        @block.tensor
        def _(pe):
            def product(n, kind, ct, c):
                pc = order.index(ct // 2)
                pe.wait_ge(ldw[pc % 3], 16 * (pc // 3 + 1))
                if n >= 4:
                    pe.wait_ge(w_qw, n - 3)
                N = C if kind == "kc" else 512
                for k in range(KT):
                    rhs = g.hcT[:, k, :] if kind == "kc" else g.hT[:, k, c * 512:(c + 1) * 512]
                    ins = pe.matmul(mp[:, n % 4, 0:N], w[:, pc % 3, k, (ct % 2) * P:(ct % 2 + 1) * P], rhs,
                                    start=(k == 0), stop=(k == KT - 1))
                ins.then_inc(mm, 1)

            def norm(n, kind):
                N = C if kind == "kc" else 512
                pe.wait_ge(w_qw, n + 1)
                if n >= 2:
                    pe.wait_ge(auxr, n - 1)
                b = 2 * (n % 2)
                pe.matmul(ap[:, b, 0:N], ones[:, :], sq[:, n % 2, 0:N], start=True, stop=True)
                pe.matmul(ap[:, b + 1, 0:N], swap[:, :], qw[:, n % 2, 0:N], start=True, stop=True).then_inc(aux, 1)

            for n, (kind, ct, c) in enumerate(qk):
                product(n, kind, ct, c)
                if n == 1:
                    pe.wait_ge(ld, 16 * 5)
                if n >= 1:
                    norm(n - 1, qk[n - 1][0])
                if n == 4:
                    for t in range(NV):
                        if t >= 4:
                            pe.wait_ge(v_cp, t - 3)
                        else:
                            pe.wait_ge(w_qw, n + 1)
                        for k in range(KT):
                            x = g.hT[:, k, t * P:(t + 1) * P] if t < NT else g.hcT[:, k, (t - NT) * P:(t - NT + 1) * P]
                            ins = pe.matmul(mp[:, (t + 1) % 4, 0:P], x, w[:, 0, k, P:2 * P],
                                            start=(k == 0), stop=(k == KT - 1))
                        ins.then_inc(v_mm, 1)
                    pe.wait_ge(v_cp, NV)
                    pe.nop().then_inc(wdone, 1)
                if kind == "q" and ct % 2 == 1 and c == CH - 1:
                    pe.wait_ge(mm, n + 1)
                    pe.nop().then_inc(wdone, 1)
            def turn(ct):
                pe.wait_ge(conv, ct + 1)
                for b in range(4):
                    if ct >= 1:
                        pe.wait_ge(z_cp, 4 * ct + b - 3)
                    for a in range(4):
                        ins = pe.transpose(ap[:, b, a * P:(a + 1) * P], y[:, ct % 2, 4 * b + a::Q], g.ident[:, :])
                    ins.then_inc(h_tr, 1)

            for n, (ct, c) in enumerate(hy):
                pc = 3 + ct // 2
                pe.wait_ge(ldw[pc % 3], 16 * (pc // 3 + 1))
                if n >= 4:
                    pe.wait_ge(h_cp, n - 3)
                else:
                    pe.wait_ge(w_qw, NQ + n - 3)
                for k in range(KT):
                    ins = pe.matmul(mp[:, (NQ + n) % 4, :], w[:, pc % 3, k, (ct % 2) * P:(ct % 2 + 1) * P],
                                    g.hT[:, k, c * 512:(c + 1) * 512], start=(k == 0), stop=(k == KT - 1))
                ins.then_inc(h_mm, 1)
                if n == 0:
                    norm(NQ - 1, "q")
                    pe.wait_ge(auxr, NQ)
                if ct % 2 == 1 and c == CH - 1:
                    pe.wait_ge(h_mm, n + 1)
                    pe.nop().then_inc(wdone, 1)
                if ct >= 1 and c == 1:
                    turn(ct - 1)
            turn(11)

        @block.scalar
        def _(act):
            def weigh(n, kind, ct):
                N = C if kind == "kc" else 512
                col = C_QN if kind == "q" else C_KN
                act.wait_ge(mm, n + 1)
                if n >= 2:
                    act.wait_ge(aux, n - 1)
                    act.wait_ge(rotd, n - 1)
                act.activation(qw[:, n % 2, 0:N], mp[:, n % 4, 0:N], ACT.Identity, scale=g.cols[:, col:col + 1])
                act.activation(sq[:, n % 2, 0:N], mp[:, n % 4, 0:N], ACT.Square).then_inc(w_qw, 1)

            def rstd(n, kind):
                N = C if kind == "kc" else 512
                act.wait_ge(inv, n + 1)
                act.activation(rs[:, n % 2, 0:N], rs[:, n % 2, 0:N], ACT.Sqrt).then_inc(root, 1)

            for n, (kind, ct, c) in enumerate(qk):
                weigh(n, kind, ct)
                if n >= 1:
                    rstd(n - 1, qk[n - 1][0])
                if n == 4:
                    for t in range(NV):
                        act.wait_ge(v_mm, t + 1)
                        at = 3 + t if t < NT else t - NT
                        act.copy(g.v[:, at, :], mp[:, (t + 1) % 4, 0:P]).then_inc(v_cp, 1)
            rstd(len(qk) - 1, "q")
            act.wait_ge(zeroed, 5)

            def turned(ct):
                for b in range(4):
                    act.wait_ge(h_tr, 4 * ct + b + 1)
                    if ct >= 2 and b == 0:
                        act.wait_ge(st_z[ct % 2], 16 * (ct // 2))
                    if ct == 0 and b == 0:
                        act.wait_ge(rotd, NQ)
                    act.copy(z[ct % 2][:, 4 * b:4 * b + 4, :].rearrange("p q c -> p (q c)"), ap[:, b, :]).then_inc(z_cp, 1)
                act.wait_ge(z_cp, 4 * ct + 4)
                dst = g.hy_dram[ct // 4].rearrange("(p q) c -> p q c", q=Q)[:, :, (ct % 4) * P:(ct % 4 + 1) * P]
                act.dma_start(dst, z[ct % 2]).then_inc(st_z[ct % 2], 16)

            for n, (ct, c) in enumerate(hy):
                act.wait_ge(h_mm, n + 1)
                if ct >= 2 and c == 0:
                    act.wait_ge(conv, ct - 1)
                act.copy(u[:, ct % 2, 1 + c * 512:1 + (c + 1) * 512], mp[:, (NQ + n) % 4, :]).then_inc(h_cp, 1)
                if ct >= 1 and c == 2:
                    turned(ct - 1)
            turned(11)
            for b in range(2):
                act.wait_ge(st_z[b], 16 * 6)

        @block.vector
        def _(ve):
            ch = Chain(ve, dve)
            ve.memset(u[:, :, 0:1], 0.0).then_inc(zeroed, 1)
            ve.memset(u[:, :, T + 1:T + 2], 0.0).then_inc(zeroed, 1)
            ve.memset(g.v[:, 2:20:17, :], 0.0).then_inc(zeroed, 1)
            for n, (kind, ct, c) in enumerate(qk):
                N = C if kind == "kc" else 512
                b = n % 2
                ve.wait_ge(aux, n + 1)
                if n >= 2:
                    ve.wait_ge(st_q[b], 32 * (n // 2))
                ch(ve.tensor_scalar(rs[:, b, 0:N], ap[:, 2 * b, 0:N], 1.0 / HD, EPS, ALU.mult, ALU.add))
                ch.wait()
                ve.reciprocal(rs[:, b, 0:N], rs[:, b, 0:N]).then_inc(inv, 1)
                if kind == "kc":
                    ve.wait_ge(root, n + 1)
                    ve.tensor_tensor(rot[:, b, 0:N], qw[:, b, 0:N], rs[:, b, 0:N], ALU.mult).then_inc(rotd, 1)
                    ve.nop().then_inc(auxr, 1)
                    continue
                ch(ve.tensor_tensor(rot[:, b, :], ap[:, 2 * b + 1, :], sin[:, c * 512:(c + 1) * 512], ALU.mult))
                ch(ve.tensor_tensor(qw[:, b, :], qw[:, b, :], cos[:, c * 512:(c + 1) * 512], ALU.mult))
                ch.wait()
                ve.tensor_tensor(rot[:, b, :], rot[:, b, :], qw[:, b, :], ALU.add).then_inc(auxr, 1)
                ve.wait_ge(root, n + 1)
                ve.wait_ge(auxr, n + 1)
                ve.tensor_tensor(rot[:, b, :], rot[:, b, :], rs[:, b, :], ALU.mult).then_inc(rotd, 1)
            for ct in range(12):
                b = ct % 2
                ve.wait_ge(h_cp, 4 * ct + 4)
                if ct >= 2:
                    ve.wait_ge(h_tr, 4 * ct - 4)
                wc = [g.cols[:, C_CW + 12 * j + ct:C_CW + 12 * j + ct + 1] for j in range(3)]
                ch(ve.tensor_scalar(y[:, b, :], u[:, b, 1:T + 1], wc[1], g.cols[:, C_CB + ct:C_CB + ct + 1],
                                    ALU.mult, ALU.add))
                ch.wait()
                ch(ve.scalar_tensor_tensor(out=y[:, b, :], in0=u[:, b, 0:T], scalar=wc[0], in1=y[:, b, :],
                                           op0=ALU.mult, op1=ALU.add))
                ch.wait()
                ve.scalar_tensor_tensor(out=y[:, b, :], in0=u[:, b, 2:T + 2], scalar=wc[2], in1=y[:, b, :],
                                        op0=ALU.mult, op1=ALU.add).then_inc(conv, 1)

        @block.gpsimd
        def _(pool):
            pool.memset(g.kT[0:HD, :, C:C + P], 0.0).then_inc(zeroed, 1)
            pool.memset(g.kT[0:HD, :, C + P + T:], 0.0).then_inc(zeroed, 1)
            for n, (kind, ct, c) in enumerate(qk):
                N = C if kind == "kc" else 512
                pool.wait_ge(rotd, n + 1)
                for h in range(2):
                    src = rot[HD * h:HD * h + HD, n % 2, 0:N]
                    if kind == "q":
                        dst = g.q_dram[4 * c:4 * c + 4, :, 2 * ct + h, :].rearrange("b d t -> d b t")
                        src = src.rearrange("p (b t) -> p b t", t=P)
                    else:
                        dst = g.kT[0:HD, h, kpos[kind](c):kpos[kind](c) + N]
                    pool.dma_start(dst, src).then_inc(st_q[n % 2], 16)
            for b in range(2):
                pool.wait_ge(st_q[b], 32 * ((len(qk) - b + 1) // 2))
            pool.wait_ge(zeroed, 5)


def stage4(e, g):
    nc, i = e.nc, e.i
    LN = 2
    jobs = [(r, o, l) for r in range(NL // LN) for o in range(2) for l in range(LN)]
    NJ, NC = len(jobs), 8
    order = []
    for b in range(0, NJ, LN):
        order += [(s, b + l) for s in ("I", "II", "V") for l in range(LN)]
    uses, use_of = [], {}
    for s, j in order:
        for c in range({"I": 8, "II": NC, "V": 4}[s]):
            use_of[s, j, c] = len(uses)
            uses.append("v" if s == "V" else "a")
    nth = [sum(x == uses[n] for x in uses[:n + 1]) for n in range(len(uses))]
    with e.stage() as st:
        fwd = e.sb(st, "fwd4", [P, Q, 2, P])
        inv = e.sb(st, "inv4", [P, Q, 2, P])
        mid = e.sb(st, "mid4", [P, 10, P])
        skip = e.sb(st, "skip", [P, LN, LANE])
        zr = [e.sb(st, f"zr{l}", [P, Q, LANE]) for l in range(LN)]
        gt = [e.sb(st, f"gt{l}", [P, Q, LANE]) for l in range(LN)]
        sp_ = [e.sb(st, f"sp{l}", [P, Q, 2, LANE]) for l in range(LN)]
        yx = [e.sb(st, f"yx{l}", [P, 32, LANE]) for l in range(LN)]
        yh = [e.sb(st, f"yh{l}", [P, 32, LANE]) for l in range(LN)]
        ab = e.sb(st, "ab", [P, 2, 2, 512])
        prod = e.ps(st, "prod", [P, 2, 3, 512])
        ob = e.ps(st, "ob", [P, 2, 512])
        y_dram = e.dram("hy_y", [LN, Q, 2, P, LANE])
        v_dram = e.dram("hy_v", [LN, Q, 2, P, LANE])
        ld = e.sem("s4_tables_loaded")
        ld_mid = e.sem("s4_middle_tables_loaded")
        ld_inv = e.sem("s4_inverse_table_loaded")
        ld_z = [e.sem(f"s4_z_loaded{l}") for l in range(LN)]
        ld_g = [e.sem(f"s4_gate_loaded{l}") for l in range(LN)]
        ld_h = [e.sem(f"s4_filter_loaded{l}") for l in range(LN)]
        i_mm = e.sem("s4_I_product")
        i_cp = [e.sem(f"s4_I_copied{l}") for l in range(LN)]
        y_st = [e.sem(f"s4_Y_stored{l}") for l in range(LN)]
        y_ld = [e.sem(f"s4_Y_loaded{l}") for l in range(LN)]
        x_mm = e.sem("s4_spectra_product")
        x_cp = e.sem("s4_X_copied")
        ab_ok = e.sem("s4_spectra_multiplied")
        v_mm = e.sem("s4_II_inverse_product")
        v_cp = [e.sem(f"s4_II_inverse_copied{l}") for l in range(LN)]
        v_st = [e.sem(f"s4_V_stored{l}") for l in range(LN)]
        v_ld = [[e.sem(f"s4_V_loaded{l}_{c}") for c in range(4)] for l in range(LN)]
        o_mm = e.sem("s4_conv_product")
        o_rd = e.sem("s4_conv_read")
        z_ok = [e.sem(f"s4_z_ready{l}") for l in range(LN)]
        z_st = [e.sem(f"s4_z_stored{l}") for l in range(LN)]
        act_rd = e.sem("s4_bank_read_by_scalar")
        dve = e.sem("s4_dve")
        block = st.enter_context(nc.Block())

        def bank_free(pe, s, j, c):
            n = use_of[s, j, c]
            if n >= 2:
                pe.wait_ge(act_rd if uses[n - 2] == "a" else o_rd, nth[n - 2])
            return n % 2

        @block.sync
        def _(sp):
            def part0(j):
                r, o, l = jobs[j]
                ln = LN * r + l
                if o == 0:
                    if r >= 1:
                        sp.wait_ge(z_st[l], 16 * r)
                    src = g.hy_dram[0].rearrange("(p q) c -> p q c", q=Q)[:, :, ln * LANE:(ln + 1) * LANE]
                    sp.dma_start(zr[l][:, :, :], src).then_inc(ld_z[l], 16)

            def inputs(j):
                r, o, l = jobs[j]
                ln = LN * r + l
                k = j // LN
                if k >= 1:
                    sp.wait_ge(z_ok[l], 4 * k)
                src = g.hy_dram[o + 1].rearrange("(p q) c -> p q c", q=Q)[:, :, ln * LANE:(ln + 1) * LANE]
                sp.dma_start(gt[l][:, :, :], src).then_inc(ld_g[l], 16)
                src = i["hy_skip"][0, o, ln * LANE:(ln + 1) * LANE].partition_broadcast(P)
                sp.dma_start(skip[:, l, :], src).then_inc(ld_g[l], 16)

            def filt(j):
                r, o, l = jobs[j]
                if j >= LN:
                    sp.wait_ge(x_mm, NC * (j - LN + 1))
                for s in range(4):
                    src = g.filt_dram[o, LN * r + l].rearrange("q r (s g) c -> s (q r) (g c)", s=4)[s]
                    sp.dma_start(yh[l][32 * s:32 * s + 32, :, :].rearrange("p g c -> p (g c)"), src).then_inc(ld_h[l], 16)

            sp.dma_start(fwd[:, :, :, :], i["dft_fwd"].rearrange("p (q r k) -> p q r k", q=Q, r=2)).then_inc(ld, 16)
            for j in range(LN):
                part0(j)
            sp.dma_start(mid[:, :, :], i["dft_mid"].rearrange("p (m k) -> p m k", m=10)).then_inc(ld_mid, 16)
            filt(0)
            for s, j in order:
                r, o, l = jobs[j]
                k = j // LN
                if s == "I":
                    for c in range(4):
                        sp.wait_ge(i_cp[l], 8 * k + 2 * c + 2)
                        dst = y_dram[l, 4 * c:4 * c + 4].rearrange("q r k c -> k (q r) c")
                        sp.dma_start(dst, sp_[l][:, 4 * c:4 * c + 4, :, :].rearrange("p q r c -> p (q r) c"))\
                          .then_inc(y_st[l], 16)
                    sp.wait_ge(y_st[l], 64 * (k + 1))
                    if k >= 1:
                        sp.wait_ge(v_st[l], 128 * k)
                    for c in range(4):
                        src = y_dram[l].rearrange("q r (s g) c -> s (q r) (g c)", s=4)[c]
                        sp.dma_start(yx[l][32 * c:32 * c + 32, :, :].rearrange("p g c -> p (g c)"), src)\
                          .then_inc(y_ld[l], 16)
                if j == 0 and s == "I":
                    filt(1)
                if j == 1 and s == "I":
                    sp.dma_start(inv[:, :, :, :], i["dft_inv"].rearrange("p (q r k) -> p q r k", q=Q, r=2)).then_inc(ld_inv, 16)
                    for first in range(LN):
                        inputs(first)
                if s == "II":
                    for half in range(2):
                        sp.wait_ge(v_cp[l], NC * k + 4 * half + 4)
                        for c in range(4):
                            dst = v_dram[l].rearrange("q r (s g) c -> s (q r) g c", s=4)[c, :, 16 * half:16 * half + 16]
                            sp.dma_start(dst, yx[l][32 * c:32 * c + 32, 16 * half:16 * half + 16, :]).then_inc(v_st[l], 16)
                    sp.wait_ge(v_st[l], 128 * (k + 1))
                    for c in range(4):
                        src = v_dram[l, 4 * c:4 * c + 4].rearrange("q r k c -> k (q r) c")
                        sp.dma_start(sp_[l][:, 4 * c:4 * c + 4, :, :].rearrange("p q r c -> p (q r) c"), src)\
                          .then_inc(v_ld[l][c], 16)
                    if j + LN < NJ:
                        filt(j + LN)
                if s == "V":
                    if o == 1:
                        sp.wait_ge(z_ok[l], 4 * (k + 1))
                        dst = g.hyo_dram.rearrange("(p q) c -> p q c", q=Q)[:, :, (LN * r + l) * LANE:(LN * r + l + 1) * LANE]
                        sp.dma_start(dst, zr[l][:, :, :]).then_inc(z_st[l], 16)
                    if j + LN < NJ:
                        part0(j + LN)
                        inputs(j + LN)
            for l in range(LN):
                sp.wait_ge(z_st[l], 16 * (NL // LN))

        @block.tensor
        def _(pe):
            pe.wait_ge(ld, 16)
            for s, j in order:
                r, o, l = jobs[j]
                k = j // LN
                if s == "I":
                    if o == 0:
                        pe.wait_ge(ld_z[l], 16 * (r + 1))
                    else:
                        pe.wait_ge(z_ok[l], 4 * k)
                    for c in range(8):
                        b = bank_free(pe, s, j, c)
                        for a in range(4):
                            ins = pe.matmul(ob[:, b, a * LANE:(a + 1) * LANE], fwd[:, 2 * c + a // 2, a % 2, :],
                                            zr[l][:, 2 * c + a // 2, :], start=True, stop=True)
                        ins.then_inc(i_mm, 1)
                if s == "II":
                    if j == 0:
                        pe.wait_ge(ld_mid, 16)
                    pe.wait_ge(y_ld[l], 64 * (k + 1))
                    pe.wait_ge(ld_h[l], 64 * (k + 1))
                    for c in range(NC + 1):
                        if c < NC:
                            n = j * NC + c
                            if n >= 2:
                                pe.wait_ge(ab_ok, n - 1)
                            for m in range(3):
                                src = yx[l] if m == 0 else yh[l]
                                if c == 0:
                                    pe.matmul(prod[:, n % 2, m, 0:LANE], mid[:, 5 + m, :], src[:, 0, :],
                                              start=True, stop=True)
                                    ins = pe.matmul(prod[:, n % 2, m, LANE:512], mid[:, m, :],
                                                    src[:, 1:4, :].rearrange("p g c -> p (g c)"), start=True, stop=True)
                                else:
                                    ins = pe.matmul(prod[:, n % 2, m, :], mid[:, m, :],
                                                    src[:, 4 * c:4 * c + 4, :].rearrange("p g c -> p (g c)"),
                                                    start=True, stop=True)
                            ins.then_inc(x_mm, 1)
                        if c >= 1:
                            cc, n = c - 1, j * NC + c - 1
                            b = bank_free(pe, s, j, cc)
                            pe.wait_ge(ab_ok, n + 1)
                            if cc == 0:
                                for m in range(2):
                                    pe.matmul(ob[:, b, 0:LANE], mid[:, 8 + m, :], ab[:, n % 2, m, 0:LANE],
                                              start=(m == 0), stop=(m == 1))
                                for m in range(2):
                                    ins = pe.matmul(ob[:, b, LANE:512], mid[:, 3 + m, :], ab[:, n % 2, m, LANE:512],
                                                    start=(m == 0), stop=(m == 1))
                            else:
                                for m in range(2):
                                    ins = pe.matmul(ob[:, b, :], mid[:, 3 + m, :], ab[:, n % 2, m, :],
                                                    start=(m == 0), stop=(m == 1))
                            ins.then_inc(v_mm, 1)
                if s == "V":
                    if j == 0:
                        pe.wait_ge(ld_inv, 16)
                    for c in range(4):
                        pe.wait_ge(v_ld[l][c], 16 * (k + 1))
                        b = bank_free(pe, s, j, c)
                        for a in range(4):
                            for ri in range(2):
                                ins = pe.matmul(ob[:, b, a * LANE:(a + 1) * LANE], inv[:, 4 * c + a, ri, :],
                                                sp_[l][:, 4 * c + a, ri, :], start=(ri == 0), stop=(ri == 1))
                        ins.then_inc(o_mm, 1)

        @block.scalar
        def _(act):
            ni = nv = na = 0
            for s, j in order:
                r, o, l = jobs[j]
                k = j // LN
                if s == "I":
                    for c in range(8):
                        ni += 1
                        act.wait_ge(i_mm, ni)
                        if k >= 1 and c == 0:
                            act.wait_ge(o_mm, 4 * (j - LN + 1))
                        act.copy(sp_[l][:, 2 * c:2 * c + 2, :, :].rearrange("p q r c -> p (q r c)"),
                                 ob[:, use_of[s, j, c] % 2, :]).then_inc(act_rd, 1)
                        na += 1
                        act.wait_ge(act_rd, na)
                        act.nop().then_inc(i_cp[l], 1)
                if s == "II":
                    for c in range(NC + 1):
                        if c < NC:
                            n = j * NC + c
                            act.wait_ge(x_mm, n + 1)
                            if n >= 2:
                                act.wait_ge(ab_ok, n - 1)
                            if n >= 2:
                                act.wait_ge(v_mm, n - 1)
                            act.copy(ab[:, n % 2, 0, :], prod[:, n % 2, 0, :]).then_inc(x_cp, 1)
                        if c >= 1:
                            cc = c - 1
                            nv += 1
                            act.wait_ge(v_mm, nv)
                            act.copy(yx[l][:, 4 * cc:4 * cc + 4, :].rearrange("p g c -> p (g c)"),
                                     ob[:, use_of[s, j, cc] % 2, :]).then_inc(act_rd, 1)
                            na += 1
                            act.wait_ge(act_rd, na)
                            act.nop().then_inc(v_cp[l], 1)

        @block.vector
        def _(ve):
            ch = Chain(ve, dve)
            no = 0
            for s, j in order:
                r, o, l = jobs[j]
                k = j // LN
                if s == "II":
                    for c in range(NC):
                        n = j * NC + c
                        ve.wait_ge(x_cp, n + 1)
                        if n >= 2:
                            ve.wait_ge(v_mm, n - 1)
                        ch(ve.tensor_tensor(ab[:, n % 2, 1, :], ab[:, n % 2, 0, :], prod[:, n % 2, 2, :], ALU.mult))
                        ch.wait()
                        ve.tensor_tensor(ab[:, n % 2, 0, :], ab[:, n % 2, 0, :], prod[:, n % 2, 1, :], ALU.mult)\
                            .then_inc(ab_ok, 1)
                if s == "V":
                    sk = skip[:, l, :].unsqueeze(1).broadcast_to([P, 4, LANE])
                    ve.wait_ge(ld_g[l], 32 * (k + 1))
                    for c in range(4):
                        zc = zr[l][:, 4 * c:4 * c + 4, :]
                        ve.wait_ge(i_mm, 8 * (j + 1))
                        ch(ve.tensor_tensor(zc, zc, sk, ALU.mult))
                        ch.wait()
                        no += 1
                        ve.wait_ge(o_mm, no)
                        ve.tensor_tensor(zc, ob[:, use_of[s, j, c] % 2, :].rearrange("p (q c) -> p q c", q=4), zc, ALU.add)\
                            .then_inc(o_rd, 1)
                        ve.wait_ge(o_rd, no)
                        ve.tensor_tensor(zc, zc, gt[l][:, 4 * c:4 * c + 4, :], ALU.mult).then_inc(z_ok[l], 1)


class Tile:

    def __init__(self, half, off):
        self.half, self.par = half + off // 2, off % 2
        self.n = 2 * half + off

    def back(self, k):
        return Tile(self.half, self.par - k)


def wait(eng, sem, value):
    if not (isinstance(value, int) and value <= 0):
        eng.wait_ge(sem, value)


def pipeline(eng, step):
    step(Tile(0, -1), True, False, False, False, False)
    step(Tile(0, 0), True, True, False, False, False)
    step(Tile(0, 1), True, True, True, False, False)
    step(Tile(0, 2), True, True, True, True, False)
    with eng.Fori(1, NT // 2 - 1) as j:
        for off in (1, 2):
            step(Tile(j, off), True, True, True, True, True)
    step(Tile(0, NT - 1), False, True, True, True, True)
    step(Tile(0, NT), False, False, True, True, True)
    step(Tile(0, NT + 1), False, False, False, True, True)
    step(Tile(0, NT + 2), False, False, False, False, True)


def stage5(e, g):
    nc, i = e.nc, e.i
    KEYS = C + 3 * P
    with e.stage() as st:
        with nc.sbuf_tensor("sb_raw_wo", [P, KT, D], F32) as wo:
            pass
        wol = e.sb(st, "wol", [P, KT, D], F32R)
        woh = e.sb(st, "woh", [P, KT, D], F32R)
        rw = e.sb(st, "rw", [P, KT, NG + NE])
        rb = e.sb(st, "rb", [P, NG + NE])
        g1 = e.sb(st, "g1row", [P, D])
        mask = e.sb(st, "mask", [P, KEYS])
        nsink = e.sb(st, "nsink", [P, NH])
        sink = e.sb(st, "sink", [P, NH])
        upper = e.sb(st, "upper", [P, P])
        ones = e.sb(st, "ones", [P, 1])
        rank8 = e.sb(st, "rank8", [P, 8])
        slot0 = e.sb(st, "slot0", [P, NE])
        token = e.sb(st, "token", [P, NT], I32)
        qb = [e.sb(st, f"qb{b}", [HD + 1, NH, P]) for b in range(2)]
        pr = [e.sb(st, f"pr{b}", [P, NH, KEYS]) for b in range(2)]
        fill = pr[1][:, :, :].rearrange("p a b -> p (a b)")[:, 0:(NE * CAP + P) * 2 // P].bitcast(I32)
        mx = e.sb(st, "mx", [P, 2, NH])
        nm = e.sb(st, "nm", [P, 2, NH])
        rsum = e.sb(st, "rsum", [P, 2, NH])
        esk = e.sb(st, "esk", [P, 2, NH])
        pt = e.sb(st, "pt", [P, 2, KEYS])
        mix = [e.sb(st, f"mix{b}", [P, 2, HW]) for b in range(2)]
        ms = e.sb(st, "ms", [P, 2, 2])
        nw = e.sb(st, "nw", [P, 3, 2])
        n2 = e.sb(st, "n2", [P, 4])
        mixn = e.sb(st, "mixn", [P, 2, HW])
        mixh = e.sb(st, "mixh", [P, KT, P], F32R)
        mixl = e.sb(st, "mixl", [P, KT, P], F32R)
        xr = [e.sb(st, f"xres{b}", [P, D]) for b in range(2)]
        x2 = [e.sb(st, f"x2_{b}", [P, D]) for b in range(2)]
        xn = [e.sb(st, f"xn2_{b}", [P, D]) for b in range(2)]
        h2T = e.sb(st, "h2T", [P, KT, P])
        lg = e.sb(st, "lg", [P, 2, NG + NE])
        gexp = e.sb(st, "gexp", [P, 2, NG])
        r4 = e.sb(st, "r4", [P, 2, 16])
        oh = e.sb(st, "oh", [P, 4, 8])
        powers = e.sb(st, "powers", [P, 3])
        selg = e.sb(st, "selg", [P, NG, EPG])
        pick = e.sb(st, "pick", [P, 2, 3, NE])
        pos = e.sb(st, "pos", [P, 2, NE])
        pxs = e.sb(st, "pxs", [P, 2, NE])
        idx = e.sb(st, "idx", [P, 2, 2], I32)
        rec = e.sb(st, "rec", [P, 2, 2, 2], I32)
        S = e.ps(st, "S", [P, 2, 512])
        PT = e.ps(st, "PT", [P, 2, 512])
        O = e.ps(st, "O", [P, NH, HD])
        M = e.ps(st, "M", [P, 2, 512])
        R = e.ps(st, "R", [P, 512])

        ld = e.sem("s5_tables_loaded")
        ld_later = e.sem("s5_later_tables_loaded")
        wo_w = e.sem("s5_w_out_weighted")
        wo_hi = e.sem("s5_w_out_high")
        wo_lo = e.sem("s5_w_out_low")
        setup = e.sem("s5_set_up")
        filled = e.sem("s5_table_filled")
        ld_q = [e.sem(f"s5_queries_loaded{b}") for b in range(2)]
        ld_x = [e.sem(f"s5_rows_loaded{b}") for b in range(2)]
        qk = e.sem("s5_scores")
        sm = e.sem("s5_scores_masked")
        nmx = e.sem("s5_maximum")
        ex = e.sem("s5_exponentials")
        esn = e.sem("s5_sink_argument")
        eso = e.sem("s5_sink_exponential")
        tp = e.sem("s5_exponentials_turned")
        tc = e.sem("s5_turned_copied")
        pv = e.sem("s5_head_values")
        att = e.sem("s5_attention_scaled")
        sqa = e.sem("s5_mixer_squares")
        mxn = e.sem("s5_mixer_normalised")
        t1 = e.sem("s5_mixer_turned")
        t1v = e.sem("s5_mixer_turned_copied_v")
        t1a = e.sem("s5_mixer_turned_copied_a")
        op = e.sem("s5_projected")
        res = e.sem("s5_residual_added")
        sq2 = e.sem("s5_residual_squares")
        xnd = e.sem("s5_residual_normalised")
        t2 = e.sem("s5_residual_turned")
        t2v = e.sem("s5_residual_turned_copied_v")
        t2a = e.sem("s5_residual_turned_copied_a")
        rt = e.sem("s5_router_product")
        lgd = e.sem("s5_logits_copied")
        rt1 = e.sem("s5_experts_picked")
        gex = e.sem("s5_gate_exponentials")
        px = e.sem("s5_prefix_product")
        pxr = e.sem("s5_prefix_read")
        rec_ok = e.sem("s5_records_ready")
        sc = [e.sem(f"s5_records_scattered{b}") for b in range(2)]
        st_x = [e.sem(f"s5_rows_stored{b}") for b in range(2)]
        dve = e.sem("s5_dve")
        ps = e.sem("s5_pool")
        ld_h = [e.sem(f"s5_hyena_rows_loaded{b}") for b in range(2)]
        n2d = e.sem("s5_residual_variance_inverted")
        passed = e.sem("s5_waits_passed_v")
        passed_p = e.sem("s5_waits_passed_p")
        block = st.enter_context(nc.Block())

        tables = [(mask[:, :], i["mask"]), (sink[:, :], i["attn_sink"][0].partition_broadcast(P))]
        later = [
                  (upper[:, :], i["upper"]), (rank8[:, :], i["rank8"]), (slot0[:, :], i["slot0"]),
                  (token[:, :], i["token"]),
                  (rb[:, 0:NG], i["router_g_b"][0].partition_broadcast(P)),
                  (rb[:, NG:], i["router_e_b"][0].partition_broadcast(P)),
                  (rw[:, :, 0:NG], i["router_g_w"][0].rearrange("(k p) n -> p k n", p=P)),
                  (rw[:, :, NG:], i["router_e_w"][0].rearrange("(k p) n -> p k n", p=P)),
                  (g1[:, :], g.gate_dram[0:D].partition_broadcast(P)),
                  (wo[:, :, :], i["w_out"][0].rearrange("(k p) n -> p k n", p=P))]

        @block.sync
        def _(sp):
            for dst, src in tables:
                sp.dma_start(dst, src).then_inc(ld, 16)

            def step(t, scores, values, project, route, place):
                if scores:
                    b = t.back(-1)
                    wait(sp, qk, 8 * (b.n - 1))
                    sp.dma_start(qb[b.par][0:HD, :, :], g.q_dram[bass.ds(b.n, 1)].rearrange("a d h t -> (a d) h t"))\
                      .then_inc(ld_q[b.par], 16)
                    wait(sp, mxn, b.n - 1)
                    if isinstance(b.n, int) and b.n == 0:
                        for dst, src in later:
                            sp.dma_start(dst, src).then_inc(ld_later, 16)
                    sp.dma_start(mix[b.par][:, 1, :], g.hyo_dram[bass.ds(b.n * P, P), :]).then_inc(ld_h[b.par], 16)
                if values:
                    wait(sp, res, t.n - 1)
                    sp.dma_start(xr[t.par][:, :], i["x"][0, bass.ds(t.n * P, P), :]).then_inc(ld_x[t.par], 16)
                if route:
                    b = t.back(2)
                    sp.wait_ge(res, b.n + 1)
                    sp.dma_start(e.out[0, bass.ds(b.n * P, P), :], x2[b.par][:, :]).then_inc(st_x[b.par], 16)
                    sp.wait_ge(xnd, b.n + 1)
                    sp.dma_start(g.xn_dram[bass.ds(b.n * P, P), :], xn[b.par][:, :]).then_inc(st_x[b.par], 16)
            pipeline(sp, step)
            for b in range(2):
                sp.wait_ge(st_x[b], 32 * (NT // 2))

        @block.gpsimd
        def _(pool):
            carry = g.carry
            pool.memset(fill, NOWHERE).then_inc(setup, 1)
            pool.memset(carry[:, :], 0.0).then_inc(setup, 1)
            pool.memset(powers[:, 0:1], -1.0).then_inc(setup, 1)
            pool.memset(powers[:, 1:3], -0.5).then_inc(setup, 1)
            pool.wait_ge(setup, 8)
            pool.dma_start(g.table.rearrange("(p a) c -> p (a c)", p=P), fill).then_inc(filled, 16)
            pool.wait_ge(filled, 16)
            pool.wait_ge(ld_later, 16 * len(later))
            for k in range(KT):
                pool.tensor_scalar(wo[:, k, :], wo[:, k, :], g.cols[:, C_GN + k:C_GN + k + 1], None, ALU.mult)\
                    .then_inc(wo_w, 1)
            pool.wait_ge(wo_w, KT)
            for k in range(0, KT, 2):
                part = slice(k, k + 2)
                pool.tensor_copy(woh[:, part, :], wo[:, part, :]).then_inc(wo_hi, 1)
                pool.wait_ge(wo_hi, k // 2 + 1)
                pool.tensor_tensor(wol[:, part, :], wo[:, part, :], woh[:, part, :].bitcast(F32), ALU.subtract).then_inc(wo_lo, 1)

            def do(ins):
                ins.then_inc(ps, 1)
                pool.wait_ge(ps, 1)
                pool.sem_clear(ps)

            def rsqrt(y, v, n):
                return pool.tensor_tensor(y, v, powers[:, 1:1 + n], ALU.pow)

            def largest(out, x, n):
                do(pool.tensor_scalar(out, x[:, 0:1], x[:, 1:2], x[:, 2:3], ALU.max, ALU.max))
                for k in range(3, n - 1, 2):
                    do(pool.tensor_scalar(out, out, x[:, k:k + 1], x[:, k + 1:k + 2], ALU.max, ALU.max))
                do(pool.tensor_scalar(out, out, x[:, n - 1:n], None, ALU.max))

            def one_hot(out, x, m, n, col):
                do(pool.tensor_scalar(out, x, m, None, ALU.is_equal))
                do(pool.tensor_tensor(out, out, rank8[:, 0:n], ALU.mult))
                largest(col, out, n)
                do(pool.tensor_scalar(out, out, col, None, ALU.is_equal))

            def step(t, scores, values, project, route, place):
                if route:
                    b = t.back(2)
                    pool.wait_ge(sq2, b.n + 1)
                    pool.sem_inc(passed_p, 1)
                    do(pool.tensor_scalar(n2[:, 2:3], n2[:, 3:4], 1.0 / D, EPS, ALU.mult, ALU.add))
                    rsqrt(n2[:, 0:1], n2[:, 2:3], 1).then_inc(n2d, 1)
                if place:
                    pl = t.back(3)
                    b = pl.par
                    pool.wait_ge(pxr, pl.n + 1)
                    wait(pool, sc[b], 32 * pl.half)
                    pool.wait_ge(gex, pl.n + 1)
                    pool.sem_inc(passed_p, 1)
                    do(pool.tensor_tensor(pxs[:, 0, :], pxs[:, 0, :], carry[:, :], ALU.add))
                    do(pool.tensor_tensor(carry[:, :], pxs[:, 1, :], carry[:, :], ALU.add))
                    do(pool.tensor_tensor(pxs[:, 0, :], pxs[:, 0, :], slot0[:, :], ALU.add))
                    do(pool.tensor_tensor(pos[:, :, :], pick[:, b, 0:2, :],
                                          pxs[:, 0:1, :].broadcast_to([P, 2, NE]), ALU.mult))
                    n = NE
                    while n > 1:
                        n //= 2
                        do(pool.tensor_tensor(pos[:, :, 0:n], pos[:, :, 0:n], pos[:, :, n:2 * n], ALU.add))
                    do(pool.tensor_copy(idx[:, b, :], pos[:, :, 0:1].rearrange("p a b -> p (a b)")))
                    for k in range(2):
                        do(pool.tensor_copy(rec[:, b, k, 0:1], token[:, bass.ds(pl.n, 1)]))
                    do(pool.tensor_scalar(r4[:, b, 8:9], r4[:, b, 5:6], 1.0, None, ALU.add))
                    do(pool.tensor_tensor(r4[:, b, 8:9], r4[:, b, 8:9], r4[:, b, 4:5], ALU.mult))
                    do(pool.tensor_tensor(rec[:, b, 0, 1:2].bitcast(F32), r4[:, b, 8:9], powers[:, 0:1], ALU.pow))
                    pool.tensor_tensor(rec[:, b, 1, 1:2].bitcast(F32), rec[:, b, 0, 1:2].bitcast(F32), r4[:, b, 5:6],
                                       ALU.mult).then_inc(rec_ok, 1)
                    pool.wait_ge(rec_ok, pl.n + 1)
                    pool.sem_inc(passed_p, 1)
                    for k in range(2):
                        pool.indirect_dma_start(g.table[0:NE * CAP, :],
                                                bass.IndirectOffsetOnAxis(ap=idx[:, b, k:k + 1], axis=0),
                                                rec[:, b, k, :], None, bounds_check=NE * CAP - 1,
                                                oob_is_err=True).then_inc(sc[b], 16)
                if route:
                    rb_ = t.back(2)
                    b = rb_.par
                    pool.wait_ge(lgd, rb_.n + 1)
                    pool.sem_inc(passed_p, 1)
                    c = r4[:, b, :]
                    largest(c[:, 1:2], lg[:, b, 0:NG], NG)
                    do(pool.tensor_scalar(c[:, 0:1], c[:, 1:2], -1.0, None, ALU.mult))
                    one_hot(oh[:, 0, 0:NG], lg[:, b, 0:NG], c[:, 1:2], NG, c[:, 9:10])
                    do(pool.tensor_tensor(selg[:, :, :], lg[:, b, NG:].rearrange("p (a c) -> p a c", a=NG),
                                          oh[:, 0, 0:NG].unsqueeze(2).broadcast_to([P, NG, EPG]), ALU.mult))
                    do(pool.tensor_tensor(selg[:, 0:2, :], selg[:, 0:2, :], selg[:, 2:4, :], ALU.add))
                    do(pool.tensor_tensor(oh[:, 3, :], selg[:, 0, :], selg[:, 1, :], ALU.add))
                    largest(c[:, 1:2], oh[:, 3, :], EPG)
                    one_hot(oh[:, 1, :], oh[:, 3, :], c[:, 1:2], EPG, c[:, 9:10])
                    do(pool.tensor_scalar(oh[:, 2, :], oh[:, 1, :], -3e38, None, ALU.mult))
                    do(pool.tensor_tensor(oh[:, 3, :], oh[:, 2, :], oh[:, 3, :], ALU.add))
                    largest(c[:, 2:3], oh[:, 3, :], EPG)
                    one_hot(oh[:, 2, :], oh[:, 3, :], c[:, 2:3], EPG, c[:, 9:10])
                    do(pool.tensor_tensor(c[:, 3:4], c[:, 2:3], c[:, 1:2], ALU.subtract))
                    for k in range(2):
                        do(pool.tensor_tensor(pick[:, b, k, :].rearrange("p (a c) -> p a c", a=NG),
                                              oh[:, 0, 0:NG].unsqueeze(2).broadcast_to([P, NG, EPG]),
                                              oh[:, 1 + k, :].unsqueeze(1).broadcast_to([P, NG, EPG]), ALU.mult))
                    pool.tensor_tensor(pick[:, b, 2, :], pick[:, b, 0, :], pick[:, b, 1, :], ALU.add).then_inc(rt1, 1)
            pipeline(pool, step)
            for b in range(2):
                pool.wait_ge(sc[b], 32 * (NT // 2))

        @block.tensor
        def _(pe):
            pe.wait_ge(setup, 8)

            def step(t, scores, values, project, route, place):
                nx, pj, ro, pl = t.back(-1), t.back(1), t.back(2), t.back(3)

                def head(h):
                    if scores:
                        if h == 0:
                            pe.wait_ge(ld_q[nx.par], 16 * (nx.half + 1))
                        wait(pe, sm, 8 * nx.n + h)
                        q = qb[nx.par][:, h, :]
                        kv = h // 4
                        pe.matmul(S[:, 0, 0:C], q, g.kT[:, kv, 0:C], start=True, stop=True)
                        pe.matmul(S[:, 0, C:512], q, g.kT[:, kv, bass.ds(nx.n * P + C, 2 * P)], start=True, stop=True)
                        pe.matmul(S[:, 1, 0:P], q, g.kT[:, kv, bass.ds(nx.n * P + C + 2 * P, P)],
                                  start=True, stop=True).then_inc(qk, 1)
                    if values:
                        pe.wait_ge(ex, 8 * t.n + h + 1)
                        wait(pe, tc, 8 * t.n + h)
                        for a in range(5):
                            ins = pe.transpose(PT[:, a // 4, (a % 4) * P:(a % 4 + 1) * P],
                                               pr[t.par][:, h, a * P:(a + 1) * P], g.ident[:, :])
                        ins.then_inc(tp, 1)
                        if h > 0:
                            head_values(h - 1)

                def head_values(h):
                    kv = h // 4
                    pe.wait_ge(tc, 8 * t.n + h + 1)
                    if h == 0:
                        wait(pe, att, t.n)
                    for a in range(5):
                        v = g.v[:, a, kv * HD:(kv + 1) * HD] if a < 2 else \
                            g.v[:, bass.ds(t.n + a, 1), kv * HD:(kv + 1) * HD].rearrange("p a d -> p (a d)")
                        ins = pe.matmul(O[:, h, :], pt[:, h % 2, a * P:(a + 1) * P], v,
                                        start=(a == 0), stop=(a == 4), skip_group_check=True)
                    ins.then_inc(pv, 1)

                for h in range(5):
                    head(h)
                if route:
                    pe.wait_ge(xnd, ro.n + 1)
                    for k in range(KT):
                        ins = pe.transpose(M[:, k // 4, (k % 4) * P:(k % 4 + 1) * P],
                                           xn[ro.par][:, k * P:(k + 1) * P], g.ident[:, :])
                    ins.then_inc(t2, 1)
                if place:
                    pe.wait_ge(rt1, pl.n + 1)
                    pe.matmul(R[:, 64:64 + NE], upper[:, :], pick[:, pl.par, 2, :], start=True, stop=True)
                    pe.matmul(R[:, 128:128 + NE], ones[:, :].broadcast_to([P, P]), pick[:, pl.par, 2, :], start=True, stop=True).then_inc(px, 1)
                for h in range(5, 7):
                    head(h)
                if route:
                    pe.wait_ge(t2v, ro.n + 1)
                    pe.wait_ge(t2a, ro.n + 1)
                if project:
                    pe.wait_ge(mxn, pj.n + 1)
                    for k in range(KT):
                        ins = pe.transpose(M[:, k // 4, (k % 4) * P:(k % 4 + 1) * P],
                                           mixn[:, k // 4, (k % 4) * P:(k % 4 + 1) * P], g.ident[:, :])
                    ins.then_inc(t1, 1)
                if route:
                    if place:
                        pe.wait_ge(pxr, pl.n + 1)
                    for k in range(KT):
                        ins = pe.matmul(R[:, 0:NG + NE], h2T[:, k, :], rw[:, k, :], start=(k == 0), stop=(k == KT - 1))
                    ins.then_inc(rt, 1)
                head(7)
                if values:
                    head_values(7)
                if project and isinstance(t.n, int) and t.n == 1:
                    pe.wait_ge(ld_later, 16 * len(later))
                    pe.wait_ge(wo_lo, KT // 2)
                if project:
                    pe.wait_ge(t1v, pj.n + 1)
                    for half in range(2):
                        cs = slice(half * 512, (half + 1) * 512)
                        for k in range(KT):
                            pe.matmul(M[:, half, :], mixh[:, k, :], woh[:, k, cs], start=(k == 0), stop=False)
                            pe.matmul(M[:, half, :], mixh[:, k, :], wol[:, k, cs], start=False, stop=False)
                            ins = pe.matmul(M[:, half, :], mixl[:, k, :], woh[:, k, cs], start=False, stop=(k == KT - 1))
                        ins.then_inc(op, 1)
            pipeline(pe, step)

        @block.scalar
        def _(act):
            def step(t, scores, values, project, route, place):
                nx, pj, ro, pl = t.back(-1), t.back(1), t.back(2), t.back(3)

                def head(h):
                    if values:
                        act.wait_ge(tp, 8 * t.n + h + 1)
                        wait(act, pv, 8 * t.n + h - 1)
                        act.copy(pt[:, h % 2, 0:512], PT[:, 0, :])
                        act.copy(pt[:, h % 2, 512:KEYS], PT[:, 1, 0:P]).then_inc(tc, 1)
                    if scores:
                        act.wait_ge(nmx, 8 * nx.n + h + 1)
                        act.activation(pr[nx.par][:, h, :], pr[nx.par][:, h, :], ACT.Exp, bias=nm[:, nx.par, h:h + 1],
                                       scale=SCALE, accum_out=rsum[:, nx.par, h:h + 1]).then_inc(ex, 1)

                head(0)
                if route:
                    act.wait_ge(res, ro.n + 1)
                    wait(act, sqa, min(ro.n + 2, NT) if isinstance(ro.n, int) else ro.n + 2)
                    wait(act, xnd, ro.n)
                    act.activation(xn[ro.par][:, :], x2[ro.par][:, :], ACT.Square, accum_out=n2[:, 3:4]).then_inc(sq2, 1)
                head(1)
                head(2)
                if place:
                    act.wait_ge(rt1, pl.n + 1)
                    act.activation(gexp[:, pl.par, :], lg[:, pl.par, 0:NG], ACT.Exp, bias=r4[:, pl.par, 0:1],
                                   accum_out=r4[:, pl.par, 4:5])
                    act.activation(r4[:, pl.par, 5:6], r4[:, pl.par, 3:4], ACT.Exp).then_inc(gex, 1)
                head(3)
                head(4)
                if route:
                    act.wait_ge(t2, ro.n + 1)
                    wait(act, rt, ro.n)
                    for k in range(4, KT):
                        ins = act.activation(h2T[:, k, :], M[:, 1, (k % 4) * P:(k % 4 + 1) * P], ACT.Identity,
                                             bias=g.mods[:, 0, 24 + k:25 + k], scale=g.scale2[:, k:k + 1])
                    ins.then_inc(t2a, 1)
                head(5)
                head(6)
                if project:
                    act.wait_ge(t1, pj.n + 1)
                    wait(act, op, 2 * pj.n)
                    act.copy(mixh[:, :, :].rearrange("p k t -> p (k t)"), M[:, :, :].rearrange("p a b -> p (a b)")).then_inc(t1a, 1)
                head(7)
                if scores:
                    act.wait_ge(esn, nx.n + 1)
                    act.activation(esk[:, nx.par, :], esk[:, nx.par, :], ACT.Exp).then_inc(eso, 1)
                if values:
                    act.wait_ge(att, t.n + 1)
                    act.wait_ge(ld_h[t.par], 16 * (t.half + 1))
                    if route:
                        act.wait_ge(sq2, ro.n + 1)
                    act.activation(mixn[:, 0, :], mix[t.par][:, 0, :], ACT.Square, accum_out=ms[:, t.par, 0:1])
                    act.activation(mixn[:, 1, :], mix[t.par][:, 1, :], ACT.Square, accum_out=ms[:, t.par, 1:2]).then_inc(sqa, 1)
            pipeline(act, step)

        @block.vector
        def _(ve):
            ve.wait_ge(ld, 16 * len(tables))
            ve.memset(ones[:, :], 1.0).then_inc(setup, 1)
            for b in range(2):
                ve.memset(qb[b][HD:HD + 1, :, :], 1.0).then_inc(setup, 1)
            ve.tensor_scalar(nsink[:, :], sink[:, :], -1.0, None, ALU.mult).then_inc(setup, 1)
            ve.wait_ge(setup, 8)

            def do(ins):
                ins.then_inc(dve, 1)
                ve.wait_ge(dve, 1)
                ve.sem_clear(dve)

            def step(t, scores, values, project, route, place):
                nx, pj, ro, pl = t.back(-1), t.back(1), t.back(2), t.back(3)

                def head(h):
                    if scores:
                        ve.wait_ge(qk, 8 * nx.n + h + 1)
                        wait(ve, tp, 8 * (nx.n - 2) + h + 1)
                        ve.sem_inc(passed, 1)
                        ve.tensor_tensor_reduce(out=pr[nx.par][:, h, :], in0=S[:, :, :].rearrange("p a b -> p (a b)")[:, 0:KEYS],
                                                in1=mask[:, :], scale=1.0, scalar=-3e38, op0=ALU.add, op1=ALU.max,
                                                accum_out=mx[:, nx.par, h:h + 1]).then_inc(sm, 1)
                        ve.wait_ge(sm, 8 * nx.n + h + 1)
                        ve.tensor_scalar(nm[:, nx.par, h:h + 1], mx[:, nx.par, h:h + 1], -SCALE, nsink[:, h:h + 1],
                                         ALU.mult, ALU.min).then_inc(nmx, 1)

                def residual(tile, half):
                    cs = slice(half * 512, (half + 1) * 512)
                    ve.wait_ge(op, 2 * tile.n + half + 1)
                    do(ve.tensor_tensor(x2[tile.par][:, cs], M[:, half, :], g1[:, cs], ALU.mult))
                    return ve.tensor_tensor(x2[tile.par][:, cs], x2[tile.par][:, cs], xr[tile.par][:, cs], ALU.add)

                if values and isinstance(t.n, int) and t.n == 0:
                    ve.wait_ge(filled, 16)
                if values and isinstance(t.n, int) and t.n == 1:
                    ve.wait_ge(ld_later, 16 * len(later))
                head(0)
                if route:
                    residual(ro, 1).then_inc(res, 1)
                for h in range(1, 4):
                    head(h)
                if route:
                    ve.wait_ge(n2d, ro.n + 1)
                    ve.tensor_scalar(xn[ro.par][:, :], x2[ro.par][:, :], n2[:, 0:1], None, ALU.mult).then_inc(xnd, 1)
                head(4)
                if route:
                    ve.wait_ge(t2, ro.n + 1)
                    wait(ve, rt, ro.n)
                    for k in range(4):
                        ins = ve.tensor_scalar(h2T[:, k, :], M[:, 0, k * P:(k + 1) * P], g.scale2[:, k:k + 1],
                                               g.mods[:, 0, 24 + k:25 + k], ALU.mult, ALU.add)
                    ins.then_inc(t2v, 1)
                if place:
                    ve.wait_ge(px, pl.n + 1)
                    wait(ve, rec_ok, pl.n)
                    ve.tensor_copy(pxs[:, :, :], R[:, 64:192].rearrange("p (a b) -> p a b", a=2)[:, :, 0:NE]).then_inc(pxr, 1)
                head(5)
                head(6)
                if route:
                    ve.wait_ge(rt, ro.n + 1)
                    wait(ve, rec_ok, ro.n - 1)
                    ve.tensor_tensor(lg[:, ro.par, :], R[:, 0:NG + NE], rb[:, :], ALU.add).then_inc(lgd, 1)
                head(7)
                if project:
                    ve.wait_ge(t1a, pj.n + 1)
                    wait(ve, op, 2 * pj.n)
                    ve.tensor_tensor(mixl[:, :, :].rearrange("p k t -> p (k t)"), M[:, :, :].rearrange("p a b -> p (a b)"),
                                     mixh[:, :, :].rearrange("p k t -> p (k t)").bitcast(F32), ALU.subtract).then_inc(t1v, 1)
                if scores:
                    wait(ve, att, nx.n - 1)
                    ve.wait_ge(nmx, 8 * nx.n + 8)
                    ve.tensor_tensor(esk[:, nx.par, :], sink[:, :], nm[:, nx.par, :], ALU.add).then_inc(esn, 1)
                if values:
                    ve.wait_ge(eso, t.n + 1)
                    ve.wait_ge(pv, 8 * t.n + 8)
                    wait(ve, mxn, t.n - 1)
                    do(ve.tensor_tensor(rsum[:, t.par, :], rsum[:, t.par, :], esk[:, t.par, :], ALU.add))
                    do(ve.reciprocal(rsum[:, t.par, :], rsum[:, t.par, :]))
                    ve.tensor_tensor(mix[t.par][:, 0, :].rearrange("p (h d) -> p h d", h=NH), O[:, :, :],
                                     rsum[:, t.par, :].unsqueeze(2).broadcast_to([P, NH, HD]), ALU.mult).then_inc(att, 1)
                if values:
                    ve.wait_ge(sqa, t.n + 1)
                    do(ve.tensor_scalar(nw[:, 2, :], ms[:, t.par, :], 1.0 / HW, EPS, ALU.mult, ALU.add))
                    y, c, v = nw[:, 0, :], nw[:, 1, :], nw[:, 2, :]
                    do(ve.tensor_scalar(y.bitcast(I32), v.bitcast(I32), -0.5, float(0x5F3759DF), ALU.mult, ALU.add))
                    for _ in range(3):
                        do(ve.tensor_tensor(c, y, y, ALU.mult))
                        do(ve.tensor_tensor(c, c, v, ALU.mult))
                        do(ve.tensor_scalar(c, c, -0.5, 1.5, ALU.mult, ALU.add))
                        do(ve.tensor_tensor(y, y, c, ALU.mult))
                    wait(ve, t1, t.n)
                    ve.tensor_scalar(mixn[:, 0, :], mix[t.par][:, 0, :], nw[:, 0, 0:1], None, ALU.mult)
                    ve.tensor_scalar(mixn[:, 1, :], mix[t.par][:, 1, :], nw[:, 0, 1:2], None, ALU.mult).then_inc(mxn, 1)
                if project:
                    ve.wait_ge(ld_x[pj.par], 16 * (pj.half + 1))
                    wait(ve, st_x[pj.par], 32 * pj.half)
                    do(residual(pj, 0))
            pipeline(ve, step)


def stage6(e, g):
    nc, i = e.nc, e.i
    FT = FH // P
    PARTS = 4
    with e.stage() as st:
        def raw_and_low(name, shape):
            with nc.sbuf_tensor("sb_raw_" + name, shape, F32) as raw:
                pass
            return raw, e.sb(st, name, shape, F32R)
        raw13, w13 = zip(*[raw_and_low(f"w13_{b}", [P, 2, KT, FH]) for b in range(2)])
        raw2, w2 = zip(*[raw_and_low(f"w2_{b}", [P, FT, D]) for b in range(2)])
        w1h = [e.sb(st, f"w1h_{b}", [P, KT, FH], F32R) for b in range(2)]
        w3h = e.sb(st, "w3h", [P, KT, FH], F32R)
        w2h = [e.sb(st, f"w2h_{b}", [P, FT, D], F32R) for b in range(2)]
        g2 = e.sb(st, "g2row", [P, D])
        info = e.sb(st, "info", [P, 3, NE], I32)
        inf = e.sb(st, "inf", [P, 2, NE])
        rec = e.sb(st, "brec", [P, 2 * NE + T // P + 5, 2], I32)
        rows_in = e.sb(st, "rows_in", [P, 1], I32)
        rows_out = e.sb(st, "rows_out", [P, 1], I32)
        xg = e.sb(st, "xg", [P, D])
        xT = e.sb(st, "bxT", [P, KT, P], F32R)
        xTh = e.sb(st, "bxTh", [P, KT, P], F32R)
        xf = e.sb(st, "bxf", [P, KT // 2, P])
        sg = e.sb(st, "sg", [P, FH])
        gT = e.sb(st, "gT", [P, FT, P], F32R)
        gTh = e.sb(st, "gTh", [P, FT, P], F32R)
        y = e.sb(st, "by", [P, D])
        tpp = e.ps(st, "btp", [P, 2, 4, P])
        hp = e.ps(st, "bh", [P, 2, 512])
        gp = e.ps(st, "bg", [P, FT, P])
        yp = e.ps(st, "byp", [P, 2, 512])
        xfp = e.ps(st, "bxfp", [P, KT // 2, P])
        cnt = e.sem("s6_counts_ready")
        ld = e.sem("s6_gate_row_loaded")
        ldw13 = [[e.sem(f"s6_w{1 + 2 * m}_loaded{b}") for b in range(2)] for m in range(2)]
        ldw2 = [e.sem(f"s6_w2_loaded{b}") for b in range(2)]
        hi13 = e.sem("s6_w13_high")
        lo13 = e.sem("s6_w13_low")
        hi2 = e.sem("s6_w2_high")
        lo2 = e.sem("s6_w2_low")
        rl = e.sem("s6_records_loaded")
        gat = e.sem("s6_rows_gathered")
        scat = e.sem("s6_rows_added")
        tt = e.sem("s6_rows_turned")
        xf_v = e.sem("s6_turned_copied_v")
        xf_a = e.sem("s6_turned_copied_a")
        xhi = e.sem("s6_turned_high")
        xok = e.sem("s6_turned_low")
        hm = e.sem("s6_hidden_product")
        sgd = e.sem("s6_silu")
        gd = e.sem("s6_hidden_gated")
        gtt = e.sem("s6_gated_turned")
        ghi = e.sem("s6_gated_high")
        glo = e.sem("s6_gated_low")
        ym = e.sem("s6_output_product")
        y_ok = e.sem("s6_output_ready")
        picked_in = e.sem("s6_rows_in_picked")
        picked_out = e.sem("s6_rows_out_picked")
        clean = e.sem("s6_buffers_cleared")
        blank = e.sem("s6_records_cleared")
        cnt0 = e.sem("s6_counts_step")
        passed = e.sem("s6_waits_passed")
        passed_s = e.sem("s6_waits_passed_by_sync")
        passed_t = e.sem("s6_waits_passed_by_tensor")
        passed_a = e.sem("s6_waits_passed_by_scalar")
        passed_v = e.sem("s6_waits_passed_by_vector")
        out_rows, xn_rows = e.out[0], g.xn_dram
        block = st.enter_context(nc.Block())

        def span(eng, ex):
            many = eng.value_load(info[0:1, 0, bass.ds(ex, 1)], min_val=1, max_val=T // P)
            base = eng.value_load(info[0:1, 1, bass.ds(ex, 1)], min_val=0, max_val=2 * NE)
            return many, base

        def experts(eng, body):
            def one(ex, par, half):
                many, base = span(eng, ex)
                body(0 if isinstance(ex, int) and ex == 0 else base, ex, par, half, True)
                with eng.If(many > 1):
                    with eng.Fori(1, many) as b:
                        body(base + b, ex, par, half, False)
            eng.wait_ge(cnt, 1)
            one(0, 0, 0)
            with eng.Fori(0, NE // 2 - 1) as pair:
                one(2 * pair + 1, 1, pair)
                one(2 * pair + 2, 0, pair + 1)
            one(NE - 1, 1, NE // 2 - 1)
            return eng.value_load(info[0:1, 2, NE - 1:NE], min_val=1, max_val=2 * NE)

        def starts(n):
            return isinstance(n, int) and n == 0

        def last(ex):
            return isinstance(ex, int) and ex == NE - 1

        def high(par, m):
            return w3h if m else w1h[par]

        def cols(t, m=None):
            return (t[:, :, :] if m is None else t[:, m, :, :]).rearrange("p k f -> p (k f)")

        def load13(eng, ex, par, m):
            src = i[("exp_w1", "exp_w3")[m]][0, bass.ds(ex, 1)].rearrange("a (k p) f -> p (a k) f", p=P)
            eng.dma_start(raw13[par][:, m, :, :], src).then_inc(ldw13[m][par], 16)

        def load2(eng, ex, par):
            src = i["exp_w2"][0, bass.ds(ex, 1)].rearrange("a (k p) f -> p (a k) f", p=P)
            eng.dma_start(raw2[par][:, :, :], src).then_inc(ldw2[par], 16)

        @block.vector
        def _(ve):
            ve.memset(rec[:, :, :], NOWHERE).then_inc(blank, 1)
            ve.memset(xg[:, :], 0.0).then_inc(clean, 1)
            ve.memset(y[:, :], 0.0).then_inc(y_ok, 1)

            def do(ins):
                ins.then_inc(cnt0, 1)
                ve.wait_ge(cnt0, 1)
                ve.sem_clear(cnt0)
            do(ve.tensor_copy(info[:, 0, :], g.carry[:, :]))
            do(ve.tensor_scalar(info[:, 0, :], info[:, 0, :], P - 1, None, ALU.add))
            do(ve.tensor_scalar(info[:, 0, :], info[:, 0, :], P.bit_length() - 1, None, ALU.arith_shift_right))
            do(ve.tensor_scalar(info[:, 0, :], info[:, 0, :], 1, None, ALU.max))
            do(ve.tensor_copy(inf[:, 0, :], info[:, 0, :]))
            do(ve.memset(inf[:, 1, :], 0.0))
            do(ve.tensor_tensor_scan(inf[:, 1, :], inf[:, 0, :], inf[:, 1, :], 0.0, ALU.add, ALU.add))
            do(ve.tensor_copy(info[:, 2, :], inf[:, 1, :]))
            do(ve.tensor_tensor(inf[:, 1, :], inf[:, 1, :], inf[:, 0, :], ALU.subtract))
            ve.tensor_copy(info[:, 1, :], inf[:, 1, :]).then_inc(cnt, 1)
            ve.sem_inc(glo, 1)

            def low13(ex, par, m):
                for part in range(PARTS):
                    ve.wait_ge(hi13, (2 * ex + m) * PARTS + part + 1)
                    cs = slice(part * (KT * FH // PARTS), (part + 1) * (KT * FH // PARTS))
                    ve.tensor_tensor(cols(w13[par], m)[:, cs], cols(raw13[par], m)[:, cs],
                                     cols(high(par, m))[:, cs].bitcast(F32), ALU.subtract).then_inc(lo13, 1)

            def turned(n):
                ve.wait_ge(tt, n + 1)
                for k in range(4):
                    ins = ve.tensor_scalar(xfp[:, k, :], tpp[:, 0, k, :], g.scale2[:, k:k + 1],
                                           g.mods[:, 0, 24 + k:25 + k], ALU.mult, ALU.add)
                ins.then_inc(xf_v, 1)

            def turned_low(n):
                ve.wait_ge(xhi, n + 1)
                for at, src in ((0, xfp), (512, xf)):
                    ins = ve.tensor_tensor(cols(xT)[:, at:at + 512], cols(src), cols(xTh)[:, at:at + 512].bitcast(F32),
                                           ALU.subtract)
                ins.then_inc(xok, 1)

            def output(n, halves=(0, 1)):
                if 0 in halves:
                    ve.wait_ge(scat, 16 * n + 16)
                for half in halves:
                    cs = slice(half * 512, (half + 1) * 512)
                    ve.wait_ge(ym, 2 * n + half)
                    ins = ve.scalar_tensor_tensor(out=y[:, cs], in0=yp[:, half, :],
                                                  scalar=rec[:, bass.ds(n + 1, 1), 1:2].rearrange("p a b -> p (a b)").bitcast(F32),
                                                  in1=g2[:, cs], op0=ALU.mult, op1=ALU.mult)
                if 1 in halves:
                    ins.then_inc(y_ok, 1)

            def gated_low(n):
                ve.wait_ge(ghi, n)
                ve.tensor_tensor(cols(gT), cols(gp), cols(gTh).bitcast(F32), ALU.subtract).then_inc(glo, 1)

            def body(n, ex, par, half, first):
                if first:
                    low13(ex, par, 1)
                if not starts(n):
                    gated_low(n)
                ve.wait_ge(sgd, n + 1)
                ve.wait_ge(hm, 2 * n + 3)
                ve.tensor_tensor(sg[:, :], sg[:, :], hp[:, 1, :], ALU.mult).then_inc(gd, 1)
                turned(n + 1)
                turned_low(n + 1)
                if not starts(n):
                    output(n, (0,))
                if first and not last(ex):
                    low13(ex + 1, 1 - par, 0)
                if not starts(n):
                    output(n, (1,))

            low13(0, 0, 0)
            turned(0)
            turned_low(0)
            ve.wait_ge(ld, 16)
            total = experts(ve, body)
            gated_low(total)
            output(total)

        @block.scalar
        def _(act):
            def high13(ex, par, half, m):
                act.wait_ge(ldw13[m][par], 16 * (half + 1))
                for part in range(PARTS):
                    cs = slice(part * (KT * FH // PARTS), (part + 1) * (KT * FH // PARTS))
                    act.copy(cols(high(par, m))[:, cs], cols(raw13[par], m)[:, cs]).then_inc(hi13, 1)

            def high2(par, half):
                act.wait_ge(ldw2[par], 16 * (half + 1))
                for part in range(2):
                    cs = slice(part * (FT * D // 2), (part + 1) * (FT * D // 2))
                    act.copy(cols(w2h[par])[:, cs], cols(raw2[par])[:, cs]).then_inc(hi2, 1)

            def turned(n):
                act.wait_ge(tt, n + 1)
                if not starts(n):
                    act.wait_ge(xok, n)
                for k in range(4, KT):
                    ins = act.activation(xf[:, k - 4, :], tpp[:, 1, k - 4, :], ACT.Identity,
                                         bias=g.mods[:, 0, 24 + k:25 + k], scale=g.scale2[:, k:k + 1])
                ins.then_inc(xf_a, 1)
                act.wait_ge(xf_a, n + 1)
                act.wait_ge(xf_v, n + 1)
                act.copy(cols(xTh)[:, 0:512], cols(xfp))
                act.copy(cols(xTh)[:, 512:], cols(xf)).then_inc(xhi, 1)

            def gated_high(n):
                act.wait_ge(gtt, n)
                act.copy(cols(gTh), cols(gp)).then_inc(ghi, 1)

            def body(n, ex, par, half, first):
                more = first and not last(ex)
                if first:
                    if not starts(n):
                        act.wait_ge(hm, 2 * n + 1)
                    high13(ex, par, half, 1)
                if not starts(n):
                    gated_high(n)
                    act.wait_ge(gd, n)
                    act.wait_ge(gtt, n)
                act.wait_ge(hm, 2 * n + 2)
                act.activation(sg[:, :], hp[:, 0, :], ACT.Silu).then_inc(sgd, 1)
                if first:
                    high2(par, half)
                turned(n + 1)
                if more:
                    high13(ex + 1, 1 - par, half + par, 0)

            load13(act, 0, 0, 0)
            high13(0, 0, 0, 0)
            act.wait_ge(gat, 16)
            load13(act, 0, 0, 1)
            turned(0)
            load2(act, 0, 0)
            for m in range(2):
                load13(act, 1, 1, m)
            load2(act, 1, 1)
            total = experts(act, body)
            gated_high(total)

        @block.gpsimd
        def _(pool):
            pool.wait_ge(clean, 1)
            pool.wait_ge(cnt, 1)

            def gather(n):
                pool.wait_ge(rl, 16 * (n + 2))
                if not starts(n):
                    pool.wait_ge(tt, n)
                pool.sem_inc(passed, 1)
                pool.tensor_copy(rows_in[:, :], rec[:, bass.ds(n + 2, 1), 0:1].rearrange("p a b -> p (a b)")).then_inc(picked_in, 1)
                pool.wait_ge(picked_in, n + 1)
                pool.sem_inc(passed, 1)
                pool.indirect_dma_start(xg[:, :], None, xn_rows, bass.IndirectOffsetOnAxis(ap=rows_in[:, :], axis=0),
                                        bounds_check=T - 1, oob_is_err=False).then_inc(gat, 16)

            def scatter(n):
                pool.wait_ge(y_ok, 1 if starts(n) else n)
                if not starts(n):
                    pool.wait_ge(scat, 16 * n)
                pool.sem_inc(passed, 1)
                pool.tensor_copy(rows_out[:, :], rec[:, bass.ds(n, 1), 0:1].rearrange("p a b -> p (a b)")).then_inc(picked_out, 1)
                pool.wait_ge(picked_out, n + 1)
                pool.sem_inc(passed, 1)
                pool.indirect_dma_start(out_rows, bass.IndirectOffsetOnAxis(ap=rows_out[:, :], axis=0), y[:, :], None,
                                        bounds_check=T - 1, oob_is_err=False, compute_op=ALU.add).then_inc(scat, 16)

            def body(n, ex, par, half, first):
                scatter(n)
                if first:
                    for part in range(2):
                        pool.wait_ge(hi2, 2 * ex + part + 1)
                        pool.sem_inc(passed, 1)
                        cs = slice(part * (FT * D // 2), (part + 1) * (FT * D // 2))
                        pool.tensor_tensor(cols(w2[par])[:, cs], cols(raw2[par])[:, cs],
                                           cols(w2h[par])[:, cs].bitcast(F32), ALU.subtract).then_inc(lo2, 1)
                gather(n + 2)
            gather(0)
            gather(1)
            total = experts(pool, body)
            scatter(total)
            scatter(total + 1)
            pool.wait_ge(scat, 16 * (total + 2))
            pool.wait_ge(gat, 16 * (total + 2))
            pool.sem_inc(passed, 1)

        @block.sync
        def _(sp):
            def records(ex):
                many, base = span(sp, ex)
                with sp.Fori(0, many) as b:
                    sp.wait_ge(rl, 16 * (base + b + 1))
                    sp.dma_start(rec[:, bass.ds(base + b + 2, 1), :], g.table[bass.ds(ex * CAP + b * P, P), :].unsqueeze(1))\
                      .then_inc(rl, 16)
            sp.wait_ge(blank, 1)
            sp.sem_inc(rl, 16)
            sp.wait_ge(cnt, 1)
            for first in range(3):
                records(first)
            sp.dma_start(g2[:, :], g.gate_dram[D:2 * D].partition_broadcast(P)).then_inc(ld, 16)

            def next_weights(ex, par):
                if not (isinstance(ex, int) and ex + 2 == NE):
                    records(ex + 2)
                many, base = span(sp, ex)
                for m in range(2):
                    sp.wait_ge(hm, 2 * base + m)
                    sp.sem_inc(passed_s, 1)
                    load13(sp, ex + 1, par, m)
                sp.wait_ge(ym, 2 * base + 1)
                sp.sem_inc(passed_s, 1)
                load2(sp, ex + 1, par)
            with sp.Fori(0, NE // 2 - 2) as pair:
                next_weights(2 * pair + 1, 0)
                next_weights(2 * pair + 2, 1)
            next_weights(NE - 3, 0)
            next_weights(NE - 2, 1)
            total = sp.value_load(info[0:1, 2, NE - 1:NE], min_val=1, max_val=2 * NE)
            for k in range(2):
                sp.wait_ge(rl, 16 * (total + k + 1))
                sp.dma_start(rec[:, bass.ds(total + k + 2, 1), :], g.table[NE * CAP:NE * CAP + P, :].unsqueeze(1)).then_inc(rl, 16)

        @block.tensor
        def _(pe):
            def split_product(out, lh, ll, rh, rl_, n, before=None):
                for k in range(n):
                    if before is not None and k % (n // PARTS) == 0:
                        before(k // (n // PARTS))
                    for j, (a, b) in enumerate(((lh, rh), (lh, rl_), (ll, rh))):
                        ins = pe.matmul(out, a[:, k, :], b(k), start=(k == 0 and j == 0), stop=(k == n - 1 and j == 2))
                return ins

            def turn(n):
                pe.wait_ge(gat, 16 * (n + 1))
                for k in range(KT):
                    ins = pe.transpose(tpp[:, k // 4, k % 4, :], xg[:, k * P:(k + 1) * P], g.ident[:, :])
                ins.then_inc(tt, 1)

            def hidden(n, ex, par, m, first):
                def split_part(part):
                    pe.wait_ge(lo13, (2 * ex + m) * PARTS + part + 1)
                    pe.sem_inc(passed_t, 1)
                split_product(hp[:, m, :], xTh, xT, lambda k: high(par, m)[:, k, :], lambda k: w13[par][:, m, k, :], KT,
                              split_part if first else None).then_inc(hm, 1)

            def turn_gated(n):
                pe.wait_ge(gd, n)
                pe.wait_ge(glo, n)
                for f in range(FT):
                    ins = pe.transpose(gp[:, f, :], sg[:, f * P:(f + 1) * P], g.ident[:, :])
                ins.then_inc(gtt, 1)

            def output(n, par):
                pe.wait_ge(glo, n + 1)
                pe.wait_ge(y_ok, n)
                for half in range(2):
                    cs = slice(half * 512, (half + 1) * 512)
                    split_product(yp[:, half, :], gTh, gT, lambda k: w2h[par][:, k, cs], lambda k: w2[par][:, k, cs], FT)\
                        .then_inc(ym, 1)

            def body(n, ex, par, half, first):
                pe.wait_ge(xok, n + 1)
                if not starts(n):
                    pe.wait_ge(sgd, n)
                pe.sem_inc(passed_t, 1)
                hidden(n, ex, par, 0, first)
                if not starts(n):
                    turn_gated(n)
                    pe.wait_ge(gd, n)
                pe.sem_inc(passed_t, 1)
                hidden(n, ex, par, 1, first)
                turn(n + 1)
                if not starts(n):
                    pe.wait_ge(lo2, 2 * ex if first else 2 * ex + 2)
                    pe.sem_inc(passed_t, 1)
                    output(n, 1 - par if first else par)
            for s in (hm, ym):
                pe.sem_inc(s, 1)
            turn(0)
            total = experts(pe, body)
            turn_gated(total)
            pe.wait_ge(lo2, 2 * NE)
            output(total, 1)


class Shared:
    pass


def program(nc, inputs, out, debug=False, stages=(1, 2, 3, 4, 5, 6)):
    with ExitStack() as stack:
        e = Env(nc, stack, inputs, debug)
        e.out = out
        g = Shared()
        g.cols = e.sb(stack, "cols", [P, P])
        g.mods = e.sb(stack, "mods", [P, 2, 48])
        g.scale1 = e.sb(stack, "scale1", [P, 2, KT])
        g.scale2 = e.sb(stack, "scale2", [P, KT])
        g.ident = e.sb(stack, "ident", [P, P])
        g.filt_dram = e.dram("filt", [2, NL, Q, 2, P, LANE])
        g.gate_dram = e.dram("gate", [2 * D])
        g.hy_dram = e.dram("hy_in", [3, T, HW])
        if 1 in stages:
            stage1(e, g)
        g.q_dram = e.dram("q", [NT + 1, HD, NH, P])
        g.carry = e.sb(stack, "carry", [P, NE])
        att = stack.enter_context(ExitStack())
        g.kT = e.sb(att, "kT", [HD + 1, NKV, C + T + 2 * P])
        g.v = e.sb(att, "v", [P, NT + 4, NKV * HD])
        with ExitStack() as mid:
            g.hT = e.sb(mid, "hT", [P, KT, T])
            g.hcT = e.sb(mid, "hcT", [P, KT, C])
            if 2 in stages:
                stage2(e, g)
            if 3 in stages:
                stage3(e, g)
            if debug and max(stages)<=3:
                e.dump(g)
        g.hyo_dram = e.dram("hy_out", [T, HW])
        if 4 in stages:
            stage4(e, g)
        g.xn_dram = e.dram("xn", [T, D])
        g.table = e.dram("table", [NE * CAP + P, 2], I32)
        if 5 in stages:
            stage5(e, g)
        att.close()
        if 6 in stages:
            stage6(e, g)
        if debug and max(stages) >= 4:
            e.dump(g)


INPUTS = ["x", "c", "ctx", "c_ctx", "ada_w", "ada_b", "norm1_w", "w_in", "q_norm_w", "k_norm_w", "attn_sink",
          "hy_conv_w", "hy_conv_b", "hy_w1", "hy_b1", "hy_w2", "hy_b2", "hy_w3", "hy_sin_freq", "hy_skip",
          "group_norm_w", "w_out", "norm2_w", "router_g_w", "router_g_b", "router_e_w", "router_e_b",
          "exp_w1", "exp_w3", "exp_w2"]


def kernel(**inputs):
    import concourse.bacc as bacc
    from concourse.bass_utils import run_bass_kernel_spmd

    nc = bacc.Bacc("TRN2", target_bir_lowering=False, num_devices=1)
    arrays, aps = {}, {}
    for name, a in [(n, inputs[n]) for n in INPUTS] + list(constants().items()):
        a = np.ascontiguousarray(a)
        arrays[f"in_{name}"] = a
        aps[name] = nc.dram_tensor(f"in_{name}", a.shape, mybir.dt.from_np(a.dtype), kind="ExternalInput").ap()
    out = nc.dram_tensor("out_0", (1, T, D), F32, kind="ExternalOutput").ap()
    program(nc, aps, out)
    r = run_bass_kernel_spmd(nc, [arrays], core_ids=[0])
    return r.results[0]["out_0"]
```
